# Optimizing a Trainium2 kernel written in Bass

```python
import numpy as np
import jax
import jax.numpy as jnp
from jax import lax

D_MODEL = 1024
BATCH = 1
SEQ = 2048
DEPTH = 1

N_MIXERS = 3
NORM_EPS = 1e-6
NEG_INF = -1e30

RWKV_HEAD_DIM = 64
RWKV_HEADS = D_MODEL // RWKV_HEAD_DIM
DECAY_LORA = 64
ICLR_LORA = 64
VALUE_LORA = 32
GATE_LORA = 128
RWKV_GN_EPS = 64e-5
N_RWKV_LAYERS = len(range(0, DEPTH, N_MIXERS))
N_VRES = N_RWKV_LAYERS - 1

NSA_HEADS = 16
NSA_KV_GROUPS = 2
NSA_HEAD_DIM = D_MODEL // NSA_HEADS
CMP_BLOCK = 32
CMP_STRIDE = 16
CMP_HIDDEN = 256
SLC_BLOCK = 64
SLC_TOPK = 16
WINDOW = 512
Q_BLOCK = 128
FORCE_BONUS = 1e4
NSA_IN_DIM = NSA_HEADS * NSA_HEAD_DIM + 6 * NSA_KV_GROUPS * NSA_HEAD_DIM + 3 * NSA_HEADS
N_NSA_LAYERS = len(range(1, DEPTH, N_MIXERS))

GLA_HEADS = 4
GLA_KEY_DIM = D_MODEL // 2
GLA_VAL_DIM = D_MODEL
GLA_GATE_LORA = 16
GLA_TAU = 16.0
GLA_CHUNK = 64
GLA_NORM_EPS = 1e-5
GLA_IN_DIM = 2 * GLA_KEY_DIM + 2 * GLA_VAL_DIM + GLA_GATE_LORA
N_GLA_LAYERS = len(range(2, DEPTH, N_MIXERS))

D_FF = 2816
FFN_CONV = 3

kernel_name = 'hybrid_rwkv7_nsa_gla_convffn'

def rms_norm(x, g, eps=NORM_EPS):
    x32 = x.astype(jnp.float32)
    y = x32 * lax.rsqrt(jnp.mean(x32 * x32, axis=-1, keepdims=True) + eps)
    return (y * g.astype(jnp.float32)).astype(x.dtype)

def shift_right(x, n):
    return jnp.pad(x, ((0, 0), (n, 0), (0, 0)))[:, :x.shape[1]]

def rwkv7_step(state, inp):
    r, w, k, v, a, b = inp
    sa = jnp.einsum('bhij,bhj->bhi', state, a)
    state = state * w[:, :, None, :] + sa[..., None] * b[:, :, None, :] + v[..., None] * k[:, :, None, :]
    y = jnp.einsum('bhij,bhj->bhi', state, r)
    return state, y

def rwkv7_time_mix(x, mu, w_rkv, w0, w1, w2, a0, a1, a2, g1, g2, k_k, k_a, r_k, ln_w, ln_b, w_o, v_first, vres):
    B, S, D = x.shape
    H, N = RWKV_HEADS, RWKV_HEAD_DIM
    f32 = jnp.float32
    xx = shift_right(x, 1) - x
    xr, xw, xk, xv, xa, xg = (x + xx * mu[c] for c in range(6))
    r = xr @ w_rkv[0]
    k = xk @ w_rkv[1]
    v = xv @ w_rkv[2]
    w = -jax.nn.softplus(-(w0 + jnp.tanh(xw @ w1) @ w2)) - 0.5
    decay = jnp.exp(-jnp.exp(w.astype(f32)))
    a = jax.nn.sigmoid(a0 + (xa @ a1) @ a2)
    g = jax.nn.sigmoid(xg @ g1) @ g2
    if vres is None:
        v_first = v
    else:
        v0, v1, v2 = vres
        v = v + (v_first - v) * jax.nn.sigmoid(v0 + (xv @ v1) @ v2)
    kk = (k * k_k).reshape(B, S, H, N).astype(f32)
    kk = kk / jnp.maximum(jnp.linalg.norm(kk, axis=-1, keepdims=True), 1e-12)
    k = k * (1 + (a - 1) * k_a)
    heads = lambda t: t.reshape(B, S, H, N).astype(f32)
    r_h, k_h, v_h, a_h = heads(r), heads(k), heads(v), heads(a)
    seq_major = lambda t: jnp.swapaxes(t, 0, 1)
    xs = (seq_major(r_h), seq_major(heads(decay)), seq_major(k_h), seq_major(v_h),
          seq_major(-kk), seq_major(kk * a_h))
    _, y = lax.scan(rwkv7_step, jnp.zeros((B, H, N, N), f32), xs)
    y = seq_major(y)
    mean = jnp.mean(y, axis=-1, keepdims=True)
    var = jnp.var(y, axis=-1, keepdims=True)
    y = ((y - mean) * lax.rsqrt(var + RWKV_GN_EPS)).reshape(B, S, D) * ln_w + ln_b
    bonus = jnp.sum(r_h * k_h * r_k, axis=-1, keepdims=True) * v_h
    out = (y + bonus.reshape(B, S, D)).astype(x.dtype) * g
    return out @ w_o, v_first

def cmp_to_slc_overlap(n_cmp, n_slc):
    start = np.arange(n_cmp) * CMP_STRIDE
    end = start + CMP_BLOCK - 1
    s_start = np.arange(n_slc) * SLC_BLOCK
    s_end = s_start + SLC_BLOCK - 1
    return ((end[:, None] >= s_start[None, :]) & (start[:, None] <= s_end[None, :])).astype(np.float32)

def nsa_mix(x, w_in, cmp_w1, cmp_b1, cmp_w2, cmp_pe, w_o):
    B, S, _ = x.shape
    H, G, dh = NSA_HEADS, NSA_KV_GROUPS, NSA_HEAD_DIM
    hpg = H // G
    f32 = jnp.float32
    q, kv, gates = jnp.split(x @ w_in, [H * dh, H * dh + 6 * G * dh], axis=-1)
    q = q.reshape(B, S, G, hpg, dh) * (dh ** -0.5)
    kv = kv.reshape(B, S, 6, G, dh)
    k_cmp, v_cmp, k_slc, v_slc, k_win, v_win = (kv[:, :, c] for c in range(6))
    gates = jax.nn.sigmoid(gates.reshape(B, S, G, hpg, 3))

    n_cmp = (S - CMP_BLOCK) // CMP_STRIDE + 1
    tok = np.arange(n_cmp)[:, None] * CMP_STRIDE + np.arange(CMP_BLOCK)[None, :]

    def compress(t, c):
        blk = t[:, tok] + cmp_pe[c][:, None, :]
        blk = jnp.swapaxes(blk, 2, 3).reshape(B, n_cmp, G, CMP_BLOCK * dh)
        return jax.nn.gelu(blk @ cmp_w1[c] + cmp_b1[c]) @ cmp_w2[c]

    kc, vc = compress(k_cmp, 0), compress(v_cmp, 1)
    cmp_end = jnp.asarray(tok[:, -1], jnp.int32)

    n_slc = S // SLC_BLOCK
    top_n = min(SLC_TOPK, n_slc)
    overlap = jnp.asarray(cmp_to_slc_overlap(n_cmp, n_slc))
    to_blocks = lambda t: jnp.transpose(t.reshape(B, n_slc, SLC_BLOCK, G, dh), (0, 3, 1, 2, 4))
    ks_b, vs_b = to_blocks(k_slc), to_blocks(v_slc)
    gather = jax.vmap(jax.vmap(lambda blocks, ix: blocks[ix]))
    blk_id = jnp.arange(n_slc, dtype=jnp.int32)
    in_blk = jnp.arange(SLC_BLOCK, dtype=jnp.int32)

    pad = ((0, 0), (WINDOW, 0), (0, 0), (0, 0))
    kw, vw = jnp.pad(k_win, pad), jnp.pad(v_win, pad)
    win_off = jnp.arange(WINDOW + Q_BLOCK, dtype=jnp.int32) - WINDOW

    def query_block(qb):
        t0 = qb * Q_BLOCK
        pos_q = t0 + jnp.arange(Q_BLOCK, dtype=jnp.int32)
        qc = lax.dynamic_slice_in_dim(q, t0, Q_BLOCK, axis=1)
        gc = lax.dynamic_slice_in_dim(gates, t0, Q_BLOCK, axis=1)
        vis = cmp_end[None, :] <= pos_q[:, None]
        s = jnp.einsum('bqghd,bngd->bghqn', qc, kc).astype(f32)
        p_cmp = jax.nn.softmax(jnp.where(vis, s, NEG_INF), axis=-1) * jnp.any(vis, axis=-1)[:, None]
        o_cmp = jnp.einsum('bghqn,bngd->bqghd', p_cmp.astype(vc.dtype), vc)
        imp = jnp.einsum('bghqn,nj->bgqj', p_cmp, overlap)
        cur = pos_q // SLC_BLOCK
        causal = blk_id[None, :] * SLC_BLOCK <= pos_q[:, None]
        forced = (blk_id[None, :] == 0) | (blk_id[None, :] == cur[:, None]) | (blk_id[None, :] == cur[:, None] - 1)
        score = jnp.where(causal, imp + FORCE_BONUS * forced, NEG_INF)
        _, idx = lax.top_k(score, top_n)
        kg, vg = gather(ks_b, idx), gather(vs_b, idx)
        tok_pos = idx[..., None] * SLC_BLOCK + in_blk
        s = jnp.einsum('bqghd,bgqnld->bghqnl', qc, kg).astype(f32)
        s = jnp.where(tok_pos[:, :, None] <= pos_q[:, None, None], s, NEG_INF)
        p = jax.nn.softmax(s.reshape(*s.shape[:4], -1), axis=-1)
        o_slc = jnp.einsum('bghqm,bgqmd->bqghd', p.astype(vg.dtype),
                           vg.reshape(B, G, Q_BLOCK, top_n * SLC_BLOCK, dh))
        kwc = lax.dynamic_slice_in_dim(kw, t0, WINDOW + Q_BLOCK, axis=1)
        vwc = lax.dynamic_slice_in_dim(vw, t0, WINDOW + Q_BLOCK, axis=1)
        pos_k = t0 + win_off
        wmask = ((pos_k[None, :] <= pos_q[:, None]) & (pos_k[None, :] > pos_q[:, None] - WINDOW)
                 & (pos_k[None, :] >= 0))
        s = jnp.einsum('bqghd,bkgd->bghqk', qc, kwc).astype(f32)
        p = jax.nn.softmax(jnp.where(wmask, s, NEG_INF), axis=-1)
        o_win = jnp.einsum('bghqk,bkgd->bqghd', p.astype(vwc.dtype), vwc)
        o = gc[..., 0:1] * o_cmp + gc[..., 1:2] * o_slc + gc[..., 2:3] * o_win
        return o.reshape(B, Q_BLOCK, H * dh)

    out = lax.map(query_block, jnp.arange(S // Q_BLOCK, dtype=jnp.int32))
    out = jnp.swapaxes(out, 0, 1).reshape(B, S, H * dh)
    return out @ w_o

def gla_step(state, inp):
    qe_c, kd_c, v_c, dec_c = inp
    o_c = jnp.einsum('bihd,bhdv->bihv', qe_c, state)
    state = dec_c[..., None] * state + jnp.einsum('bjhd,bjhv->bhdv', kd_c, v_c)
    return state, o_c

def gla_mix(x, w_in, a_up, a_bias, norm_w, w_o):
    B, S, D = x.shape
    H = GLA_HEADS
    dk, dv = GLA_KEY_DIM // H, GLA_VAL_DIM // H
    C = GLA_CHUNK
    nc = S // C
    f32 = jnp.float32
    q, k, v, r, a_dn = jnp.split(x @ w_in, [GLA_KEY_DIM, 2 * GLA_KEY_DIM, 2 * GLA_KEY_DIM + GLA_VAL_DIM,
                                            2 * GLA_KEY_DIM + 2 * GLA_VAL_DIM], axis=-1)
    q = (q.reshape(B, nc, C, H, dk) * (dk ** -0.5)).astype(f32)
    k = k.reshape(B, nc, C, H, dk).astype(f32)
    v = v.reshape(B, nc, C, H, dv).astype(f32)
    log_a = jax.nn.log_sigmoid((a_dn @ a_up + a_bias).astype(f32)) / GLA_TAU
    b = jnp.cumsum(log_a.reshape(B, nc, C, H, dk), axis=2)
    b_last = b[:, :, -1:]
    qe = q * jnp.exp(b)
    ke = k * jnp.exp(-b)
    kd = k * jnp.exp(b_last - b)
    A = jnp.einsum('bnihd,bnjhd->bnhij', qe, ke)
    A = jnp.where(jnp.tril(jnp.ones((C, C), bool)), A, 0.0)
    o_intra = jnp.einsum('bnhij,bnjhv->bnihv', A, v)
    decay = jnp.exp(b_last[:, :, 0])
    xs = tuple(jnp.moveaxis(t, 1, 0) for t in (qe, kd, v, decay))
    _, o_inter = lax.scan(gla_step, jnp.zeros((B, H, dk, dv), f32), xs)
    o = (o_intra + jnp.moveaxis(o_inter, 0, 1)).reshape(B, S, H, dv)
    o = o * lax.rsqrt(jnp.mean(o * o, axis=-1, keepdims=True) + GLA_NORM_EPS) * norm_w.astype(f32)
    o = o * jax.nn.silu(r.reshape(B, S, H, dv).astype(f32))
    return o.reshape(B, S, GLA_VAL_DIM).astype(x.dtype) @ w_o

def conv_ffn(x, w_in, conv_w, conv_b, w_out):
    gate, up = jnp.split(x @ w_in, 2, axis=-1)
    gate = sum(conv_w[FFN_CONV - 1 - s] * shift_right(gate, s) for s in range(FFN_CONV)) + conv_b
    return (jax.nn.silu(gate) * up) @ w_out

def setup_inputs(seed: int = 0) -> dict:
    key = jax.random.key(seed)
    ks = iter(jax.random.split(key, 40))

    def nrm(shape, scale):
        return scale * jax.random.normal(next(ks), shape, jnp.float32)

    D, F = D_MODEL, D_FF
    R, V, NN, NG = N_RWKV_LAYERS, N_VRES, N_NSA_LAYERS, N_GLA_LAYERS
    H, N = RWKV_HEADS, RWKV_HEAD_DIM
    dh = NSA_HEAD_DIM
    gla_dv = GLA_VAL_DIM // GLA_HEADS
    return {
        'x': nrm((BATCH, SEQ, D), 1.0),
        'norm_g': 1.0 + nrm((DEPTH, 4, D), 0.02),
        'ffn_w_in': nrm((DEPTH, D, 2 * F), D ** -0.5),
        'ffn_conv_w': nrm((DEPTH, FFN_CONV, F), FFN_CONV ** -0.5),
        'ffn_conv_b': nrm((DEPTH, F), 0.02),
        'ffn_w_out': nrm((DEPTH, F, D), F ** -0.5),
        'rwkv_mu': jax.random.uniform(next(ks), (R, 6, D), jnp.float32),
        'rwkv_w_rkv': nrm((R, 3, D, D), D ** -0.5),
        'rwkv_w0': nrm((R, D), 0.5),
        'rwkv_w1': nrm((R, D, DECAY_LORA), D ** -0.5),
        'rwkv_w2': nrm((R, DECAY_LORA, D), 0.1 * DECAY_LORA ** -0.5),
        'rwkv_a0': nrm((R, D), 0.5),
        'rwkv_a1': nrm((R, D, ICLR_LORA), D ** -0.5),
        'rwkv_a2': nrm((R, ICLR_LORA, D), 0.1 * ICLR_LORA ** -0.5),
        'rwkv_g1': nrm((R, D, GATE_LORA), D ** -0.5),
        'rwkv_g2': nrm((R, GATE_LORA, D), GATE_LORA ** -0.5),
        'rwkv_k_k': 0.85 + nrm((R, D), 0.05),
        'rwkv_k_a': 1.0 + nrm((R, D), 0.05),
        'rwkv_r_k': nrm((R, H, N), 0.1),
        'rwkv_ln_w': 1.0 + nrm((R, D), 0.02),
        'rwkv_ln_b': nrm((R, D), 0.02),
        'rwkv_w_o': nrm((R, D, D), D ** -0.5),
        'rwkv_v0': nrm((V, D), 0.5),
        'rwkv_v1': nrm((V, D, VALUE_LORA), D ** -0.5),
        'rwkv_v2': nrm((V, VALUE_LORA, D), 0.1 * VALUE_LORA ** -0.5),
        'nsa_w_in': nrm((NN, D, NSA_IN_DIM), D ** -0.5),
        'nsa_cmp_w1': nrm((NN, 2, CMP_BLOCK * dh, CMP_HIDDEN), (CMP_BLOCK * dh) ** -0.5),
        'nsa_cmp_b1': nrm((NN, 2, CMP_HIDDEN), 0.02),
        'nsa_cmp_w2': nrm((NN, 2, CMP_HIDDEN, dh), CMP_HIDDEN ** -0.5),
        'nsa_cmp_pe': nrm((NN, 2, CMP_BLOCK, dh), 0.1),
        'nsa_w_o': nrm((NN, NSA_HEADS * dh, D), (NSA_HEADS * dh) ** -0.5),
        'gla_w_in': nrm((NG, D, GLA_IN_DIM), D ** -0.5),
        'gla_a_up': nrm((NG, GLA_GATE_LORA, GLA_KEY_DIM), GLA_GATE_LORA ** -0.5),
        'gla_a_bias': nrm((NG, GLA_KEY_DIM), 0.5),
        'gla_norm_w': 1.0 + nrm((NG, gla_dv), 0.02),
        'gla_w_o': nrm((NG, GLA_VAL_DIM, D), GLA_VAL_DIM ** -0.5),
    }

def reference(x, norm_g, ffn_w_in, ffn_conv_w, ffn_conv_b, ffn_w_out,
              rwkv_mu, rwkv_w_rkv, rwkv_w0, rwkv_w1, rwkv_w2, rwkv_a0, rwkv_a1, rwkv_a2,
              rwkv_g1, rwkv_g2, rwkv_k_k, rwkv_k_a, rwkv_r_k, rwkv_ln_w, rwkv_ln_b, rwkv_w_o,
              rwkv_v0, rwkv_v1, rwkv_v2,
              nsa_w_in, nsa_cmp_w1, nsa_cmp_b1, nsa_cmp_w2, nsa_cmp_pe, nsa_w_o,
              gla_w_in, gla_a_up, gla_a_bias, gla_norm_w, gla_w_o):
    h = x
    v_first = None
    for i in range(DEPTH):
        kind, j = i % N_MIXERS, i // N_MIXERS
        y = rms_norm(h, norm_g[i, 0])
        if kind == 0:
            vres = None if j == 0 else (rwkv_v0[j - 1], rwkv_v1[j - 1], rwkv_v2[j - 1])
            y, v_first = rwkv7_time_mix(y, rwkv_mu[j], rwkv_w_rkv[j], rwkv_w0[j], rwkv_w1[j], rwkv_w2[j],
                                        rwkv_a0[j], rwkv_a1[j], rwkv_a2[j], rwkv_g1[j], rwkv_g2[j],
                                        rwkv_k_k[j], rwkv_k_a[j], rwkv_r_k[j], rwkv_ln_w[j], rwkv_ln_b[j],
                                        rwkv_w_o[j], v_first, vres)
        elif kind == 1:
            y = nsa_mix(y, nsa_w_in[j], nsa_cmp_w1[j], nsa_cmp_b1[j], nsa_cmp_w2[j], nsa_cmp_pe[j], nsa_w_o[j])
        else:
            y = gla_mix(y, gla_w_in[j], gla_a_up[j], gla_a_bias[j], gla_norm_w[j], gla_w_o[j])
        h = h + rms_norm(y, norm_g[i, 1])
        y = conv_ffn(rms_norm(h, norm_g[i, 2]), ffn_w_in[i], ffn_conv_w[i], ffn_conv_b[i], ffn_w_out[i])
        h = h + rms_norm(y, norm_g[i, 3])
    return h


_drawn_inputs = setup_inputs


def setup_inputs(seed=0):
    import zlib

    import numpy as np

    out = dict(_drawn_inputs(seed))
    spreads = {}
    factors = {'ffn_conv_b': 5.01,
     'rwkv_w1': 5.391,
     'rwkv_w2': 5.367,
     'rwkv_k_k': 5.465,
     'rwkv_ln_w': 3.553,
     'rwkv_ln_b': 3.615}
    for name, (base, spread) in spreads.items():
        noise = np.random.default_rng([zlib.crc32(name.encode()), seed]).standard_normal(out[name].shape)
        drawn = base * np.exp(spread * noise) if base else spread * noise
        out[name] = jnp.asarray(drawn.astype(out[name].dtype))
    for name, factor in factors.items():
        out[name] = (out[name] * factor).astype(out[name].dtype)
    return out
```

```python
import concourse.bass as bass
from concourse import mybir
from contextlib import ExitStack

import numpy as np

f32 = mybir.dt.float32
f16 = mybir.dt.float16
bf16 = mybir.dt.bfloat16
u32 = mybir.dt.uint32
ALU = mybir.AluOpType
ACT = mybir.ActivationFunctionType

P = 128
D = 1024
S = 2048
KC = D // P
HD = 64
C = 128
NCH = S // C
LW, LA, LG = 64, 64, 128
F = 2816
FC = F // P
NORM_EPS = 1e-6
GN_EPS = 64e-5
DECAY = float(np.exp(-0.5))

G0, MU, W0, A0, K_K, K_A, R_K, LN_W, LN_B, G2 = 0, 8, 56, 64, 72, 80, 88, 96, 104, 112
NV = 120
SA, SR, SB, SK, SV, SG, SBV, SM, SE = 0, 128, 256, 384, 512, 640, 768, 896, 897
ROW = 898
HP = KC // 2


class Consts:
    pass


def constants(nc, ctx, a):
    k = Consts()
    sb = lambda n, s, d=f32: ctx.enter_context(nc.sbuf_tensor(n, s, d))
    k.ident = sb("ident", [P, P])
    k.ones_head = sb("ones_head", [P, P])
    k.vec = sb("vec", [P, NV])
    k.w0_half = sb("w0_half", [P, KC])
    k.a0_half = sb("a0_half", [P, KC])
    k.one_less_ka = sb("one_less_ka", [P, KC])
    with ExitStack() as c:
        rows = c.enter_context(nc.sbuf_tensor("vec_rows", [P, P], f32))
        pv = c.enter_context(nc.psum_tensor("pv", [P, P], f32))
        sem = lambda n: c.enter_context(nc.semaphore(n))
        rows_loaded, built, transposed, copied = sem("rows_loaded"), sem("built"), sem("transposed"), sem("copied")
        with nc.Block() as block:
            @block.sync
            def _(sp):
                lots = [(G0, a["norm_g"][0, 0, :]), (W0, a["rwkv_w0"][0, :]), (A0, a["rwkv_a0"][0, :]),
                        (K_K, a["rwkv_k_k"][0, :]), (K_A, a["rwkv_k_a"][0, :]), (LN_W, a["rwkv_ln_w"][0, :]),
                        (LN_B, a["rwkv_ln_b"][0, :]), (G2, a["norm_g"][0, 2, :])]
                for at, v in lots:
                    sp.dma_start(rows[at:at + KC, :], v.rearrange("(c p) -> c p", p=P)).then_inc(rows_loaded, 16)
                sp.dma_start(rows[R_K:R_K + KC, :],
                             a["rwkv_r_k"][0, :, :].rearrange("(c h) n -> c (h n)", h=2)).then_inc(rows_loaded, 16)
                sp.dma_start(rows[MU:MU + 6 * KC, :],
                             a["rwkv_mu"][0, :, :].rearrange("m (c p) -> (m c) p", p=P)).then_inc(rows_loaded, 16)

            @block.gpsimd
            def _(pool):
                nc.gpsimd.memset(k.ident[:, :], 0.0).then_inc(built, 1)
                nc.gpsimd.memset(k.ones_head[:, :], 1.0).then_inc(built, 1)
                pool.wait_ge(built, 2)
                nc.gpsimd.affine_select(out=k.ident[:, :], in_=k.ident[:, :], pattern=[[-1, P]],
                                        compare_op=ALU.not_equal, fill=1.0, base=0,
                                        channel_multiplier=1).then_inc(built, 1)
                nc.gpsimd.affine_select(out=k.ones_head[:, 0:HD], in_=k.ones_head[:, 0:HD], pattern=[[0, HD]],
                                        compare_op=ALU.is_ge, fill=0.0, base=HD - 1,
                                        channel_multiplier=-1).then_inc(built, 1)
                nc.gpsimd.affine_select(out=k.ones_head[:, HD:P], in_=k.ones_head[:, HD:P], pattern=[[0, HD]],
                                        compare_op=ALU.is_ge, fill=0.0, base=-HD,
                                        channel_multiplier=1).then_inc(built, 1)

            @block.tensor
            def _(pe):
                pe.wait_ge(built, 5)
                pe.wait_ge(rows_loaded, 160)
                nc.tensor.transpose(pv[:, 0:NV], rows[0:NV, :], k.ident[0:NV, 0:NV]).then_inc(transposed, 1)

            @block.vector
            def _(dve):
                dve.wait_ge(transposed, 1)
                nc.vector.tensor_copy(k.vec[:, :], pv[:, 0:NV]).then_inc(copied, 1)
                dve.wait_ge(copied, 1)
                nc.vector.tensor_scalar(k.w0_half[:, :], k.vec[:, W0:W0 + KC], 0.5, None, ALU.mult).then_inc(copied, 1)
                nc.vector.tensor_scalar(k.a0_half[:, :], k.vec[:, A0:A0 + KC], 0.5, None, ALU.mult).then_inc(copied, 1)
                nc.vector.tensor_scalar(k.one_less_ka[:, :], k.vec[:, K_A:K_A + KC], -1.0, 1.0,
                                        ALU.mult, ALU.add).then_inc(copied, 1)
                dve.wait_ge(copied, 4)
    return k


def project(nc, k, a, scratch):
    T = 256
    NT = S // T
    TB = T // P
    assert TB == T // C
    x_rows = a["x"][0, :, :].rearrange("(n p) d -> n p d", p=P)
    with ExitStack() as c:
        sb = lambda n, s, d=f32: c.enter_context(nc.sbuf_tensor(n, s, d))
        ps = lambda n: c.enter_context(nc.psum_tensor(n, [P, 512], f32))
        sem = lambda n: c.enter_context(nc.semaphore(n))
        w_rkv = [sb(f"w_{n}", [P, KC, D]) for n in "rkv"]
        w1 = sb("w1", [P, KC, LW]); a1 = sb("a1", [P, KC, LA]); g1 = sb("g1", [P, KC, LG])
        w2 = sb("w2", [LW, D]); a2 = sb("a2", [LA, D]); g2 = sb("g2", [LG, D])
        xb = sb("xb", [P, TB, D])
        xsq = sb("xsq", [P, 2]); rstd = sb("rstd", [P, 2])
        yT = sb("yT", [P, KC, T + 1])
        xx = sb("xx", [P, KC, T])
        mix = [sb(f"mix{i}", [P, KC, T]) for i in range(2)]
        hid_w = sb("hid_w", [LW, T]); hid_a = sb("hid_a", [LA, T]); hid_g = sb("hid_g", [LG, T])
        kT = sb("kT", [P, KC, T])
        rnorm = sb("rnorm", [P, KC, T])
        out_rows = [sb(f"out_rows{i}", [P, TB, ROW]) for i in range(2)]
        sq = sb("sq", [P, T])
        not_first = sb("not_first", [P, T])
        tw = sb("tw", [P, T]); lw = sb("lw", [P, T]); cum = sb("cum", [P, T]); cm = sb("cm", [P, T])
        cx = sb("cx", [P, T]); e_in = sb("e_in", [P, T]); e_out = sb("e_out", [P, T]); e_pre = sb("e_pre", [P, T])
        gS = sb("gS", [P, T]); ta = sb("ta", [P, T]); kk = sb("kk", [P, T]); kn = sb("kn", [P, T]); rS = sb("rS", [P, T])
        zero = sb("zero", [P, HP, 1])

        pX = [ps("pX0"), ps("pX1")]; pP = [ps("pP0"), ps("pP1")]
        pH, pZ, pG, pS = ps("pH"), ps("pZ"), ps("pG"), ps("pS")

        x_loaded = sem("x_loaded"); rkv_loaded = [sem(f"{n}_loaded") for n in ("wr", "wk", "wv")]
        lora_loaded = sem("lora_loaded")
        x_squared = sem("x_squared"); x_root = sem("x_root"); mean_ready = sem("mean_ready")
        rstd_ready = sem("rstd_ready"); xn_ready = sem("xn_ready")
        xt_ready = sem("xt_ready"); yt_ready = sem("yt_ready"); carried = sem("carried"); xx_ready = sem("xx_ready")
        mix_ready = sem("mix_ready"); hid_ready = sem("hid_ready"); hid_taken = sem("hid_taken")
        proj_ready = sem("proj_ready"); proj_taken = sem("proj_taken")
        sq_ready = sem("sq_ready"); ss_ready = sem("ss_ready"); ss_taken = sem("ss_taken")
        norm_root = sem("norm_root"); norm_ready = sem("norm_ready")
        z_ready = sem("z_ready"); zw_taken = sem("zw_taken"); za_taken = sem("za_taken")
        gate_ready = sem("gate_ready"); gate_taken = sem("gate_taken")
        lw_ready = sem("lw_ready"); cum_ready = sem("cum_ready"); cm_ready = sem("cm_ready"); cx_ready = sem("cx_ready")
        exp_ready = sem("exp_ready"); ends_ready = sem("ends_ready"); mid_ready = sem("mid_ready")
        rate_ready = sem("rate_ready"); kk_ready = sem("kk_ready"); b_ready = sem("b_ready")
        kn_ready = sem("kn_ready"); k_half = sem("k_half"); rk_ready = sem("rk_ready")
        bonus_ready = sem("bonus_ready"); bonus_taken = sem("bonus_taken"); rows_ready = sem("rows_ready")
        rows_stored = [sem(f"rows_stored{i}") for i in range(2)]
        set_up = sem("set_up"); zero_stored = sem("zero_stored")

        with nc.Block() as block:
            @block.sync
            def _(sp):
                sp.dma_start(xb[:, :, :], x_rows[0:TB, :, :].rearrange("n p d -> p n d")).then_inc(x_loaded, 16)
                for n in (1, 0, 2):
                    sp.dma_start(w_rkv[n][:, :, :], a["rwkv_w_rkv"][0, n, :, :].rearrange("(c p) f -> p c f", p=P))\
                      .then_inc(rkv_loaded[n], 16)
                    if n == 1:
                        for t, s in ((w1, "rwkv_w1"), (a1, "rwkv_a1"), (g1, "rwkv_g1")):
                            sp.dma_start(t[:, :, :], a[s][0, :, :].rearrange("(c p) f -> p c f", p=P))\
                              .then_inc(lora_loaded, 16)
                        for t, s in ((w2, "rwkv_w2"), (a2, "rwkv_a2"), (g2, "rwkv_g2")):
                            sp.dma_start(t[:, :], a[s][0, :, :]).then_inc(lora_loaded, 16)
                with sp.Fori(1, NT) as tt:
                    sp.wait_ge(xt_ready, 2 * TB * tt)
                    sp.dma_start(xb[:, :, :], x_rows[bass.ts(tt, TB), :, :].rearrange("n p d -> p n d"))\
                      .then_inc(x_loaded, 16)

            @block.gpsimd
            def _(pool):
                nc.gpsimd.memset(not_first[:, :], 1.0).then_inc(set_up, 1)
                pool.wait_ge(set_up, 1)
                nc.gpsimd.memset(not_first[:, 0:T:C], 0.0).then_inc(set_up, 1)
                nc.gpsimd.memset(yT[:, :, T:T + 1], 0.0).then_inc(set_up, 1)
                nc.gpsimd.memset(zero[:, :, :], 0.0).then_inc(set_up, 1)
                with pool.Fori(0, NT) as tt:
                    for p in range(KC):
                        pool.wait_ge(rows_ready, KC * tt + p + 1)
                        pool.dma_start(
                            scratch[bass.ds((p // HP) * NCH + tt * TB, TB), p % HP, :, :].rearrange("c q r -> q c r"),
                            out_rows[p % 2][:, :, :]).then_inc(rows_stored[p % 2], 16)
                for i in range(2):
                    pool.wait_ge(rows_stored[i], 16 * NT * KC // 2)
                for half in range(2):
                    pool.dma_start(scratch[half * NCH, :, :, SM:SM + 1].rearrange("h q r -> q h r"),
                                   zero[:, :, :], allow_slow_non_contiguous=True).then_inc(zero_stored, 16)
                pool.wait_ge(zero_stored, 32)

            @block.scalar
            def _(act):
                with act.Fori(0, NT) as tt:
                    act.wait_ge(x_loaded, 16 * (tt + 1))
                    act.wait_ge(mix_ready, 6 * tt)
                    for b in range(TB):
                        nc.scalar.activation(xx[:, b * (D // T):(b + 1) * (D // T), :], xb[:, b, :], ACT.Square,
                                             accum_out=xsq[:, b:b + 1]).then_inc(x_squared, 1)
                    act.wait_ge(mean_ready, tt + 1)
                    nc.scalar.activation(rstd[:, :], xsq[:, :], ACT.Sqrt).then_inc(x_root, 1)

                    def take_k(p):
                        act.wait_ge(proj_ready, 3 * KC * tt + p + 1)
                        if p == 0:
                            act.wait_ge(k_half, KC * tt)
                        nc.scalar.activation(kT[:, p, :], pP[p % 2][:, 0:T], ACT.Copy).then_inc(proj_taken, 1)
                        act.wait_ge(proj_taken, 3 * KC * tt + p + 1)
                        if p == 0:
                            act.wait_ge(ss_ready, KC * tt)
                        else:
                            act.wait_ge(ss_ready, KC * tt + p)
                        nc.scalar.activation(sq[:, :], kT[:, p, :], ACT.Square,
                                             scale=k.vec[:, K_K + p:K_K + p + 1]).then_inc(sq_ready, 1)

                    for p in range(KC):
                        take_k(p)
                    act.wait_ge(hid_ready, 3 * tt + 1)
                    nc.scalar.activation(hid_w[:, :], pX[0][0:LW, 0:T], ACT.Tanh).then_inc(hid_taken, 1)
                    act.wait_ge(hid_ready, 3 * tt + 2)
                    nc.scalar.activation(hid_a[:, :], pX[1][0:LA, 0:T], ACT.Copy).then_inc(hid_taken, 1)
                    act.wait_ge(hid_ready, 3 * tt + 3)
                    nc.scalar.activation(hid_g[:, :], pH[:, 0:T], ACT.Tanh, scale=0.5).then_inc(hid_taken, 1)
                    act.wait_ge(ss_taken, KC * (tt + 1))
                    nc.scalar.activation(rnorm[:, :, :], rnorm[:, :, :], ACT.Sqrt).then_inc(norm_root, 1)
                    for p in range(KC):
                        rows = out_rows[p % 2]
                        n = KC * tt + p
                        act.wait_ge(z_ready, n + 1)
                        act.wait_ge(lw_ready, n)
                        nc.scalar.activation(tw[:, :], pZ[:, 0:T], ACT.Tanh, bias=k.w0_half[:, p:p + 1],
                                             scale=0.5).then_inc(zw_taken, 1)
                        act.wait_ge(rk_ready, n)
                        nc.scalar.activation(ta[:, :], pZ[:, T:2 * T], ACT.Tanh, bias=k.a0_half[:, p:p + 1],
                                             scale=0.5).then_inc(za_taken, 1)
                        act.wait_ge(proj_ready, 3 * KC * tt + KC + 2 * p + 1)
                        act.wait_ge(bonus_ready, n)
                        nc.scalar.activation(rS[:, :], pP[0][:, 0:T], ACT.Copy).then_inc(proj_taken, 1)
                        if p >= 2:
                            act.wait_ge(rows_stored[p % 2], 16 * (KC // 2 * tt + p // 2))
                        else:
                            act.wait_ge(rows_stored[p % 2], 16 * (KC // 2) * tt)
                        act.wait_ge(gate_ready, n + 1)
                        act.wait_ge(rows_ready, n)
                        nc.scalar.activation(gS[:, :], pG[:, 0:T], ACT.Copy).then_inc(gate_taken, 1)
                        act.wait_ge(proj_ready, 3 * KC * tt + KC + 2 * p + 2)
                        nc.scalar.activation(rows[:, :, SV:SV + C], pP[1][:, 0:T].rearrange("q (c t) -> q c t", t=C),
                                             ACT.Copy).then_inc(proj_taken, 1)
                        act.wait_ge(cm_ready, n + 1)
                        nc.scalar.activation(e_in[:, :], cm[:, :], ACT.Exp).then_inc(exp_ready, 1)
                        nc.scalar.activation(e_out[:, :], cm[:, :], ACT.Exp, scale=-1.0).then_inc(exp_ready, 1)
                        act.wait_ge(cx_ready, n + 1)
                        nc.scalar.activation(e_pre[:, :], cx[:, :], ACT.Exp).then_inc(exp_ready, 1)
                        nc.scalar.activation(rows[:, :, SM], cum[:, C // 2 - 1:T:C], ACT.Exp).then_inc(exp_ready, 1)
                        nc.scalar.activation(rows[:, :, SE], cm[:, C - 1:T:C], ACT.Exp).then_inc(exp_ready, 1)

            @block.vector
            def _(dve):
                V = nc.vector
                dve.wait_ge(set_up, 4)
                with dve.Fori(0, NT) as tt:
                    dve.wait_ge(x_squared, TB * (tt + 1))
                    V.tensor_scalar(xsq[:, :], xsq[:, :], 1.0 / D, NORM_EPS, ALU.mult, ALU.add).then_inc(mean_ready, 1)
                    dve.wait_ge(x_root, tt + 1)
                    V.reciprocal(rstd[:, :], rstd[:, :]).then_inc(rstd_ready, 1)
                    dve.wait_ge(rstd_ready, tt + 1)
                    for b in range(TB):
                        V.tensor_scalar(xb[:, b, :], xb[:, b, :], rstd[:, b:b + 1], None, ALU.mult).then_inc(xn_ready, 1)
                    dve.wait_ge(mix_ready, 6 * tt)
                    dve.wait_ge(proj_ready, 3 * KC * tt)
                    V.tensor_copy(yT[:, :, 0:1], yT[:, :, T:T + 1]).then_inc(carried, 1)
                    dve.wait_ge(carried, tt + 1)
                    for b in range(TB):
                        for q in range(2):
                            dve.wait_ge(xt_ready, 2 * TB * tt + 2 * b + q + 1)
                            V.tensor_tensor(yT[:, 4 * q:4 * q + 4, 1 + b * P:1 + (b + 1) * P],
                                            pX[q][:, :].rearrange("p (c t) -> p c t", t=P),
                                            k.vec[:, G0 + 4 * q:G0 + 4 * q + 4].unsqueeze(2).to_broadcast([P, 4, P]),
                                            ALU.mult).then_inc(yt_ready, 1)
                    dve.wait_ge(yt_ready, 2 * TB * (tt + 1))
                    V.tensor_tensor(xx[:, :, :], yT[:, :, 0:T], yT[:, :, 1:T + 1], ALU.subtract).then_inc(xx_ready, 1)
                    dve.wait_ge(xx_ready, tt + 1)

                    def blend(n, m):
                        for q in range(KC):
                            last = V.scalar_tensor_tensor(
                                out=mix[n % 2][:, q, :], in0=xx[:, q, :],
                                scalar=k.vec[:, MU + m * KC + q:MU + m * KC + q + 1],
                                in1=yT[:, q, 1:T + 1], op0=ALU.mult, op1=ALU.add)
                        last.then_inc(mix_ready, 1)

                    blend(0, 2)
                    blend(1, 1)
                    dve.wait_ge(norm_root, tt) 
                    dve.wait_ge(kk_ready, KC * tt)
                    for p in range(KC):
                        dve.wait_ge(ss_ready, KC * tt + p + 1)
                        V.tensor_scalar(rnorm[:, p, :], pS[:, 0:T], 1e-24, None, ALU.max).then_inc(ss_taken, 1)
                    dve.wait_ge(proj_ready, 3 * KC * tt + KC)
                    blend(2, 4)
                    dve.wait_ge(hid_ready, 3 * tt + 1)
                    blend(3, 5)
                    dve.wait_ge(norm_root, tt + 1)
                    V.reciprocal(rnorm[:, :, :], rnorm[:, :, :]).then_inc(norm_ready, 1)
                    dve.wait_ge(hid_taken, 3 * tt + 3)
                    V.tensor_scalar(hid_g[:, :], hid_g[:, :], 0.5, 0.5, ALU.mult, ALU.add).then_inc(norm_ready, 1)
                    dve.wait_ge(hid_ready, 3 * tt + 2)
                    blend(4, 0)
                    dve.wait_ge(hid_ready, 3 * tt + 3)
                    blend(5, 3)
                    dve.wait_ge(norm_ready, 2 * tt + 2)
                    for p in range(KC):
                        rows = out_rows[p % 2]
                        n = KC * tt + p
                        by_chunk = lambda t: t[:, :].rearrange("q (c t) -> q c t", t=C)
                        dve.wait_ge(zw_taken, n + 1)
                        V.tensor_scalar(lw[:, :], tw[:, :], -0.5 * DECAY, -0.5 * DECAY, ALU.mult, ALU.add)\
                            .then_inc(lw_ready, 1)
                        dve.wait_ge(lw_ready, n + 1)
                        dve.wait_ge(exp_ready, 5 * n)
                        V.tensor_tensor_scan(cum[:, :], not_first[:, :], lw[:, :], 0.0, ALU.mult, ALU.add)\
                            .then_inc(cum_ready, 1)
                        dve.wait_ge(cum_ready, n + 1)
                        V.tensor_tensor(by_chunk(cm), by_chunk(cum),
                                        cum[:, C // 2 - 1:T:C].unsqueeze(2).to_broadcast([P, TB, C]),
                                        ALU.subtract).then_inc(cm_ready, 1)
                        dve.wait_ge(cm_ready, n + 1)
                        V.tensor_tensor(cx[:, :], cm[:, :], lw[:, :], ALU.subtract).then_inc(cx_ready, 1)
                        V.scalar_tensor_tensor(out=kk[:, :], in0=kT[:, p, :], scalar=k.vec[:, K_K + p:K_K + p + 1],
                                               in1=rnorm[:, p, :], op0=ALU.mult, op1=ALU.mult).then_inc(kk_ready, 1)
                        dve.wait_ge(za_taken, n + 1)
                        V.tensor_scalar(ta[:, :], ta[:, :], 0.5, 0.5, ALU.mult, ALU.add).then_inc(rate_ready, 1)
                        dve.wait_ge(rate_ready, n + 1)
                        V.tensor_scalar(kn[:, :], ta[:, :], k.vec[:, K_A + p:K_A + p + 1], k.one_less_ka[:, p:p + 1],
                                        ALU.mult, ALU.add).then_inc(kn_ready, 1)
                        dve.wait_ge(kn_ready, 2 * n + 1)
                        V.tensor_tensor(kn[:, :], kn[:, :], kT[:, p, :], ALU.mult).then_inc(kn_ready, 1)
                        dve.wait_ge(kn_ready, 2 * n + 2)
                        if p >= 2:
                            dve.wait_ge(rows_stored[p % 2], 16 * (KC // 2 * tt + p // 2))
                        else:
                            dve.wait_ge(rows_stored[p % 2], 16 * (KC // 2) * tt)
                        dve.wait_ge(kk_ready, n + 1)
                        V.tensor_tensor(ta[:, :], ta[:, :], kk[:, :], ALU.mult).then_inc(b_ready, 1)
                        dve.wait_ge(exp_ready, 5 * n + 5)
                        V.tensor_tensor(rows[:, :, SK:SK + C], by_chunk(kn), by_chunk(e_out), ALU.mult)\
                            .then_inc(k_half, 1)
                        V.tensor_tensor(rows[:, :, SA:SA + C], by_chunk(kk), by_chunk(e_pre), ALU.mult)
                        dve.wait_ge(b_ready, n + 1)
                        V.tensor_tensor(rows[:, :, SB:SB + C], by_chunk(ta), by_chunk(e_out), ALU.mult)
                        dve.wait_ge(proj_taken, 3 * KC * tt + KC + 2 * p + 2)
                        V.tensor_tensor(rows[:, :, SR:SR + C], by_chunk(rS), by_chunk(e_in), ALU.mult)
                        V.scalar_tensor_tensor(out=rS[:, :], in0=rS[:, :], scalar=k.vec[:, R_K + p:R_K + p + 1],
                                               in1=kn[:, :], op0=ALU.mult, op1=ALU.mult).then_inc(rk_ready, 1)
                        dve.wait_ge(gate_taken, n + 1)
                        V.tensor_scalar(rows[:, :, SG:SG + C], by_chunk(gS), k.vec[:, LN_W + p:LN_W + p + 1], None,
                                        ALU.mult)
                        dve.wait_ge(bonus_ready, n + 1)
                        V.tensor_tensor(by_chunk(cx), pS[:, 0:T].rearrange("q (c t) -> q c t", t=C),
                                        rows[:, :, SV:SV + C], ALU.mult).then_inc(bonus_taken, 1)
                        dve.wait_ge(bonus_taken, n + 1)
                        V.scalar_tensor_tensor(out=rows[:, :, SBV:SBV + C], in0=by_chunk(cx),
                                               scalar=k.vec[:, LN_B + p:LN_B + p + 1], in1=by_chunk(gS),
                                               op0=ALU.add, op1=ALU.mult).then_inc(rows_ready, 1)

            @block.tensor
            def _(pe):
                T_ = nc.tensor

                def proj(n, w, p, m, tt):
                    if n >= 1:
                        pe.wait_ge(proj_taken, 3 * KC * tt + n - 1)
                    else:
                        pe.wait_ge(proj_taken, 3 * KC * tt)
                    for q in range(KC):
                        mm = T_.matmul(pP[n % 2][:, 0:T], w[:, q, p * P:(p + 1) * P], mix[m % 2][:, q, :],
                                       start=(q == 0), stop=(q == KC - 1))
                    mm.then_inc(proj_ready, 1)

                with pe.Fori(0, NT) as tt:
                    pe.wait_ge(hid_taken, 3 * tt)
                    for b in range(TB):
                        pe.wait_ge(xn_ready, TB * tt + b + 1)
                        for q in range(2):
                            if b >= 1:
                                pe.wait_ge(yt_ready, 2 * TB * tt + 2 * b + q - 1)
                            for j in range(4):
                                mm = T_.transpose(pX[q][:, j * P:(j + 1) * P],
                                                  xb[:, b, (4 * q + j) * P:(4 * q + j + 1) * P], k.ident[:, :])
                            mm.then_inc(xt_ready, 1)
                    pe.wait_ge(rkv_loaded[1], 16)
                    pe.wait_ge(mix_ready, 6 * tt + 1)

                    def sums(p):
                        pe.wait_ge(sq_ready, KC * tt + p + 1)
                        pe.wait_ge(ss_taken, KC * tt + p)
                        if p == 0:
                            pe.wait_ge(rows_ready, KC * tt)
                        T_.matmul(pS[:, 0:T], k.ones_head[:, :], sq[:, :], start=True, stop=True).then_inc(ss_ready, 1)

                    for p in range(KC):
                        proj(p, w_rkv[1], p, 0, tt)
                        if p >= 1:
                            sums(p - 1)
                    pe.wait_ge(lora_loaded, 96)
                    sums(KC - 1)
                    pe.wait_ge(yt_ready, 2 * TB * (tt + 1))
                    for i, (dst, w) in enumerate(((pX[0][0:LW, 0:T], w1), (pX[1][0:LA, 0:T], a1), (pH[:, 0:T], g1))):
                        pe.wait_ge(mix_ready, 6 * tt + 2 + i)
                        for q in range(KC):
                            mm = T_.matmul(dst, w[:, q, :], mix[(1 + i) % 2][:, q, :],
                                           start=(q == 0), stop=(q == KC - 1))
                        mm.then_inc(hid_ready, 1)
                    pe.wait_ge(hid_taken, 3 * tt + 3)
                    pe.wait_ge(norm_ready, 2 * tt + 2)

                    def bonus(p):
                        pe.wait_ge(rk_ready, KC * tt + p + 1)
                        pe.wait_ge(rows_ready, KC * tt + p)
                        T_.matmul(pS[:, 0:T], k.ones_head[:, :], rS[:, :], start=True, stop=True)\
                            .then_inc(bonus_ready, 1)

                    for p in range(KC):
                        n = KC * tt + p
                        f = slice(p * P, (p + 1) * P)
                        pe.wait_ge(za_taken, n)
                        T_.matmul(pZ[:, 0:T], w2[:, f], hid_w[:, :], start=True, stop=True)
                        T_.matmul(pZ[:, T:2 * T], a2[:, f], hid_a[:, :], start=True, stop=True).then_inc(z_ready, 1)
                        if p == 0:
                            pe.wait_ge(mix_ready, 6 * tt + 5)
                            pe.wait_ge(rkv_loaded[0], 16)
                        proj(KC + 2 * p, w_rkv[0], p, 0, tt)
                        pe.wait_ge(gate_taken, n)
                        T_.matmul(pG[:, 0:T], g2[:, f], hid_g[:, :], start=True, stop=True).then_inc(gate_ready, 1)
                        if p == 0:
                            pe.wait_ge(mix_ready, 6 * tt + 6)
                            pe.wait_ge(rkv_loaded[2], 16)
                        if p >= 1:
                            bonus(p - 1)
                        proj(KC + 2 * p + 1, w_rkv[2], p, 1, tt)
                    bonus(KC - 1)




def recur(nc, k, scratch, gated):
    Q = 2
    QP = HP // Q
    QH = 2 * QP
    LEVELS = [2, 4, 8, 16, 32, 64]
    NI = 2 * NCH
    with ExitStack() as c:
        sb = lambda n, s, d=f32: c.enter_context(nc.sbuf_tensor(n, s, d))
        sem = lambda n: c.enter_context(nc.semaphore(n))
        rows = [sb(f"rows{i}", [P, HP, ROW]) for i in range(2)]
        arx = [[sb(f"arx{u}_{q}", [P, QP, 2, 2 * C]) for q in range(Q)] for u in range(2)]
        att_b = [sb(f"att_b{q}", [P, QP, 2, 2 * C]) for q in range(Q)]
        att_k = [sb(f"att_k{q}", [P, QP, 2, 2 * C]) for q in range(Q)]
        tok = [sb(f"tok{q}", [P, QP, 3, P]) for q in range(Q)]
        rhs = [sb(f"rhs{q}", [P, QP, 2, 2, HD]) for q in range(Q)]
        rhs16 = [sb(f"rhs16_{q}", [P, QP, 2, 2, HD], bf16) for q in range(Q)]
        res16 = [sb(f"res16_{q}", [P, QP, 2, 2, HD], bf16) for q in range(Q)]
        sol = [sb(f"sol{q}", [P, QP, 2, 2, HD]) for q in range(Q)]
        lT16 = [sb(f"lT16_{q}", [P, QH, C], f16) for q in range(Q)]
        t16 = [sb(f"t16_{q}", [P, QH, C], f16) for q in range(Q)]
        tT16 = [sb(f"tT16_{q}", [P, QH, C], f16) for q in range(Q)]
        u16 = [sb(f"u16_{q}", [P, QH, C], f16) for q in range(Q)]
        w1T = [sb(f"w1T{q}", [P, QP, C]) for q in range(Q)]
        U = [sb(f"U{q}", [P, QP, P]) for q in range(Q)]
        z = [sb(f"z{q}", [P, QP, P]) for q in range(Q)]
        zt = [sb(f"zt{q}", [P, QP, P]) for q in range(Q)]
        scale = sb("scale", [P, HP, 1])
        eps = sb("eps", [P, 1])
        y = sb("y", [P, HP, C]); yc = sb("yc", [P, HP, C]); ysq = sb("ysq", [P, HP, C])
        ysd = sb("ysd", [P, HP, C]); yn = sb("yn", [P, HP, C]); ya = sb("ya", [P, HP, C]); yg = sb("yg", [P, HP, C])
        causal = sb("causal", [P, 2 * C])
        lower = sb("lower", [P, len(LEVELS), C])
        upper = sb("upper", [P, 1 + len(LEVELS), C])
        start = sb("start", [P, C])
        ident16 = sb("ident16", [P, P], f16)

        bank = [[c.enter_context(nc.psum_tensor(f"bank{q}_{j}", [P, 512], f32)) for j in range(3)] for q in range(Q)]
        p_mean = c.enter_context(nc.psum_tensor("p_mean", [P, 512], f32))
        p_var = c.enter_context(nc.psum_tensor("p_var", [P, 512], f32))

        fills = [("tok0", "act"), ("tok1", "act"), ("b0", "dve"), ("k0", "dve"), ("b1", "dve"), ("k1", "dve"),
                 ("mv", "act"), ("t", "act")]
        for m in LEVELS:
            fills += [(f"u{m}", "act")] + ([(f"w{m}", "dve")] if m != LEVELS[-1] else []) + [(f"wT{m}", "dve")]
        fills += [("z0", "act"), ("r0", "dve"), ("d0", "dve"), ("r1", "dve"), ("d1", "dve"),
                  ("w1T", "act"), ("U", "dve"), ("zn", "dve"), ("Y", "act")]
        names = [f for f, _ in fills]
        NF = len(fills)
        per = {e: sum(t == e for _, t in fills) for e in ("act", "dve")}
        place = lambda name: names.index(name)
        bank_of = lambda q, name: bank[q][place(name) % 3]

        def nth(name):
            n = place(name)
            return fills[n][1], sum(t == fills[n][1] for _, t in fills[:n + 1])

        filled = [sem(f"filled{q}") for q in range(Q)]
        took = {e: [sem(f"{e}_took{q}") for q in range(Q)] for e in ("act", "dve")}

        def wait_taken(eng, q, i, name):
            e, n = nth(name)
            eng.wait_ge(took[e][q], per[e] * i + n)

        def wait_filled(eng, q, i, name):
            eng.wait_ge(filled[q], NF * i + place(name) + 1)

        def wait_bank(eng, q, i, name, *needs):
            n = place(name)
            for e in ("act", "dve"):
                counts = [nth(f)[1] for f in (*needs, *names[n - 3:n - 2]) if nth(f)[0] == e] if n >= 3 else [0]
                if counts:
                    eng.wait_ge(took[e][q], per[e] * i + max(counts))

        rows_loaded = [sem(f"rowsB_loaded{s}") for s in range(2)]
        expanded = sem("expanded"); lT_ready = [sem(f"lT_ready{q}") for q in range(Q)]
        tT_ready = [sem(f"tT_ready{q}") for q in range(Q)]; rhs16_ready = [sem(f"rhs16_ready{q}") for q in range(Q)]
        scale_ready = sem("scale_ready"); z_scaled = sem("z_scaled")
        masks = sem("masks")
        held = sem("held")
        mean_ready = sem("gn_mean_ready"); yc_ready = sem("yc_ready"); ysq_ready = sem("ysq_ready")
        var_ready = sem("var_ready"); ysd_ready = sem("ysd_ready"); yrs_ready = sem("yrs_ready")
        ya_ready = sem("ya_ready"); yg_ready = sem("yg_ready")
        yg_stored = sem("yg_stored")

        flat = lambda t: t[:, :, :, :, :].rearrange("p g a h d -> p (g a h d)")
        set_up = {}

        with nc.Block() as block:
            @block.gpsimd
            def _(pool):
                G = nc.gpsimd
                n = 0
                for t in (causal, lower, upper):
                    G.memset(t[:], 1.0).then_inc(masks, 1); n += 1
                for t in att_b + att_k + arx[0] + arx[1] + zt + z + [y, scale]:
                    G.memset(t[:], 0.0).then_inc(masks, 1); n += 1
                G.memset(eps[:, :], GN_EPS).then_inc(masks, 1); n += 1
                G.memset(rows[1][:, :, SG:ROW], 0.0).then_inc(masks, 1); n += 1
                G.tensor_copy(ident16[:, :], k.ident[:, :]).then_inc(masks, 1); n += 1
                pool.wait_ge(masks, n)
                for j, op in ((0, ALU.is_gt), (1, ALU.is_ge)):
                    v = causal[:, j * C:(j + 1) * C]
                    G.affine_select(out=v, in_=v, pattern=[[1, C]], compare_op=op, fill=0.0, base=0,
                                    channel_multiplier=-1).then_inc(masks, 1); n += 1
                for q in range(Q):
                    for p in range(QP):
                        for h in range(2):
                            G.tensor_copy(att_b[q][:, p, h, 0:C], k.ident[:, :]).then_inc(masks, 1); n += 1
                for table, part, sizes in ((lower, 0, LEVELS), (upper, 1, [1] + LEVELS)):
                    for j, m in enumerate(sizes):
                        v = table[:, j, :].rearrange("p (b e x) -> p b e x", e=2, x=m)
                        G.memset(v[:, :, 1 - part, :], 0.0).then_inc(masks, 1); n += 1
                        v = v[:, :, part, :]
                        row0 = m * (1 - part)
                        G.affine_select(out=v, in_=v, pattern=[[-2 * m, C // (2 * m)], [0, m]], compare_op=ALU.is_ge,
                                        fill=0.0, base=-row0, channel_multiplier=1).then_inc(masks, 1); n += 1
                        pool.wait_ge(masks, n)
                        G.affine_select(out=v, in_=v, pattern=[[2 * m, C // (2 * m)], [0, m]], compare_op=ALU.is_ge,
                                        fill=0.0, base=row0 + m - 1, channel_multiplier=-1).then_inc(masks, 1); n += 1
                pool.wait_ge(masks, n)
                G.tensor_tensor(start[:, :], k.ident[:, :], upper[:, 0, :], ALU.subtract).then_inc(masks, 1); n += 1
                pool.wait_ge(masks, n)
                set_up["n"] = n

                def finish(i, slot):
                    pool.wait_ge(yrs_ready, 2 * (i + 1))
                    pool.wait_ge(yg_ready, i)
                    G.tensor_tensor(ya[:, :, :], yn[:, :, :], rows[slot][:, :, SG:SG + C], ALU.mult)\
                     .then_inc(ya_ready, 1)
                    pool.wait_ge(ya_ready, i + 1)
                    pool.wait_ge(yg_stored, 16 * i)
                    G.tensor_tensor(yg[:, :, :], ya[:, :, :], rows[slot][:, :, SBV:SBV + C], ALU.add)\
                     .then_inc(yg_ready, 1)

                with pool.Fori(0, NI // 2) as j:
                    for u in range(2):
                        i = 2 * j + u
                        pool.wait_ge(rows_loaded[u], 16 * (j + 1))
                        pool.sem_inc(held, 1)
                        for q in range(Q):
                            for p in range(QP):
                                for h in range(2):
                                    part = slice(h * HD, (h + 1) * HD)
                                    G.tensor_copy(arx[u][q][part, p, h, :], rows[u][part, q * QP + p, SA:SB])\
                                        .then_inc(expanded, 1)
                        for q in range(Q):
                            wait_taken(pool, q, i, "mv")
                            pool.sem_inc(held, 1)
                            G.tensor_copy(flat(rhs16[q]), flat(rhs[q]))\
                             .then_inc(rhs16_ready[q], 1)
                        finish(i, 1 - u)
                finish(NI, 1)

            @block.sync
            def _(sp):
                sp.wait_ge(masks, set_up["n"])
                with sp.Fori(0, NI // 2) as j:
                    for u in range(2):
                        i = 2 * j + u
                        sp.wait_ge(yg_ready, i)
                        sp.dma_start(rows[u][:, :, :], scratch[bass.ds(i, 1), :, :, :].rearrange("o p q r -> q (o p) r"))\
                          .then_inc(rows_loaded[u], 16)
                        sp.wait_ge(yg_ready, i + 1)
                        sp.dma_start(gated[bass.ds(i, 1), :, :, :].rearrange("o p q r -> q (o p) r"), yg[:, :, :])\
                          .then_inc(yg_stored, 16)
                sp.wait_ge(yg_ready, NI + 1)
                sp.dma_start(gated[NI, :, :, :].rearrange("p q r -> q p r"), yg[:, :, :]).then_inc(yg_stored, 16)
                sp.wait_ge(yg_stored, 16 * (NI + 1))

            @block.scalar
            def _(act):
                def copy(q, i, name, out, in_, scale=1.0, last=True):
                    wait_filled(act, q, i, name)
                    ins = nc.scalar.activation(out, in_, ACT.Copy, scale=scale)
                    if last:
                        ins.then_inc(took["act"][q], 1)

                def norm_step(i):
                    act.wait_ge(yc_ready, i + 1)
                    nc.scalar.activation(ysq[:, :, :], yc[:, :, :], ACT.Square).then_inc(ysq_ready, 1)
                    act.wait_ge(var_ready, i + 1)
                    nc.scalar.activation(ysd[:, :, :], p_var[:, :].rearrange("p (a t) -> p a t", t=C), ACT.Sqrt,
                                         bias=eps[:, :], scale=1.0 / HD).then_inc(ysd_ready, 1)

                act.wait_ge(masks, set_up["n"])
                with act.Fori(0, NI // 2) as j:
                    for u in range(2):
                        i = 2 * j + u
                        for name, p in (("tok0", 0), ("tok1", 1)):
                            for q in range(Q):
                                b = bank_of(q, name)
                                copy(q, i, name, rhs[q][:, p, 0, :, :],
                                     b[:, 0:P].rearrange("p (h d) -> p h d", h=2), last=False)
                                copy(q, i, name, tok[q][:, p, :, :], b[:, P:4 * P].rearrange("p (a d) -> p a d", a=3))
                        for q in range(Q):
                            b = bank_of(q, "mv")[:, :].rearrange("p (a h e d) -> p a h e d", a=QP, h=2, e=2)
                            for h in range(2):
                                copy(q, i, "mv", rhs[q][:, :, 1, h, :], b[:, :, h, h, :], last=(h == 1))
                        for q in range(Q):
                            wait_taken(act, q, i, "b1")
                            nc.scalar.activation(lT16[q][:, :, :].rearrange("p (a h) t -> p a h t", h=2),
                                                 att_b[q][:, :, :, 0:C], ACT.Copy).then_inc(lT_ready[q], 1)
                        for q in range(Q):
                            copy(q, i, "t", t16[q][:, :, :],
                                 bank_of(q, "t")[:, 0:256].bitcast(f16).rearrange("p (h t) -> p h t", t=C))
                        for m in LEVELS:
                            for q in range(Q):
                                copy(q, i, f"u{m}", u16[q][:, :, :],
                                     bank_of(q, f"u{m}")[:, :].rearrange("p (h t) -> p h t", t=C), scale=-1.0)
                            if m == 4:
                                norm_step(i)
                        for q in range(Q):
                            copy(q, i, "z0", flat(sol[q]), bank_of(q, "z0")[:, :])
                        for q in range(Q):
                            copy(q, i, "w1T", w1T[q][:, :, :],
                                 bank_of(q, "w1T")[:, 0:QP * C].rearrange("p (a t) -> p a t", t=C))
                        for q in range(Q):
                            act.wait_ge(yc_ready, i + 1)
                            copy(q, i, "Y", y[:, q * QP:(q + 1) * QP, :],
                                 bank_of(q, "Y")[:, 0:QP * C].rearrange("p (a t) -> p a t", t=C))
                norm_step(NI)

            @block.vector
            def _(dve):
                V = nc.vector
                by_head = lambda b: b[:, :].rearrange("p (h t) -> p h t", t=C)

                def center_step(i):
                    dve.wait_ge(mean_ready, i + 1)
                    V.scalar_tensor_tensor(out=yc[:, :, :], in0=p_mean[:, :].rearrange("p (a t) -> p a t", t=C),
                                           scalar=-1.0 / HD, in1=y[:, :, :], op0=ALU.mult, op1=ALU.add)\
                     .then_inc(yc_ready, 1)

                def norm_step(i):
                    dve.wait_ge(ysd_ready, i + 1)
                    dve.wait_ge(ya_ready, i)
                    V.reciprocal(yn[:, :, :], ysd[:, :, :]).then_inc(yrs_ready, 1)
                    dve.wait_ge(yrs_ready, 2 * i + 1)
                    V.tensor_tensor(yn[:, :, :], yn[:, :, :], yc[:, :, :], ALU.mult).then_inc(yrs_ready, 1)

                dve.wait_ge(masks, set_up["n"])
                with dve.Fori(0, NI // 2) as j:
                    for u in range(2):
                        i = 2 * j + u
                        for name, dst, p in (("b0", att_b, 0), ("k0", att_k, 0), ("b1", att_b, 1), ("k1", att_k, 1)):
                            for q in range(Q):
                                wait_filled(dve, q, i, name)
                                if name == "b0":
                                    dve.wait_ge(lT_ready[q], i)
                                dve.sem_inc(held, 1)
                                V.copy_predicated(dst[q][:, p, :, :],
                                                  causal[:, :].bitcast(u32).unsqueeze(1).to_broadcast([P, 2, 2 * C]),
                                                  bank_of(q, name)[:, :].rearrange("p (h t) -> p h t", h=2))\
                                 .then_inc(took["dve"][q], 1)
                        for q in range(Q):
                            wait_taken(dve, q, i, "b1")
                            V.tensor_tensor(tT16[q][:, :, :].rearrange("p (a h) t -> p (a h) t", h=2),
                                            att_b[q][:, :, :, 0:C].rearrange("p a h t -> p (a h) t"),
                                            start[:, :].unsqueeze(1).to_broadcast([P, QH, C]), ALU.mult)\
                             .then_inc(tT_ready[q], 1)
                        for l, m in enumerate(LEVELS):
                            for q in range(Q):
                                if m != LEVELS[-1]:
                                    wait_filled(dve, q, i, f"w{m}")
                                    wait_taken(dve, q, i, "t") if l == 0 else wait_taken(dve, q, i, f"w{m // 2}")
                                    dve.sem_inc(held, 1)
                                    V.copy_predicated(t16[q][:, :, :],
                                                      lower[:, l, :].bitcast(u32).unsqueeze(1).to_broadcast([P, QH, C]),
                                                      by_head(bank_of(q, f"w{m}"))).then_inc(took["dve"][q], 1)
                                wait_filled(dve, q, i, f"wT{m}")
                                if l == 0:
                                    dve.wait_ge(tT_ready[q], i + 1)
                                else:
                                    wait_taken(dve, q, i, f"wT{m // 2}")
                                dve.sem_inc(held, 1)
                                V.copy_predicated(tT16[q][:, :, :],
                                                  upper[:, 1 + l, :].bitcast(u32).unsqueeze(1).to_broadcast([P, QH, C]),
                                                  by_head(bank_of(q, f"wT{m}"))).then_inc(took["dve"][q], 1)
                            if m == 2:
                                center_step(i)
                            if m == 8:
                                norm_step(i)
                        for n in range(2):
                            for q in range(Q):
                                wait_filled(dve, q, i, f"r{n}")
                                V.tensor_tensor(flat(res16[q]), flat(rhs[q]), bank_of(q, f"r{n}")[:, :], ALU.subtract)\
                                 .then_inc(took["dve"][q], 1)
                            for q in range(Q):
                                wait_filled(dve, q, i, f"d{n}")
                                if n == 0:
                                    wait_taken(dve, q, i, "z0")
                                else:
                                    wait_taken(dve, q, i, "d0")
                                V.tensor_tensor(flat(sol[q]), flat(sol[q]), bank_of(q, f"d{n}")[:, :], ALU.add)\
                                 .then_inc(took["dve"][q], 1)
                        dve.wait_ge(rows_loaded[u], 16 * (j + 1))
                        dve.wait_ge(scale_ready, 2 * i)
                        V.tensor_tensor(scale[:, :, :], scale[:, :, :], rows[u][:, :, SM:SM + 1], ALU.mult)\
                         .then_inc(scale_ready, 1)
                        dve.wait_ge(scale_ready, 2 * i + 1)
                        for q in range(Q):
                            dve.wait_ge(took["dve"][q], per["dve"] * i)
                            wait_filled(dve, q, i, "d1")
                            for p in range(QP):
                                V.scalar_tensor_tensor(
                                    out=z[q][:, p, :], in0=zt[q][:, p, :], scalar=scale[:, q * QP + p, :],
                                    in1=k.ones_head[:, :], op0=ALU.mult, op1=ALU.mult).then_inc(z_scaled, 1)
                        dve.wait_ge(z_scaled, HP * (i + 1))
                        V.tensor_copy(scale[:, :, :], rows[u][:, :, SE:SE + 1]).then_inc(scale_ready, 1)
                        for q in range(Q):
                            wait_filled(dve, q, i, "U")
                            wait_taken(dve, q, i, "d1")
                            V.scalar_tensor_tensor(
                                out=U[q][:, :, :], in0=bank_of(q, "U")[:, 0:QP * P].rearrange("p (g d) -> p g d", g=QP),
                                scalar=-1.0, in1=sol[q][:, :, 1, :, :].rearrange("p g h d -> p g (h d)"), op0=ALU.mult, op1=ALU.subtract).then_inc(took["dve"][q], 1)
                        for q in range(Q):
                            wait_filled(dve, q, i, "zn")
                            V.tensor_tensor(zt[q][:, :, :], z[q][:, :, :],
                                            bank_of(q, "zn")[:, 0:QP * P].rearrange("p (a d) -> p a d", a=QP),
                                            ALU.add).then_inc(took["dve"][q], 1)
                center_step(NI)
                norm_step(NI)

            @block.tensor
            def _(pe):
                T = nc.tensor
                pe.wait_ge(masks, set_up["n"])

                def sum_mean(i):
                    for q in range(Q):
                        pe.wait_ge(took["act"][q], per["act"] * i)
                    pe.wait_ge(yc_ready, i)
                    T.matmul(p_mean[:, :], k.ones_head[:, :], y[:, :, :].rearrange("p a t -> p (a t)"),
                             start=True, stop=True).then_inc(mean_ready, 1)

                def sum_var(i):
                    pe.wait_ge(ysq_ready, i + 1)
                    pe.wait_ge(ysd_ready, i)
                    T.matmul(p_var[:, :], k.ones_head[:, :], ysq[:, :, :].rearrange("p a t -> p (a t)"),
                             start=True, stop=True).then_inc(var_ready, 1)

                with pe.Fori(0, NI // 2) as j:
                    for u in range(2):
                        i = 2 * j + u
                        pe.wait_ge(rows_loaded[u], 16 * (j + 1))
                        for p in range(QP):
                            for q in range(Q):
                                wait_bank(pe, q, i, f"tok{p}")
                                b = bank_of(q, f"tok{p}")
                                for n, at in enumerate((SA, SB, SK, SV)):
                                    mm = T.transpose(b[:, n * P:(n + 1) * P], rows[u][:, q * QP + p, at:at + C],
                                                     k.ident[:, :])
                                mm.then_inc(filled[q], 1)
                        for p in range(QP):
                            for q in range(Q):
                                pe.wait_ge(expanded, 2 * HP * i + 2 * (q * QP + p) + 2)
                                for name, at in ((f"b{p}", SB), (f"k{p}", SK)):
                                    wait_bank(pe, q, i, name)
                                    T.matmul(bank_of(q, name)[:, :], rows[u][:, q * QP + p, at:at + C],
                                             arx[u][q][:, p, :, :].rearrange("p h t -> p (h t)"),
                                             start=True, stop=True).then_inc(filled[q], 1)
                        for q in range(Q):
                            wait_bank(pe, q, i, "mv", "k1", "tok1")
                            for h in range(QH):
                                mm = T.matmul(bank_of(q, "mv")[:, h * P:(h + 1) * P], att_k[q][:, h // 2, h % 2, 0:C],
                                              tok[q][:, h // 2, 2, :], start=True, stop=True)
                            mm.then_inc(filled[q], 1)
                        for q in range(Q):
                            wait_bank(pe, q, i, "t")
                            pe.wait_ge(tT_ready[q], i + 1)
                            for h in range(QH):
                                mm = T.transpose(bank_of(q, "t")[:, 64 * h:64 * (h + 1)].bitcast(f16), tT16[q][:, h, :],
                                                 ident16[:, :])
                            mm.then_inc(filled[q], 1)
                        for l, m in enumerate(LEVELS):
                            for q in range(Q):
                                wait_bank(pe, q, i, f"u{m}", "t" if l == 0 else f"w{m // 2}")
                                if l == 0:
                                    pe.wait_ge(lT_ready[q], i + 1)
                                for h in range(QH):
                                    mm = T.matmul(bank_of(q, f"u{m}")[:, h * C:(h + 1) * C], lT16[q][:, h, :],
                                                  t16[q][:, h, :], start=True, stop=True)
                                mm.then_inc(filled[q], 1)
                            if m == 2:
                                sum_mean(i)
                            if m == 8:
                                sum_var(i)
                            for q in range(Q):
                                needs = [f"u{m}"] + ([f"wT{m // 2}"] if l > 0 else [])
                                if m != LEVELS[-1]:
                                    wait_bank(pe, q, i, f"w{m}", *needs)
                                    for h in range(QH):
                                        mm = T.matmul(bank_of(q, f"w{m}")[:, h * C:(h + 1) * C], tT16[q][:, h, :],
                                                      u16[q][:, h, :], start=True, stop=True)
                                    mm.then_inc(filled[q], 1)
                                wait_bank(pe, q, i, f"wT{m}", *needs)
                                for h in range(QH):
                                    mm = T.matmul(bank_of(q, f"wT{m}")[:, h * C:(h + 1) * C], u16[q][:, h, :],
                                                  tT16[q][:, h, :], start=True, stop=True)
                                mm.then_inc(filled[q], 1)

                        def solve(name, lhs, right):
                            for h in range(QH):
                                out = bank_of(q, name)[:, :].rearrange("p (g a h d) -> p g a h d", g=QP, a=2, h=2)
                                mm = T.matmul(out[:, h // 2, :, h % 2, :], lhs(h), right[:, h // 2, :, h % 2, :],
                                              start=True, stop=True)
                            mm.then_inc(filled[q], 1)

                        for q in range(Q):
                            wait_bank(pe, q, i, "z0", f"wT{LEVELS[-1]}")
                            pe.wait_ge(rhs16_ready[q], i + 1)
                            solve("z0", lambda h: tT16[q][:, h, :], rhs16[q])
                        for n in range(2):
                            for q in range(Q):
                                wait_bank(pe, q, i, f"r{n}", "z0" if n == 0 else "d0")
                                solve(f"r{n}", lambda h: att_b[q][:, h // 2, h % 2, 0:C],
                                      sol[q])
                            for q in range(Q):
                                wait_bank(pe, q, i, f"d{n}", f"r{n}")
                                solve(f"d{n}", lambda h: tT16[q][:, h, :], res16[q])
                        for q in range(Q):
                            wait_bank(pe, q, i, "w1T", "d1")
                            for p in range(QP):
                                mm = T.transpose(bank_of(q, "w1T")[:, p * C:(p + 1) * C], sol[q][:, p, 0, :, :].rearrange("p h d -> p (h d)"),
                                                 k.ident[:, :])
                            mm.then_inc(filled[q], 1)
                        for q in range(Q):
                            wait_bank(pe, q, i, "U", "w1T")
                            pe.wait_ge(z_scaled, HP * (i + 1))
                            for p in range(QP):
                                mm = T.matmul(bank_of(q, "U")[:, p * P:(p + 1) * P], w1T[q][:, p, :], z[q][:, p, :],
                                              start=True, stop=True)
                            mm.then_inc(filled[q], 1)
                        for q in range(Q):
                            wait_bank(pe, q, i, "zn", "U")
                            for p in range(QP):
                                out = bank_of(q, "zn")[:, p * P:(p + 1) * P]
                                T.matmul(out, tok[q][:, p, 0, :], U[q][:, p, :], start=True, stop=False)
                                mm = T.matmul(out, tok[q][:, p, 1, :], tok[q][:, p, 2, :], start=False, stop=True)
                            mm.then_inc(filled[q], 1)
                        for q in range(Q):
                            wait_bank(pe, q, i, "Y")
                            b = bank_of(q, "Y")
                            for p in range(QP):
                                cols = slice(p * C, (p + 1) * C)
                                T.matmul(b[:, cols], z[q][:, p, :], rows[u][:, q * QP + p, SR:SR + C],
                                         start=True, stop=False, skip_group_check=True)
                                for of, att, last in (("U", att_b, False), ("V", att_k, True)):
                                    for h in range(2):
                                        part = slice(h * HD, (h + 1) * HD)
                                        left = U[q][:, p, part] if of == "U" else tok[q][:, p, 2, part]
                                        mm = T.matmul(b[part, cols], left, att[q][:, p, h, C:2 * C],
                                                      start=False, stop=last, skip_group_check=True)
                            mm.then_inc(filled[q], 1)
                sum_mean(NI)
                sum_var(NI)


def attend_out(nc, k, a, gated, h_dram, y2_dram):
    NB = S // P
    HALVES = D // 512
    x_rows = a["x"][0, :, :].rearrange("(n p) d -> n p d", p=P)
    with ExitStack() as c:
        sb = lambda n, s, d=f32: c.enter_context(nc.sbuf_tensor(n, s, d))
        ps = lambda n: c.enter_context(nc.psum_tensor(n, [P, 512], f32))
        sem = lambda n: c.enter_context(nc.semaphore(n))
        w_o = sb("w_o", [P, KC, D])
        post_g = sb("post_g", [P, D])
        gT = [sb(f"gT{s}", [P, KC, P]) for s in range(2)]
        xr = [sb(f"xr{s}", [P, D]) for s in range(2)]
        squares = sb("squares", [P, D])
        ss = [sb(f"ss{s}", [P, 2]) for s in range(2)]
        rs = [sb(f"rs{s}", [P, 1]) for s in range(2)]
        ss2 = [sb(f"ss2_{s}", [P, 1]) for s in range(2)]
        rs2 = [sb(f"rs2_{s}", [P, 1]) for s in range(2)]
        h = [sb(f"h{s}", [P, D]) for s in range(2)]
        hn = [sb(f"hn{s}", [P, D]) for s in range(2)]
        y2 = [sb(f"y2_{s}", [P, KC, P]) for s in range(2)]
        eps = sb("eps_c", [P, 1])
        pO = [[ps(f"pO{s}_{j}") for j in range(HALVES)] for s in range(2)]
        pT = [ps(f"pT{j}") for j in range(2)]
        w_loaded = sem("wo_loaded"); g_loaded = [sem(f"g_loaded{s}") for s in range(2)]
        xr_loaded = [sem(f"xr_loaded{s}") for s in range(2)]
        o_ready = sem("o_ready"); squared = sem("squared"); mean1 = sem("mean1"); root1 = sem("root1")
        rs_ready = sem("rs_ready"); scaled = sem("scaled"); h_ready = sem("h_ready"); squared2 = sem("squared2")
        mean2 = sem("mean2"); root2 = sem("root2"); rs2_ready = sem("rs2_ready"); hn_ready = sem("hn_ready")
        t_ready = sem("t_ready"); y2_ready = sem("y2_ready"); eps_set = sem("eps_set")
        h_stored = [sem(f"h_stored{s}") for s in range(2)]; y2_stored = [sem(f"y2_stored{s}") for s in range(2)]

        with nc.Block() as block:
            @block.sync
            def _(sp):
                sp.dma_start(w_o[:, :, :], a["rwkv_w_o"][0, :, :].rearrange("(c p) f -> p c f", p=P)).then_inc(w_loaded, 16)
                sp.dma_start(post_g[:, :], a["norm_g"][0, 1:2, :].to_broadcast([P, D])).then_inc(w_loaded, 16)
                with sp.Fori(0, NB // 2) as j:
                    for s in range(2):
                        n = 2 * j + s
                        sp.wait_ge(o_ready, 2 * (2 * j))
                        for half in range(2):
                            sp.dma_start(gT[s][:, half * HP:(half + 1) * HP, :],
                                         gated[bass.ds(half * NCH + 1 + n, 1), :, :, :].rearrange("o p q r -> q (o p) r"))\
                              .then_inc(g_loaded[s], 16)
                        sp.wait_ge(h_ready, 2 * (2 * j))
                        sp.dma_start(xr[s][:, :], x_rows[bass.ds(n, 1), :, :].rearrange("o p d -> p (o d)"))\
                          .then_inc(xr_loaded[s], 16)

            @block.gpsimd
            def _(pool):
                nc.gpsimd.memset(eps[:, :], NORM_EPS).then_inc(eps_set, 1)
                with pool.Fori(0, NB // 2) as j:
                    for s in range(2):
                        n = 2 * j + s
                        pool.wait_ge(h_ready, 2 * (n + 1))
                        pool.dma_start(h_dram[bass.ds(n, 1), :, :].rearrange("o p d -> p (o d)"), h[s][:, :])\
                            .then_inc(h_stored[s], 16)
                        pool.wait_ge(y2_ready, 2 * (n + 1))
                        pool.dma_start(y2_dram[:, :, bass.ts(n, P)], y2[s][:, :, :]).then_inc(y2_stored[s], 16)
                for s in range(2):
                    pool.wait_ge(h_stored[s], 16 * (NB // 2))
                    pool.wait_ge(y2_stored[s], 16 * (NB // 2))

            @block.tensor
            def _(pe):
                pe.wait_ge(w_loaded, 32)
                with pe.Fori(0, NB // 2) as j:
                    for s in range(2):
                        pe.wait_ge(g_loaded[s], 32 * (j + 1))
                        pe.wait_ge(scaled, 4 * j)
                        for half in range(HALVES):
                            for q in range(KC):
                                mm = nc.tensor.matmul(pO[s][half][:, :], gT[s][:, q, :],
                                                      w_o[:, q, half * 512:(half + 1) * 512],
                                                      start=(q == 0), stop=(q == KC - 1))
                            mm.then_inc(o_ready, 1)
                    for s in range(2):
                        pe.wait_ge(hn_ready, 2 * j + s + 1)
                        pe.wait_ge(y2_ready, 2 * (2 * j + s))
                        for i in range(2):
                            for q in range(4):
                                mm = nc.tensor.transpose(pT[i][:, q * P:(q + 1) * P],
                                                         hn[s][:, (4 * i + q) * P:(4 * i + q + 1) * P], k.ident[:, :])
                            mm.then_inc(t_ready, 1)

            @block.scalar
            def _(act):
                act.wait_ge(eps_set, 1)
                with act.Fori(0, NB // 2) as j:
                    def first(s):
                        n = 2 * j + s
                        act.wait_ge(rs_ready, n)
                        for half in range(HALVES):
                            act.wait_ge(o_ready, 2 * n + half + 1)
                            nc.scalar.activation(squares[:, half * 512:(half + 1) * 512], pO[s][half][:, :], ACT.Square,
                                                 accum_out=ss[s][:, half:half + 1]).then_inc(squared, 1)
                        act.wait_ge(mean1, n + 1)
                        nc.scalar.activation(rs[s][:, :], ss[s][:, 0:1], ACT.Sqrt, bias=eps[:, :], scale=1.0 / D)\
                            .then_inc(root1, 1)

                    def second(s):
                        n = 2 * j + s
                        act.wait_ge(h_ready, 2 * (n + 1))
                        act.wait_ge(squared, 2 * (2 * j + 1) + 2 * s)
                        act.wait_ge(squared2, n)
                        nc.scalar.activation(squares[:, :], h[s][:, :], ACT.Square, accum_out=ss2[s][:, :])\
                            .then_inc(squared2, 1)
                        act.wait_ge(squared2, n + 1)
                        nc.scalar.activation(rs2[s][:, :], ss2[s][:, :], ACT.Sqrt, bias=eps[:, :], scale=1.0 / D)\
                            .then_inc(root2, 1)

                    first(0)
                    second(0)
                    first(1)
                    second(1)

            @block.vector
            def _(dve):
                V = nc.vector
                dve.wait_ge(w_loaded, 32)
                with dve.Fori(0, NB // 2) as j:
                    for s in range(2):
                        n = 2 * j + s
                        dve.wait_ge(squared, 2 * (n + 1))
                        V.tensor_tensor(ss[s][:, 0:1], ss[s][:, 0:1], ss[s][:, 1:2], ALU.add).then_inc(mean1, 1)
                        dve.wait_ge(root1, n + 1)
                        V.reciprocal(rs[s][:, :], rs[s][:, :]).then_inc(rs_ready, 1)
                        dve.wait_ge(rs_ready, n + 1)
                        dve.wait_ge(h_stored[s], 16 * j)
                        for half in range(HALVES):
                            cols = slice(half * 512, (half + 1) * 512)
                            V.scalar_tensor_tensor(out=h[s][:, cols], in0=pO[s][half][:, :], scalar=rs[s][:, :],
                                                   in1=post_g[:, cols], op0=ALU.mult, op1=ALU.mult).then_inc(scaled, 1)
                        dve.wait_ge(xr_loaded[s], 16 * (j + 1))
                        for half in range(HALVES):
                            cols = slice(half * 512, (half + 1) * 512)
                            dve.wait_ge(scaled, 2 * n + half + 1)
                            V.tensor_tensor(h[s][:, cols], h[s][:, cols], xr[s][:, cols], ALU.add).then_inc(h_ready, 1)
                        dve.wait_ge(root2, n + 1)
                        V.reciprocal(rs2[s][:, :], rs2[s][:, :]).then_inc(rs2_ready, 1)
                        dve.wait_ge(rs2_ready, n + 1)
                        V.tensor_scalar(hn[s][:, :], h[s][:, :], rs2[s][:, :], None, ALU.mult).then_inc(hn_ready, 1)
                    for s in range(2):
                        n = 2 * j + s
                        dve.wait_ge(y2_stored[s], 16 * j)
                        for i in range(2):
                            dve.wait_ge(t_ready, 2 * n + i + 1)
                            V.tensor_tensor(y2[s][:, 4 * i:4 * i + 4, :], pT[i][:, :].rearrange("p (c t) -> p c t", t=P),
                                            k.vec[:, G2 + 4 * i:G2 + 4 * i + 4].unsqueeze(2).to_broadcast([P, 4, P]),
                                            ALU.mult).then_inc(y2_ready, 1)


def ffn(nc, k, a, h_dram, y2_dram, out):
    T = 512
    NT = S // T
    TB = T // P
    HALVES = D // 512
    NW = 2
    w_in = a["ffn_w_in"][0, :, :].rearrange("(c p) f -> p c f", p=P)
    out_rows = out[0, :, :].rearrange("(n p) d -> n p d", p=P)
    with ExitStack() as c:
        sb = lambda n, s, d=f32: c.enter_context(nc.sbuf_tensor(n, s, d))
        ps = lambda n: c.enter_context(nc.psum_tensor(n, [P, 512], f32))
        sem = lambda n: c.enter_context(nc.semaphore(n))
        w_out = sb("w_out", [P, FC, D])
        post_g = sb("post_g3", [P, D])
        y2 = sb("y2_tile", [P, KC, T])
        wg = [sb(f"wg{s}", [P, KC, P]) for s in range(NW)]
        wu = [sb(f"wu{s}", [P, KC, P]) for s in range(NW)]
        acts = sb("acts", [P, FC, T])
        halo = sb("halo", [P, FC, 2])
        gate = [sb(f"gate{s}", [P, T + 2]) for s in range(2)]
        conv = [sb(f"conv{s}", [P, T]) for s in range(2)]
        conv_rows = sb("conv_rows", [4 * FC, P])
        conv_vec = sb("conv_vec", [P, 4, FC])
        hb = [sb(f"hb{s}", [P, D]) for s in range(2)]
        normed = sb("normed", [P, D])
        squares = sb("squares_f", [P, 512]); ss = sb("ss_f", [P, 2]); rs = sb("rs_f", [P, 1]); eps = sb("eps_f", [P, 1])
        pg = [ps(f"pg{s}") for s in range(2)]
        pu = [ps(f"pu{s}") for s in range(2)]
        po = [[ps(f"po{s}_{h}") for h in range(HALVES)] for s in range(2)]
        w_out_loaded = sem("w_out_loaded"); conv_loaded = sem("conv_loaded"); y2_loaded = sem("y2_loaded")
        w_loaded = [sem(f"w_in_loaded{s}") for s in range(NW)]; hb_loaded = [sem(f"hb_loaded{s}") for s in range(2)]
        held = sem("held_f")
        conv_t = sem("conv_t"); set_up = sem("set_up_f")
        gate_made = sem("gate_made"); up_made = sem("up_made"); gate_copied = sem("gate_copied"); halo_in = sem("halo_in")
        halo_out = sem("halo_out"); conv0 = sem("conv0"); conv1 = sem("conv1"); conv2 = sem("conv2")
        silu_ready = sem("silu_ready"); act_ready = sem("act_ready")
        o_made = sem("o_made"); squared = sem("squared_f"); mean = sem("mean_f"); root = sem("root_f")
        rs_ready = sem("rs_ready_f"); scaled = sem("scaled_f"); out_ready = sem("out_ready")
        out_stored = [sem(f"out_stored{s}") for s in range(2)]

        with nc.Block() as block:
            @block.sync
            def _(sp):
                sp.dma_start(conv_rows[0:3 * FC, :], a["ffn_conv_w"][0, :, :].rearrange("w (c p) -> (w c) p", p=P))\
                  .then_inc(conv_loaded, 16)
                sp.dma_start(conv_rows[3 * FC:4 * FC, :], a["ffn_conv_b"][0, :].rearrange("(c p) -> c p", p=P))\
                  .then_inc(conv_loaded, 16)
                with sp.Fori(0, NT) as tt:
                    sp.wait_ge(up_made, FC * tt)
                    sp.dma_start(y2[:, :, :], y2_dram[:, :, bass.ts(tt, T)]).then_inc(y2_loaded, 16)
                    with sp.Fori(0, FC // 2) as g:
                        for s in range(2):
                            f = 2 * g + s
                            sp.wait_ge(up_made, FC * tt + 2 * g)
                            sp.dma_start(wg[s][:, :, :], w_in[:, :, bass.ts(f, P)]).then_inc(w_loaded[s], 16)
                            sp.dma_start(wu[s][:, :, :], w_in[:, :, bass.ds(f * P + F, P)]).then_inc(w_loaded[s], 16)

            def store(pool, tt, b):
                pool.wait_ge(out_ready, 2 * (TB * tt + b + 1))
                pool.sem_inc(held, 1)
                pool.dma_start(out_rows[bass.ds(TB * tt + b, 1), :, :].rearrange("o p d -> p (o d)"), hb[b % 2][:, :])\
                    .then_inc(out_stored[b % 2], 16)

            @block.gpsimd
            def _(pool):
                nc.gpsimd.memset(eps[:, :], NORM_EPS).then_inc(set_up, 1)
                nc.gpsimd.memset(halo[:, :, :], 0.0).then_inc(set_up, 1)
                pool.dma_start(w_out[:, :, :], a["ffn_w_out"][0, :, :].rearrange("(c p) f -> p c f", p=P))\
                    .then_inc(w_out_loaded, 16)
                pool.dma_start(post_g[:, :], a["norm_g"][0, 3:4, :].to_broadcast([P, D])).then_inc(w_out_loaded, 16)
                with pool.Fori(0, NT) as tt:
                    for b in range(TB):
                        s = b % 2
                        if b >= 2:
                            pool.wait_ge(out_stored[s], 16 * (TB // 2 * tt + b // 2))
                        else:
                            pool.wait_ge(out_stored[s], 16 * (TB // 2) * tt)
                        pool.dma_start(hb[s][:, :], h_dram[bass.ds(TB * tt + b, 1), :, :].rearrange("o p d -> p (o d)"))\
                            .then_inc(hb_loaded[s], 16)
                        if b >= 1:
                            store(pool, tt, b - 1)
                    store(pool, tt, TB - 1)
                for s in range(2):
                    pool.wait_ge(out_stored[s], 16 * (TB // 2) * NT)

            @block.tensor
            def _(pe):
                pe.wait_ge(conv_loaded, 32)
                nc.tensor.transpose(po[0][0][:, 0:4 * FC], conv_rows[:, :], k.ident[0:4 * FC, 0:4 * FC]).then_inc(conv_t, 1)
                with pe.Fori(0, NT) as tt:
                    with pe.Fori(0, FC // 2) as g:
                        pe.wait_ge(y2_loaded, 16 * (tt + 1))
                        for s in range(2):
                            pe.wait_ge(w_loaded[s], 32 * (FC // 2 * tt + g + 1))
                            pe.wait_ge(gate_copied, FC * tt + 2 * g)
                            for q in range(KC):
                                mm = nc.tensor.matmul(pg[s][:, :], wg[s][:, q, :], y2[:, q, :],
                                                      start=(q == 0), stop=(q == KC - 1))
                            mm.then_inc(gate_made, 1)
                            pe.wait_ge(act_ready, FC * tt + 2 * g)
                            for q in range(KC):
                                mm = nc.tensor.matmul(pu[s][:, :], wu[s][:, q, :], y2[:, q, :],
                                                      start=(q == 0), stop=(q == KC - 1))
                            mm.then_inc(up_made, 1)
                    pe.wait_ge(act_ready, FC * (tt + 1))
                    pe.wait_ge(w_out_loaded, 32)
                    pe.wait_ge(set_up, 3)
                    for b in range(TB):
                        s = b % 2
                        if b >= 2:
                            pe.wait_ge(scaled, 2 * (TB * tt + b - 1))
                        else:
                            pe.wait_ge(scaled, 2 * TB * tt)
                        for half in range(HALVES):
                            for f in range(FC):
                                mm = nc.tensor.matmul(po[s][half][:, :], acts[:, f, b * P:(b + 1) * P],
                                                      w_out[:, f, half * 512:(half + 1) * 512],
                                                      start=(f == 0), stop=(f == FC - 1))
                            mm.then_inc(o_made, 1)

            @block.scalar
            def _(act):
                act.wait_ge(set_up, 2)
                with act.Fori(0, NT) as tt:
                    with act.Fori(0, FC // 2) as g:
                        for s in range(2):
                            n = FC * tt + 2 * g + s
                            act.wait_ge(gate_made, n + 1)
                            act.wait_ge(conv2, FC * tt + 2 * g)
                            act.wait_ge(halo_out, FC * tt + 2 * g)
                            nc.scalar.activation(gate[s][:, 2:T + 2], pg[s][:, :], ACT.Copy).then_inc(gate_copied, 1)
                            act.wait_ge(conv2, n + 1)
                            nc.scalar.activation(conv[s][:, :], conv[s][:, :], ACT.Silu).then_inc(silu_ready, 1)
                    for b in range(TB):
                        n = TB * tt + b
                        for half in range(HALVES):
                            act.wait_ge(o_made, 2 * n + half + 1)
                            act.wait_ge(squared, 2 * n + half)
                            if half == 0:
                                act.wait_ge(root, n)
                            nc.scalar.activation(squares[:, :], po[b % 2][half][:, :], ACT.Square,
                                                 accum_out=ss[:, half:half + 1]).then_inc(squared, 1)
                        act.wait_ge(mean, n + 1)
                        act.wait_ge(scaled, 2 * n)
                        nc.scalar.activation(rs[:, :], ss[:, 0:1], ACT.Sqrt, bias=eps[:, :], scale=1.0 / D)\
                            .then_inc(root, 1)

            @block.vector
            def _(dve):
                V = nc.vector
                dve.wait_ge(conv_t, 1)
                dve.wait_ge(set_up, 2)
                V.tensor_copy(conv_vec[:, :, :].rearrange("p w c -> p (w c)"), po[0][0][:, 0:4 * FC]).then_inc(set_up, 1)
                dve.wait_ge(set_up, 3)
                with dve.Fori(0, NT) as tt:
                    with dve.Fori(0, FC // 2) as g:
                        for s in range(2):
                            f = 2 * g + s
                            n = FC * tt + f
                            weight = lambda w: conv_vec[:, w, bass.ds(f, 1)]
                            dve.wait_ge(conv2, FC * tt + 2 * g)
                            V.tensor_copy(gate[s][:, 0:2], halo[:, bass.ds(f, 1), :].rearrange("p o t -> p (o t)"))\
                             .then_inc(halo_in, 1)
                            dve.wait_ge(gate_copied, n + 1)
                            dve.wait_ge(act_ready, FC * tt + 2 * g)
                            V.tensor_scalar(conv[s][:, :], gate[s][:, 2:T + 2], weight(2), weight(3), ALU.mult, ALU.add)\
                             .then_inc(conv0, 1)
                            dve.wait_ge(halo_in, n + 1)
                            V.tensor_scalar(halo[:, bass.ds(f, 1), :].rearrange("p o t -> p (o t)"),
                                            gate[s][:, T:T + 2], 1.0, None, ALU.mult)\
                             .then_inc(halo_out, 1)
                            dve.wait_ge(conv0, n + 1)
                            V.scalar_tensor_tensor(out=conv[s][:, :], in0=gate[s][:, 1:T + 1], scalar=weight(1),
                                                   in1=conv[s][:, :], op0=ALU.mult, op1=ALU.add).then_inc(conv1, 1)
                            dve.wait_ge(conv1, n + 1)
                            V.scalar_tensor_tensor(out=conv[s][:, :], in0=gate[s][:, 0:T], scalar=weight(0),
                                                   in1=conv[s][:, :], op0=ALU.mult, op1=ALU.add).then_inc(conv2, 1)
                            dve.wait_ge(silu_ready, n + 1)
                            dve.wait_ge(up_made, n + 1)
                            dve.wait_ge(o_made, 2 * TB * tt)
                            V.tensor_tensor(acts[:, bass.ds(f, 1), :].rearrange("p o t -> p (o t)"), conv[s][:, :],
                                            pu[s][:, :], ALU.mult).then_inc(act_ready, 1)
                    for b in range(TB):
                        n = TB * tt + b
                        s = b % 2
                        dve.wait_ge(squared, 2 * (n + 1))
                        V.tensor_tensor(ss[:, 0:1], ss[:, 0:1], ss[:, 1:2], ALU.add).then_inc(mean, 1)
                        dve.wait_ge(root, n + 1)
                        V.reciprocal(rs[:, :], rs[:, :]).then_inc(rs_ready, 1)
                        dve.wait_ge(rs_ready, n + 1)
                        dve.wait_ge(out_ready, 2 * n)
                        dve.wait_ge(hb_loaded[s], 16 * (TB // 2 * tt + b // 2 + 1))
                        for half in range(HALVES):
                            cols = slice(half * 512, (half + 1) * 512)
                            V.scalar_tensor_tensor(out=normed[:, cols], in0=po[s][half][:, :], scalar=rs[:, :],
                                                   in1=post_g[:, cols], op0=ALU.mult, op1=ALU.mult).then_inc(scaled, 1)
                        for half in range(HALVES):
                            cols = slice(half * 512, (half + 1) * 512)
                            dve.wait_ge(scaled, 2 * n + half + 1)
                            V.tensor_tensor(hb[s][:, cols], hb[s][:, cols], normed[:, cols], ALU.add)\
                             .then_inc(out_ready, 1)


def trunk(nc: bass.Bass, a, out):
    scratch = nc.dram_tensor("scratch_rows", [2 * NCH, HP, P, ROW], f32, kind="Internal").ap()
    gated = nc.dram_tensor("gated", [2 * NCH + 1, HP, P, C], f32, kind="Internal").ap()
    h_dram = nc.dram_tensor("h_dram", [S // P, P, D], f32, kind="Internal").ap()
    y2_dram = nc.dram_tensor("y2_dram", [P, KC, S], f32, kind="Internal").ap()
    with ExitStack() as ctx:
        k = constants(nc, ctx, a)
        project(nc, k, a, scratch)
        recur(nc, k, scratch, gated)
        attend_out(nc, k, a, gated, h_dram, y2_dram)
        ffn(nc, k, a, h_dram, y2_dram, out)


_INS = ["x", "norm_g", "ffn_w_in", "ffn_conv_w", "ffn_conv_b", "ffn_w_out", "rwkv_mu", "rwkv_w_rkv", "rwkv_w0",
        "rwkv_w1", "rwkv_w2", "rwkv_a0", "rwkv_a1", "rwkv_a2", "rwkv_g1", "rwkv_g2", "rwkv_k_k", "rwkv_k_a",
        "rwkv_r_k", "rwkv_ln_w", "rwkv_ln_b", "rwkv_w_o"]


def kernel(**inputs):
    import numpy as _np
    import concourse.bacc as _bacc
    from concourse import mybir as _mybir
    from concourse.bass_utils import run_bass_kernel_spmd as _run

    nc = _bacc.Bacc("TRN2", target_bir_lowering=False, num_devices=1)
    arrays, args = {}, {}
    for name in _INS:
        a = _np.ascontiguousarray(inputs[name])
        arrays[f"in_{name}_dram"] = a
        args[name] = nc.dram_tensor(f"in_{name}_dram", a.shape, _mybir.dt.from_np(a.dtype), kind="ExternalInput").ap()
    out = nc.dram_tensor("out_0_dram", (1, S, D), _mybir.dt.float32, kind="ExternalOutput").ap()
    trunk(nc, args, out)
    r = _run(nc, [arrays], core_ids=[0])
    return r.results[0]["out_0_dram"]
```

```python
import concourse.bass as bass
from concourse import mybir
from contextlib import ExitStack

import numpy as np

f32 = mybir.dt.float32
f16 = mybir.dt.float16
bf16 = mybir.dt.bfloat16
u32 = mybir.dt.uint32
f32r = mybir.dt.float32r
ALU = mybir.AluOpType
ACT = mybir.ActivationFunctionType

P = 128
D = 1024
S = 2048
KC = D // P
HD = 64
C = 128
NCH = S // C
LW, LA, LG = 64, 64, 128
F = 2816
FC = F // P
NORM_EPS = 1e-6
GN_EPS = 64e-5
CREDIT = 64
DECAY = float(np.exp(-0.5))

G0, MU, W0, A0, K_K, K_A, R_K, LN_W, LN_B, G2 = 0, 8, 56, 64, 72, 80, 88, 96, 104, 112
NV = 120
SA, SR, SB, SK, SV, SG, SBV, SM, SE = 0, 128, 256, 384, 512, 640, 768, 896, 897
ROW = 898


class Consts:
    pass


def constants(nc, ctx, a):
    k = Consts()
    sb = lambda n, s, d=f32: ctx.enter_context(nc.sbuf_tensor(n, s, d))
    k.ident = sb("ident", [P, P])
    k.ones_head = sb("ones_head", [P, P])
    k.vec = sb("vec", [P, NV])
    k.w0_half = sb("w0_half", [P, KC])
    k.a0_half = sb("a0_half", [P, KC])
    k.one_less_ka = sb("one_less_ka", [P, KC])
    with ExitStack() as c:
        rows = c.enter_context(nc.sbuf_tensor("vec_rows", [P, P], f32))
        pv = c.enter_context(nc.psum_tensor("pv", [P, P], f32))
        sem = lambda n: c.enter_context(nc.semaphore(n))
        rows_loaded, built, transposed, copied = sem("rows_loaded"), sem("built"), sem("transposed"), sem("copied")
        with nc.Block() as block:
            @block.sync
            def _(sp):
                lots = [(G0, a["norm_g"][0, 0, :]), (W0, a["rwkv_w0"][0, :]), (A0, a["rwkv_a0"][0, :]),
                        (K_K, a["rwkv_k_k"][0, :]), (K_A, a["rwkv_k_a"][0, :]), (LN_W, a["rwkv_ln_w"][0, :]),
                        (LN_B, a["rwkv_ln_b"][0, :]), (G2, a["norm_g"][0, 2, :])]
                for at, v in lots:
                    sp.dma_start(rows[at:at + KC, :], v.rearrange("(c p) -> c p", p=P)).then_inc(rows_loaded, 16)
                sp.dma_start(rows[R_K:R_K + KC, :],
                             a["rwkv_r_k"][0, :, :].rearrange("(c h) n -> c (h n)", h=2)).then_inc(rows_loaded, 16)
                sp.dma_start(rows[MU:MU + 6 * KC, :],
                             a["rwkv_mu"][0, :, :].rearrange("m (c p) -> (m c) p", p=P)).then_inc(rows_loaded, 16)

            @block.gpsimd
            def _(pool):
                nc.gpsimd.memset(k.ident[:, :], 0.0).then_inc(built, 1)
                nc.gpsimd.memset(k.ones_head[:, :], 1.0).then_inc(built, 1)
                pool.wait_ge(built, 2)
                nc.gpsimd.affine_select(out=k.ident[:, :], in_=k.ident[:, :], pattern=[[-1, P]],
                                        compare_op=ALU.not_equal, fill=1.0, base=0,
                                        channel_multiplier=1).then_inc(built, 1)
                nc.gpsimd.affine_select(out=k.ones_head[:, 0:HD], in_=k.ones_head[:, 0:HD], pattern=[[0, HD]],
                                        compare_op=ALU.is_ge, fill=0.0, base=HD - 1,
                                        channel_multiplier=-1).then_inc(built, 1)
                nc.gpsimd.affine_select(out=k.ones_head[:, HD:P], in_=k.ones_head[:, HD:P], pattern=[[0, HD]],
                                        compare_op=ALU.is_ge, fill=0.0, base=-HD,
                                        channel_multiplier=1).then_inc(built, 1)

            @block.tensor
            def _(pe):
                pe.wait_ge(built, 5)
                pe.wait_ge(rows_loaded, 160)
                nc.tensor.transpose(pv[:, 0:NV], rows[0:NV, :], k.ident[0:NV, 0:NV]).then_inc(transposed, 1)

            @block.vector
            def _(dve):
                dve.wait_ge(transposed, 1)
                nc.vector.tensor_copy(k.vec[:, :], pv[:, 0:NV]).then_inc(copied, 1)
                dve.wait_ge(copied, 1)
                nc.vector.tensor_scalar(k.w0_half[:, :], k.vec[:, W0:W0 + KC], 0.5, None, ALU.mult).then_inc(copied, 1)
                nc.vector.tensor_scalar(k.a0_half[:, :], k.vec[:, A0:A0 + KC], 0.5, None, ALU.mult).then_inc(copied, 1)
                nc.vector.tensor_scalar(k.one_less_ka[:, :], k.vec[:, K_A:K_A + KC], -1.0, 1.0,
                                        ALU.mult, ALU.add).then_inc(copied, 1)
                dve.wait_ge(copied, 4)
    return k


def project(nc, k, a, scratch):
    T = 256
    NT = S // T
    TB = T // P
    assert TB == T // C
    x_rows = a["x"][0, :, :].rearrange("(n p) d -> n p d", p=P)
    with ExitStack() as c:
        sb = lambda n, s, d=f32: c.enter_context(nc.sbuf_tensor(n, s, d))
        ps = lambda n: c.enter_context(nc.psum_tensor(n, [P, 512], f32))
        sem = lambda n: nc.alloc_semaphore(name=n)
        w_rkv = [sb(f"w_{n}", [P, KC, D]) for n in "rkv"]
        w1 = sb("w1", [P, KC, LW]); a1 = sb("a1", [P, KC, LA]); g1 = sb("g1", [P, KC, LG])
        w2 = sb("w2", [LW, D]); a2 = sb("a2", [LA, D]); g2 = sb("g2", [LG, D])
        xb = sb("xb", [P, TB, D])
        xsq = sb("xsq", [P, 2]); rstd = sb("rstd", [P, 2])
        yT = sb("yT", [P, KC, T + 1])
        xx = sb("xx", [P, KC, T])
        mix = [sb(f"mix{i}", [P, KC, T]) for i in range(2)]
        hid_w = sb("hid_w", [LW, T]); hid_a = sb("hid_a", [LA, T]); hid_g = sb("hid_g", [LG, T])
        kT = sb("kT", [P, KC, T])
        rnorm = sb("rnorm", [P, KC, T])
        out_rows = [sb(f"out_rows{i}", [P, TB, ROW]) for i in range(2)]
        sq = sb("sq", [P, T])
        not_first = sb("not_first", [P, T])
        tw = sb("tw", [P, T]); lw = sb("lw", [P, T]); cum = sb("cum", [P, T]); cm = sb("cm", [P, T])
        cx = sb("cx", [P, T]); e_in = sb("e_in", [P, T]); e_out = sb("e_out", [P, T]); e_pre = sb("e_pre", [P, T])
        gS = sb("gS", [P, T]); ta = sb("ta", [P, T]); kk = sb("kk", [P, T]); kn = sb("kn", [P, T]); rS = sb("rS", [P, T])
        zero = sb("zero", [P, KC, 1])

        pX = [ps("pX0"), ps("pX1")]; pP = [ps("pP0"), ps("pP1")]
        pH, pZ, pG, pS = ps("pH"), ps("pZ"), ps("pG"), ps("pS")

        credited = []

        def csem(n):
            credited.append(sem(n))
            return credited[-1]
        x_loaded = csem("x_loaded"); rkv_loaded = [sem(f"{n}_loaded") for n in ("wr", "wk", "wv")]
        lora_loaded = sem("lora_loaded")
        x_squared = csem("x_squared"); x_root = csem("x_root"); mean_ready = csem("mean_ready")
        rstd_ready = csem("rstd_ready"); xn_ready = csem("xn_ready")
        xt_ready = csem("xt_ready"); yt_ready = csem("yt_ready"); carried = csem("carried"); xx_ready = csem("xx_ready")
        mix_ready = csem("mix_ready"); hid_ready = csem("hid_ready"); hid_taken = csem("hid_taken")
        proj_ready = csem("proj_ready"); proj_taken = csem("proj_taken")
        sq_ready = csem("sq_ready"); ss_ready = csem("ss_ready"); ss_taken = csem("ss_taken")
        norm_root = csem("norm_root"); norm_ready = csem("norm_ready"); hid_g_ready = csem("hid_g_ready")
        z_ready = csem("z_ready"); zw_taken = csem("zw_taken"); za_taken = csem("za_taken")
        gate_ready = csem("gate_ready"); gate_taken = csem("gate_taken")
        lw_ready = csem("lw_ready"); cum_ready = csem("cum_ready"); cm_ready = csem("cm_ready"); cx_ready = csem("cx_ready")
        exp_ready = csem("exp_ready"); ends_ready = csem("ends_ready"); mid_ready = csem("mid_ready")
        rate_ready = csem("rate_ready"); kk_ready = csem("kk_ready"); b_ready = csem("b_ready")
        kn_ready = csem("kn_ready"); k_half = csem("k_half"); rk_ready = csem("rk_ready")
        bonus_ready = csem("bonus_ready"); bonus_taken = csem("bonus_taken"); rows_ready = csem("rows_ready")
        rows_stored = [csem(f"rows_stored{i}") for i in range(2)]
        set_up = sem("set_up"); zero_stored = sem("zero_stored")

        with nc.Block() as block:
            @block.gpsimd
            def _(pool):
                for s in credited:
                    pool.sem_inc(s, CREDIT)

        with nc.Block() as block:
            @block.sync
            def _(sp):
                sp.dma_start(xb[:, :, :], x_rows[0:TB, :, :].rearrange("n p d -> p n d")).then_inc(x_loaded, 16)
                for n in (1, 0, 2):
                    sp.dma_start(w_rkv[n][:, :, :], a["rwkv_w_rkv"][0, n, :, :].rearrange("(c p) f -> p c f", p=P))\
                      .then_inc(rkv_loaded[n], 16)
                    if n == 1:
                        for t, s in ((w1, "rwkv_w1"), (a1, "rwkv_a1"), (g1, "rwkv_g1")):
                            sp.dma_start(t[:, :, :], a[s][0, :, :].rearrange("(c p) f -> p c f", p=P))\
                              .then_inc(lora_loaded, 16)
                        for t, s in ((w2, "rwkv_w2"), (a2, "rwkv_a2"), (g2, "rwkv_g2")):
                            sp.dma_start(t[:, :], a[s][0, :, :]).then_inc(lora_loaded, 16)
                def load_x(tt):
                    sp.wait_ge(xt_ready, CREDIT + 2 * TB * tt)
                    sp.dma_start(xb[:, :, :], x_rows[bass.ts(tt, TB), :, :].rearrange("n p d -> p n d"))\
                      .then_inc(x_loaded, 16)

                def store_rows(tt):
                    for p in range(KC):
                        sp.wait_ge(rows_ready, CREDIT + KC * tt + p + 1)
                        sp.dma_start(scratch[bass.ts(tt, TB), p, :, :].rearrange("c q r -> q c r"),
                                     out_rows[p % 2][:, :, :]).then_inc(rows_stored[p % 2], 16)

                load_x(1)
                with sp.Fori(0, NT - 2) as tt:
                    store_rows(tt)
                    load_x(tt + 2)
                store_rows(NT - 2)
                store_rows(NT - 1)

            @block.gpsimd
            def _(pool):
                nc.gpsimd.memset(not_first[:, :], 1.0).then_inc(set_up, 1)
                pool.wait_ge(set_up, 1)
                nc.gpsimd.memset(not_first[:, 0:T:C], 0.0).then_inc(set_up, 1)
                nc.gpsimd.memset(yT[:, :, T:T + 1], 0.0).then_inc(set_up, 1)
                nc.gpsimd.memset(zero[:, :, :], 0.0).then_inc(set_up, 1)
                for i in range(2):
                    pool.wait_ge(rows_stored[i], CREDIT + 16 * NT * KC // 2)
                pool.dma_start(scratch[0, :, :, SM:SM + 1].rearrange("h q r -> q h r"),
                               zero[:, :, :], allow_slow_non_contiguous=True).then_inc(zero_stored, 16)
                pool.wait_ge(zero_stored, 16)

            @block.scalar
            def _(act):
                def square_x(tt):
                    act.wait_ge(x_loaded, CREDIT + 16 * (tt + 1))
                    act.wait_ge(mix_ready, CREDIT + 6 * tt)
                    for b in range(TB):
                        nc.scalar.activation(xx[:, b * (D // T):(b + 1) * (D // T), :], xb[:, b, :], ACT.Square,
                                             accum_out=xsq[:, b:b + 1]).then_inc(x_squared, 1)

                def root_x(tt):
                    act.wait_ge(mean_ready, CREDIT + tt + 1)
                    nc.scalar.activation(rstd[:, :], xsq[:, :], ACT.Sqrt).then_inc(x_root, 1)

                def tile(tt, last):
                    def take_k(p):
                        act.wait_ge(proj_ready, CREDIT + 3 * KC * tt + p + 1)
                        if p == 0:
                            act.wait_ge(k_half, CREDIT + KC * tt)
                        nc.scalar.activation(kT[:, p, :], pP[p % 2][:, 0:T], ACT.Copy).then_inc(proj_taken, 1)
                        act.wait_ge(proj_taken, CREDIT + 3 * KC * tt + p + 1)
                        if p == 0:
                            act.wait_ge(ss_ready, CREDIT + KC * tt)
                        else:
                            act.wait_ge(ss_ready, CREDIT + KC * tt + p)
                        nc.scalar.activation(sq[:, :], kT[:, p, :], ACT.Square,
                                             scale=k.vec[:, K_K + p:K_K + p + 1]).then_inc(sq_ready, 1)

                    for p in range(KC):
                        take_k(p)
                    act.wait_ge(hid_ready, CREDIT + 3 * tt + 1)
                    nc.scalar.activation(hid_w[:, :], pX[0][0:LW, 0:T], ACT.Tanh).then_inc(hid_taken, 1)
                    act.wait_ge(hid_ready, CREDIT + 3 * tt + 2)
                    nc.scalar.activation(hid_a[:, :], pX[1][0:LA, 0:T], ACT.Copy).then_inc(hid_taken, 1)
                    act.wait_ge(hid_ready, CREDIT + 3 * tt + 3)
                    nc.scalar.activation(hid_g[:, :], pH[:, 0:T], ACT.Tanh, scale=0.5).then_inc(hid_taken, 1)
                    act.wait_ge(ss_taken, CREDIT + KC * (tt + 1))
                    nc.scalar.activation(rnorm[:, :, :], rnorm[:, :, :], ACT.Sqrt).then_inc(norm_root, 1)
                    for p in range(KC):
                        rows = out_rows[p % 2]
                        n = KC * tt + p
                        act.wait_ge(z_ready, CREDIT + n + 1)
                        act.wait_ge(lw_ready, CREDIT + n)
                        nc.scalar.activation(tw[:, :], pZ[:, 0:T], ACT.Tanh, bias=k.w0_half[:, p:p + 1],
                                             scale=0.5).then_inc(zw_taken, 1)
                        act.wait_ge(rk_ready, CREDIT + n)
                        nc.scalar.activation(ta[:, :], pZ[:, T:2 * T], ACT.Tanh, bias=k.a0_half[:, p:p + 1],
                                             scale=0.5).then_inc(za_taken, 1)
                        act.wait_ge(proj_ready, CREDIT + 3 * KC * tt + KC + 2 * p + 1)
                        act.wait_ge(bonus_ready, CREDIT + n)
                        nc.scalar.activation(rS[:, :], pP[0][:, 0:T], ACT.Copy).then_inc(proj_taken, 1)
                        act.wait_ge(rows_stored[p % 2], CREDIT + 16 * (KC // 2 * tt + p // 2))
                        act.wait_ge(gate_ready, CREDIT + n + 1)
                        act.wait_ge(rows_ready, CREDIT + n)
                        nc.scalar.activation(gS[:, :], pG[:, 0:T], ACT.Copy).then_inc(gate_taken, 1)
                        act.wait_ge(proj_ready, CREDIT + 3 * KC * tt + KC + 2 * p + 2)
                        nc.scalar.activation(rows[:, :, SV:SV + C], pP[1][:, 0:T].rearrange("q (c t) -> q c t", t=C),
                                             ACT.Copy).then_inc(proj_taken, 1)
                        act.wait_ge(cm_ready, CREDIT + n + 1)
                        nc.scalar.activation(e_in[:, :], cm[:, :], ACT.Exp).then_inc(exp_ready, 1)
                        nc.scalar.activation(e_out[:, :], cm[:, :], ACT.Exp, scale=-1.0).then_inc(exp_ready, 1)
                        act.wait_ge(cx_ready, CREDIT + n + 1)
                        nc.scalar.activation(e_pre[:, :], cx[:, :], ACT.Exp).then_inc(exp_ready, 1)
                        nc.scalar.activation(rows[:, :, SM], cum[:, C // 2 - 1:T:C], ACT.Exp).then_inc(exp_ready, 1)
                        nc.scalar.activation(rows[:, :, SE], cm[:, C - 1:T:C], ACT.Exp).then_inc(exp_ready, 1)
                        if p == 2 and not last:
                            square_x(tt + 1)
                        if p == 3 and not last:
                            root_x(tt + 1)

                square_x(0)
                root_x(0)
                with act.Fori(0, NT - 1) as tt:
                    tile(tt, False)
                tile(NT - 1, True)

            @block.vector
            def _(dve):
                V = nc.vector
                dve.wait_ge(set_up, 4)
                def norm_x(tt):
                    dve.wait_ge(x_squared, CREDIT + TB * (tt + 1))
                    V.tensor_scalar(xsq[:, :], xsq[:, :], 1.0 / D, NORM_EPS, ALU.mult, ALU.add).then_inc(mean_ready, 1)
                    dve.wait_ge(x_root, CREDIT + tt + 1)
                    V.reciprocal(rstd[:, :], rstd[:, :]).then_inc(rstd_ready, 1)
                    dve.wait_ge(rstd_ready, CREDIT + tt + 1)
                    for b in range(TB):
                        V.tensor_scalar(xb[:, b, :], xb[:, b, :], rstd[:, b:b + 1], None, ALU.mult).then_inc(xn_ready, 1)

                def take_y(tt, b):
                    if b == 0:
                        dve.wait_ge(mix_ready, CREDIT + 6 * tt)
                        V.tensor_copy(yT[:, :, 0:1], yT[:, :, T:T + 1]).then_inc(carried, 1)
                        dve.wait_ge(carried, CREDIT + tt + 1)
                    for q in range(2):
                        dve.wait_ge(xt_ready, CREDIT + 2 * TB * tt + 2 * b + q + 1)
                        V.tensor_tensor(yT[:, 4 * q:4 * q + 4, 1 + b * P:1 + (b + 1) * P],
                                        pX[q][:, :].rearrange("p (c t) -> p c t", t=P),
                                        k.vec[:, G0 + 4 * q:G0 + 4 * q + 4].unsqueeze(2).to_broadcast([P, 4, P]),
                                        ALU.mult).then_inc(yt_ready, 1)
                    if b == TB - 1:
                        dve.wait_ge(yt_ready, CREDIT + 2 * TB * (tt + 1))
                        V.tensor_tensor(xx[:, :, :], yT[:, :, 0:T], yT[:, :, 1:T + 1], ALU.subtract).then_inc(xx_ready, 1)

                def blend(tt, n, m):
                    if n < 2:
                        dve.wait_ge(proj_ready, CREDIT + 3 * KC * tt - 1 + n)
                    elif n == 2:
                        dve.wait_ge(proj_ready, CREDIT + 3 * KC * tt + KC)
                    else:
                        dve.wait_ge(hid_ready, CREDIT + 3 * tt + n - 2)
                    dve.wait_ge(xx_ready, CREDIT + tt + 1)
                    for q in range(KC):
                        last = V.scalar_tensor_tensor(
                            out=mix[n % 2][:, q, :], in0=xx[:, q, :],
                            scalar=k.vec[:, MU + m * KC + q:MU + m * KC + q + 1],
                            in1=yT[:, q, 1:T + 1], op0=ALU.mult, op1=ALU.add)
                    last.then_inc(mix_ready, 1)

                def tile(tt, last):
                    blend(tt, 1, 1)
                    dve.wait_ge(kk_ready, CREDIT + KC * tt)
                    for p in range(KC):
                        dve.wait_ge(ss_ready, CREDIT + KC * tt + p + 1)
                        V.tensor_scalar(rnorm[:, p, :], pS[:, 0:T], 1e-24, None, ALU.max).then_inc(ss_taken, 1)
                    blend(tt, 2, 4)
                    blend(tt, 3, 5)
                    blend(tt, 4, 0)
                    dve.wait_ge(hid_taken, CREDIT + 3 * tt + 3)
                    V.tensor_scalar(hid_g[:, :], hid_g[:, :], 0.5, 0.5, ALU.mult, ALU.add).then_inc(hid_g_ready, 1)
                    blend(tt, 5, 3)
                    dve.wait_ge(norm_root, CREDIT + tt + 1)
                    for p in range(KC):
                        rows = out_rows[p % 2]
                        n = KC * tt + p
                        by_chunk = lambda t: t[:, :].rearrange("q (c t) -> q c t", t=C)
                        if p == KC - 1 and not last:
                            blend(tt + 1, 0, 2)
                        dve.wait_ge(zw_taken, CREDIT + n + 1)
                        V.tensor_scalar(lw[:, :], tw[:, :], -0.5 * DECAY, -0.5 * DECAY, ALU.mult, ALU.add)\
                            .then_inc(lw_ready, 1)
                        dve.wait_ge(lw_ready, CREDIT + n + 1)
                        dve.wait_ge(exp_ready, CREDIT + 5 * n)
                        V.tensor_tensor_scan(cum[:, :], not_first[:, :], lw[:, :], 0.0, ALU.mult, ALU.add)\
                            .then_inc(cum_ready, 1)
                        dve.wait_ge(cum_ready, CREDIT + n + 1)
                        V.tensor_tensor(by_chunk(cm), by_chunk(cum),
                                        cum[:, C // 2 - 1:T:C].unsqueeze(2).to_broadcast([P, TB, C]),
                                        ALU.subtract).then_inc(cm_ready, 1)
                        dve.wait_ge(cm_ready, CREDIT + n + 1)
                        V.tensor_tensor(cx[:, :], cm[:, :], lw[:, :], ALU.subtract).then_inc(cx_ready, 1)
                        V.reciprocal(rnorm[:, p, :], rnorm[:, p, :]).then_inc(norm_ready, 1)
                        dve.wait_ge(norm_ready, CREDIT + n + 1)
                        V.scalar_tensor_tensor(out=kk[:, :], in0=kT[:, p, :], scalar=k.vec[:, K_K + p:K_K + p + 1],
                                               in1=rnorm[:, p, :], op0=ALU.mult, op1=ALU.mult).then_inc(kk_ready, 1)
                        dve.wait_ge(za_taken, CREDIT + n + 1)
                        V.tensor_scalar(ta[:, :], ta[:, :], 0.5, 0.5, ALU.mult, ALU.add).then_inc(rate_ready, 1)
                        dve.wait_ge(rate_ready, CREDIT + n + 1)
                        V.tensor_scalar(kn[:, :], ta[:, :], k.vec[:, K_A + p:K_A + p + 1], k.one_less_ka[:, p:p + 1],
                                        ALU.mult, ALU.add).then_inc(kn_ready, 1)
                        dve.wait_ge(kn_ready, CREDIT + 2 * n + 1)
                        V.tensor_tensor(kn[:, :], kn[:, :], kT[:, p, :], ALU.mult).then_inc(kn_ready, 1)
                        dve.wait_ge(kn_ready, CREDIT + 2 * n + 2)
                        dve.wait_ge(rows_stored[p % 2], CREDIT + 16 * (KC // 2 * tt + p // 2))
                        dve.wait_ge(kk_ready, CREDIT + n + 1)
                        V.tensor_tensor(ta[:, :], ta[:, :], kk[:, :], ALU.mult).then_inc(b_ready, 1)
                        dve.wait_ge(exp_ready, CREDIT + 5 * n + 5)
                        V.tensor_tensor(rows[:, :, SK:SK + C], by_chunk(kn), by_chunk(e_out), ALU.mult)\
                            .then_inc(k_half, 1)
                        V.tensor_tensor(rows[:, :, SA:SA + C], by_chunk(kk), by_chunk(e_pre), ALU.mult)
                        dve.wait_ge(b_ready, CREDIT + n + 1)
                        V.tensor_tensor(rows[:, :, SB:SB + C], by_chunk(ta), by_chunk(e_out), ALU.mult)
                        dve.wait_ge(proj_taken, CREDIT + 3 * KC * tt + KC + 2 * p + 2)
                        V.tensor_tensor(rows[:, :, SR:SR + C], by_chunk(rS), by_chunk(e_in), ALU.mult)
                        V.scalar_tensor_tensor(out=rS[:, :], in0=rS[:, :], scalar=k.vec[:, R_K + p:R_K + p + 1],
                                               in1=kn[:, :], op0=ALU.mult, op1=ALU.mult).then_inc(rk_ready, 1)
                        dve.wait_ge(gate_taken, CREDIT + n + 1)
                        V.tensor_scalar(rows[:, :, SG:SG + C], by_chunk(gS), k.vec[:, LN_W + p:LN_W + p + 1], None,
                                        ALU.mult)
                        dve.wait_ge(bonus_ready, CREDIT + n + 1)
                        V.tensor_tensor(by_chunk(cx), pS[:, 0:T].rearrange("q (c t) -> q c t", t=C),
                                        rows[:, :, SV:SV + C], ALU.mult).then_inc(bonus_taken, 1)
                        dve.wait_ge(bonus_taken, CREDIT + n + 1)
                        V.scalar_tensor_tensor(out=rows[:, :, SBV:SBV + C], in0=by_chunk(cx),
                                               scalar=k.vec[:, LN_B + p:LN_B + p + 1], in1=by_chunk(gS),
                                               op0=ALU.add, op1=ALU.mult).then_inc(rows_ready, 1)
                        if p == 3 and not last:
                            norm_x(tt + 1)
                        if p in (4, 6) and not last:
                            take_y(tt + 1, p // 2 - 2)

                norm_x(0)
                take_y(0, 0)
                take_y(0, 1)
                blend(0, 0, 2)
                with dve.Fori(0, NT - 1) as tt:
                    tile(tt, False)
                tile(NT - 1, True)

            @block.tensor
            def _(pe):
                T_ = nc.tensor

                def proj(n, w, p, m, tt):
                    pe.wait_ge(proj_taken, CREDIT + 3 * KC * tt + n - 1)
                    for q in range(KC):
                        mm = T_.matmul(pP[n % 2][:, 0:T], w[:, q, p * P:(p + 1) * P], mix[m % 2][:, q, :],
                                       start=(q == 0), stop=(q == KC - 1))
                    mm.then_inc(proj_ready, 1)

                def transposes(tt, b):
                    pe.wait_ge(hid_taken, CREDIT + 3 * tt)
                    pe.wait_ge(xn_ready, CREDIT + TB * tt + b + 1)
                    for q in range(2):
                        if b >= 1:
                            pe.wait_ge(yt_ready, CREDIT + 2 * TB * tt + 2 * b + q - 1)
                        for j in range(4):
                            mm = T_.transpose(pX[q][:, j * P:(j + 1) * P],
                                              xb[:, b, (4 * q + j) * P:(4 * q + j + 1) * P], k.ident[:, :])
                        mm.then_inc(xt_ready, 1)

                def first_key(tt):
                    pe.wait_ge(mix_ready, CREDIT + 6 * tt + 1)
                    proj(0, w_rkv[1], 0, 0, tt)

                def tile(tt, last):
                    def sums(p):
                        pe.wait_ge(sq_ready, CREDIT + KC * tt + p + 1)
                        pe.wait_ge(ss_taken, CREDIT + KC * tt + p)
                        if p == 0:
                            pe.wait_ge(rows_ready, CREDIT + KC * tt)
                        T_.matmul(pS[:, 0:T], k.ones_head[:, :], sq[:, :], start=True, stop=True).then_inc(ss_ready, 1)

                    for p in range(1, KC):
                        proj(p, w_rkv[1], p, 0, tt)
                        sums(p - 1)
                    pe.wait_ge(lora_loaded, 96)
                    sums(KC - 1)
                    pe.wait_ge(yt_ready, CREDIT + 2 * TB * (tt + 1))
                    for i, (dst, w) in enumerate(((pX[0][0:LW, 0:T], w1), (pX[1][0:LA, 0:T], a1), (pH[:, 0:T], g1))):
                        pe.wait_ge(mix_ready, CREDIT + 6 * tt + 2 + i)
                        for q in range(KC):
                            mm = T_.matmul(dst, w[:, q, :], mix[(1 + i) % 2][:, q, :],
                                           start=(q == 0), stop=(q == KC - 1))
                        mm.then_inc(hid_ready, 1)
                    pe.wait_ge(hid_taken, CREDIT + 3 * tt + 3)
                    pe.wait_ge(hid_g_ready, CREDIT + tt + 1)

                    def bonus(p):
                        pe.wait_ge(rk_ready, CREDIT + KC * tt + p + 1)
                        pe.wait_ge(rows_ready, CREDIT + KC * tt + p)
                        T_.matmul(pS[:, 0:T], k.ones_head[:, :], rS[:, :], start=True, stop=True)\
                            .then_inc(bonus_ready, 1)

                    for p in range(KC):
                        n = KC * tt + p
                        f = slice(p * P, (p + 1) * P)
                        pe.wait_ge(za_taken, CREDIT + n)
                        T_.matmul(pZ[:, 0:T], w2[:, f], hid_w[:, :], start=True, stop=True)
                        T_.matmul(pZ[:, T:2 * T], a2[:, f], hid_a[:, :], start=True, stop=True).then_inc(z_ready, 1)
                        if p == 0:
                            pe.wait_ge(mix_ready, CREDIT + 6 * tt + 5)
                            pe.wait_ge(rkv_loaded[0], 16)
                        proj(KC + 2 * p, w_rkv[0], p, 0, tt)
                        pe.wait_ge(gate_taken, CREDIT + n)
                        T_.matmul(pG[:, 0:T], g2[:, f], hid_g[:, :], start=True, stop=True).then_inc(gate_ready, 1)
                        if p == 0:
                            pe.wait_ge(mix_ready, CREDIT + 6 * tt + 6)
                            pe.wait_ge(rkv_loaded[2], 16)
                        if p >= 1:
                            bonus(p - 1)
                        proj(KC + 2 * p + 1, w_rkv[2], p, 1, tt)
                        if p in (4, 6) and not last:
                            transposes(tt + 1, p // 2 - 2)
                    if not last:
                        first_key(tt + 1)
                    bonus(KC - 1)

                transposes(0, 0)
                transposes(0, 1)
                pe.wait_ge(rkv_loaded[1], 16)
                first_key(0)
                with pe.Fori(0, NT - 1) as tt:
                    tile(tt, False)
                tile(NT - 1, True)




def recur(nc, k, scratch, gated):
    Q = 4
    NBK = 2
    QP = KC // Q
    QH = 2 * QP
    LEVELS = [2, 4, 8, 16, 32, 64]
    MASKED = 4
    NI = NCH
    with ExitStack() as c:
        sb = lambda n, s, d=f32: c.enter_context(nc.sbuf_tensor(n, s, d))
        sem = lambda n: nc.alloc_semaphore(name=n)
        rows = [sb(f"rows{i}", [P, KC, ROW]) for i in range(2)]
        arx = [sb(f"arx{q}", [P, QP, 2, 2 * C]) for q in range(Q)]
        att_b = [sb(f"att_b{q}", [P, QP, 2, 2 * C]) for q in range(Q)]
        att_k = [sb(f"att_k{q}", [P, QP, 2, 2 * C]) for q in range(Q)]
        tok = [sb(f"tok{q}", [P, QP, 3, P]) for q in range(Q)]
        rhs = [sb(f"rhs{q}", [P, QP, 2, 2, HD]) for q in range(Q)]
        rhs16 = [sb(f"rhs16_{q}", [P, QP, 2, 2, HD], bf16) for q in range(Q)]
        res16 = [sb(f"res16_{q}", [P, QP, 2, 2, HD], bf16) for q in range(Q)]
        sol = [sb(f"sol{q}", [P, QP, 2, 2, HD]) for q in range(Q)]
        lT16 = [sb(f"lT16_{q}", [P, QH, C], f16) for q in range(Q)]
        t16 = [sb(f"t16_{q}", [P, QH, C], f16) for q in range(Q)]
        tT16 = [sb(f"tT16_{q}", [P, QH, C], f16) for q in range(Q)]
        u16 = [sb(f"u16_{q}", [P, QH, C], f16) for q in range(Q)]
        w1T = [sb(f"w1T{q}", [P, QP, C]) for q in range(Q)]
        U = [sb(f"U{q}", [P, QP, P]) for q in range(Q)]
        z = [sb(f"z{q}", [P, QP, P]) for q in range(Q)]
        zt = [sb(f"zt{q}", [P, QP, P]) for q in range(Q)]
        scale = sb("scale", [P, KC, 1])
        eps = sb("eps", [P, 1])
        y = [sb(f"y{q}", [P, QP, C]) for q in range(Q)]
        yc = [sb(f"yc{q}", [P, QP, C]) for q in range(Q)]
        yn = [sb(f"yn{q}", [P, QP, C]) for q in range(Q)]
        yg = [sb(f"yg{q}", [P, QP, C]) for q in range(Q)]
        causal = sb("causal", [P, 2 * C])
        lower = sb("lower", [P, MASKED, C])
        upper = sb("upper", [P, 1 + MASKED, C])
        start = sb("start", [P, C])
        centre = sb("centre", [P, P])
        ident16 = sb("ident16", [P, P], f16)

        bank = [[c.enter_context(nc.psum_tensor(f"bank{q}_{j}", [P, 512], f32)) for j in range(NBK)] for q in range(Q)]

        fills = [("tok0", "act"), ("tok1", "act"), ("centred", "act"), ("b0", "dve"), ("k0", "dve"),
                 ("var", "act"), ("b1", "dve"), ("k1", "dve"),
                 ("mv", "act"), ("t", "act")]
        for m in LEVELS:
            fills += [(f"u{m}", "act")] + ([(f"w{m}", "dve")] if m != LEVELS[-1] else []) + [(f"wT{m}", "dve")]
        fills += [("z0", "act"), ("r0", "dve"), ("d0", "dve"), ("r1", "dve"), ("d1", "dve"),
                  ("w1T", "act"), ("U", "dve"), ("zn", "dve"), ("Y", "act")]
        names = [f for f, _ in fills]
        NF = len(fills)
        assert NF % NBK == 0
        per = {e: sum(t == e for _, t in fills) for e in ("act", "dve")}
        place = lambda name: names.index(name)
        bank_of = lambda q, name: bank[q][place(name) % NBK]

        credited = []

        def csem(n):
            credited.append(sem(n))
            return credited[-1]

        ends = {"centred": 1, "var": 2}

        def nth(name, i=0):
            n = place(name)
            after = type(i) is int and i == NI
            return fills[n][1], ends[name] if after else sum(t == fills[n][1] for _, t in fills[:n + 1])

        filled = [csem(f"filled{q}") for q in range(Q)]
        took = {e: [csem(f"{e}_took{q}") for q in range(Q)] for e in ("act", "dve")}

        def wait_taken(eng, q, i, name):
            e, n = nth(name, i)
            eng.wait_ge(took[e][q], CREDIT + per[e] * i + n)

        def wait_filled(eng, q, i, name):
            n = ends[name] if type(i) is int and i == NI else place(name) + 1
            eng.wait_ge(filled[q], CREDIT + NF * i + n)

        def wait_bank(eng, q, i, name, *needs):
            n = place(name)
            for e in ("act", "dve"):
                counts = [nth(f)[1] for f in needs if nth(f)[0] == e]
                last, its = fills[n - NBK]
                if its == e:
                    counts.append(nth(last)[1] - (per[e] if n < NBK else 0))
                if counts:
                    eng.wait_ge(took[e][q], CREDIT + per[e] * i + max(counts))

        rows_loaded = [csem(f"rowsB_loaded{u}") for u in range(2)]
        expanded = csem("expanded"); lT_ready = [csem(f"lT_ready{q}") for q in range(Q)]
        tT_ready = [csem(f"tT_ready{q}") for q in range(Q)]; rhs16_ready = [csem(f"rhs16_ready{q}") for q in range(Q)]
        scale_ready = csem("scale_ready"); z_scaled = [csem(f"z_scaled{q}") for q in range(Q)]
        masks = sem("masks")
        held = sem("held")
        yn_ready = csem("yn_ready"); ya_ready = csem("ya_ready"); gated_ready = csem("gated_ready"); yg_ready = csem("yg_ready")
        yg_stored = csem("yg_stored")

        flat = lambda t: t[:, :, :, :, :].rearrange("p g a h d -> p (g a h d)")
        set_up = {}

        with nc.Block() as block:
            @block.gpsimd
            def _(pool):
                for s in credited:
                    pool.sem_inc(s, CREDIT)

        with nc.Block() as block:
            @block.gpsimd
            def _(pool):
                G = nc.gpsimd
                n = 0
                for t in (causal, lower, upper):
                    G.memset(t[:], 1.0).then_inc(masks, 1); n += 1
                for t in att_b + att_k + arx + zt + z + y + [scale]:
                    G.memset(t[:], 0.0).then_inc(masks, 1); n += 1
                G.memset(eps[:, :], GN_EPS).then_inc(masks, 1); n += 1
                G.memset(rows[1][:, :, SG:ROW], 0.0).then_inc(masks, 1); n += 1
                G.tensor_copy(ident16[:, :], k.ident[:, :]).then_inc(masks, 1); n += 1
                pool.wait_ge(masks, n)
                for j, op in ((0, ALU.is_gt), (1, ALU.is_ge)):
                    v = causal[:, j * C:(j + 1) * C]
                    G.affine_select(out=v, in_=v, pattern=[[1, C]], compare_op=op, fill=0.0, base=0,
                                    channel_multiplier=-1).then_inc(masks, 1); n += 1
                for q in range(Q):
                    for p in range(QP):
                        for h in range(2):
                            G.tensor_copy(att_b[q][:, p, h, 0:C], k.ident[:, :]).then_inc(masks, 1); n += 1
                for table, part, sizes in ((lower, 0, LEVELS[:MASKED]), (upper, 1, [1] + LEVELS[:MASKED])):
                    for j, m in enumerate(sizes):
                        v = table[:, j, :].rearrange("p (b e x) -> p b e x", e=2, x=m)
                        G.memset(v[:, :, 1 - part, :], 0.0).then_inc(masks, 1); n += 1
                        v = v[:, :, part, :]
                        row0 = m * (1 - part)
                        G.affine_select(out=v, in_=v, pattern=[[-2 * m, C // (2 * m)], [0, m]], compare_op=ALU.is_ge,
                                        fill=0.0, base=-row0, channel_multiplier=1).then_inc(masks, 1); n += 1
                        pool.wait_ge(masks, n)
                        G.affine_select(out=v, in_=v, pattern=[[2 * m, C // (2 * m)], [0, m]], compare_op=ALU.is_ge,
                                        fill=0.0, base=row0 + m - 1, channel_multiplier=-1).then_inc(masks, 1); n += 1
                pool.wait_ge(masks, n)
                G.tensor_tensor(start[:, :], k.ident[:, :], upper[:, 0, :], ALU.subtract).then_inc(masks, 1); n += 1
                pool.wait_ge(masks, n)
                set_up["n"] = n

                def finish(i, slot):
                    for q in range(Q):
                        pool.wait_ge(yn_ready, CREDIT + Q * i + q + 1)
                        pairs = slice(q * QP, (q + 1) * QP)
                        if q == 0:
                            pool.wait_ge(yg_stored, CREDIT + 16 * Q * i)
                        G.tensor_tensor(yg[q][:, :, :], yc[q][:, :, :], yn[q][:, :, :], ALU.mult).then_inc(ya_ready, 1)
                        pool.wait_ge(ya_ready, CREDIT + Q * i + q + 1)
                        G.tensor_tensor(yg[q][:, :, :], yg[q][:, :, :], rows[slot][:, pairs, SG:SG + C], ALU.mult)\
                         .then_inc(gated_ready, 1)
                        pool.wait_ge(gated_ready, CREDIT + Q * i + q + 1)
                        G.tensor_tensor(yg[q][:, :, :], yg[q][:, :, :], rows[slot][:, pairs, SBV:SBV + C], ALU.add)\
                         .then_inc(yg_ready, 1)

                with pool.Fori(0, NI // 2) as j:
                    for u in range(2):
                        i = 2 * j + u
                        pool.wait_ge(rows_loaded[u], CREDIT + 16 * (j + 1))
                        wait_filled(pool, Q - 1, i - 1, "k1")
                        pool.sem_inc(held, 1)
                        for q in range(Q):
                            for p in range(QP):
                                for h in range(2):
                                    part = slice(h * HD, (h + 1) * HD)
                                    G.tensor_copy(arx[q][part, p, h, :], rows[u][part, q * QP + p, SA:SB])\
                                        .then_inc(expanded, 1)
                        pool.wait_ge(expanded, CREDIT + 2 * KC * (i + 1))
                        for q in range(Q):
                            wait_taken(pool, q, i, "b1")
                            G.tensor_tensor(tT16[q][:, :, :].rearrange("p (a h) t -> p (a h) t", h=2),
                                            att_b[q][:, :, :, 0:C].rearrange("p a h t -> p (a h) t"),
                                            start[:, :].unsqueeze(1).to_broadcast([P, QH, C]), ALU.mult)\
                             .then_inc(tT_ready[q], 1)
                        for q in range(Q):
                            wait_taken(pool, q, i, "mv")
                            pool.sem_inc(held, 1)
                            G.tensor_copy(flat(rhs16[q]), flat(rhs[q]))\
                             .then_inc(rhs16_ready[q], 1)
                        finish(i, 1 - u)
                finish(NI, 1)

            @block.sync
            def _(sp):
                def store(i):
                    for q in range(Q):
                        sp.wait_ge(yg_ready, CREDIT + Q * i + q + 1)
                        sp.dma_start(gated[bass.ds(i, 1), q * QP:(q + 1) * QP, :, :].rearrange("o p q r -> q (o p) r"),
                                     yg[q][:, :, :]).then_inc(yg_stored, 16)

                sp.wait_ge(masks, set_up["n"])
                with sp.Fori(0, NI // 2) as j:
                    for u in range(2):
                        i = 2 * j + u
                        sp.wait_ge(yg_ready, CREDIT + Q * i)
                        sp.dma_start(rows[u][:, :, :], scratch[bass.ds(i, 1), :, :, :].rearrange("o p q r -> q (o p) r"))\
                          .then_inc(rows_loaded[u], 16)
                        store(i)
                store(NI)
                sp.wait_ge(yg_stored, CREDIT + 16 * Q * (NI + 1))

            @block.scalar
            def _(act):
                def copy(q, i, name, out, in_, scale=1.0, last=True):
                    wait_filled(act, q, i, name)
                    ins = nc.scalar.activation(out, in_, ACT.Copy, scale=scale)
                    if last:
                        ins.then_inc(took["act"][q], 1)

                def center(i):
                    for q in range(Q):
                        act.wait_ge(ya_ready, CREDIT + Q * (i - 1) + q + 1)
                        wait_filled(act, q, i, "centred")
                        got = bank_of(q, "centred")[:, 0:QP * C].rearrange("p (a t) -> p a t", t=C)
                        nc.scalar.activation(yc[q][:, :, :], got, ACT.Copy)
                        nc.scalar.activation(yn[q][:, :, :], got, ACT.Square).then_inc(took["act"][q], 1)

                def deviation(i):
                    for q in range(Q):
                        wait_filled(act, q, i, "var")
                        nc.scalar.activation(yn[q][:, :, :], bank_of(q, "var")[:, 0:QP * C]
                                             .rearrange("p (a t) -> p a t", t=C), ACT.Sqrt,
                                             bias=eps[:, :], scale=1.0 / HD).then_inc(took["act"][q], 1)

                act.wait_ge(masks, set_up["n"])
                with act.Fori(0, NI // 2) as j:
                    for u in range(2):
                        i = 2 * j + u
                        for name, p in (("tok0", 0), ("tok1", 1)):
                            for q in range(Q):
                                b = bank_of(q, name)
                                copy(q, i, name, rhs[q][:, p, 0, :, :],
                                     b[:, 0:P].rearrange("p (h d) -> p h d", h=2), last=False)
                                copy(q, i, name, tok[q][:, p, :, :], b[:, P:4 * P].rearrange("p (a d) -> p a d", a=3))
                        center(i)
                        deviation(i)
                        for q in range(Q):
                            b = bank_of(q, "mv")[:, :].rearrange("p (a h e d) -> p a h e d", a=QP, h=2, e=2)
                            for h in range(2):
                                copy(q, i, "mv", rhs[q][:, :, 1, h, :], b[:, :, h, h, :], last=(h == 1))
                        for q in range(Q):
                            wait_taken(act, q, i, "b1")
                            nc.scalar.activation(lT16[q][:, :, :].rearrange("p (a h) t -> p a h t", h=2),
                                                 att_b[q][:, :, :, 0:C], ACT.Copy).then_inc(lT_ready[q], 1)
                        for q in range(Q):
                            copy(q, i, "t", t16[q][:, :, :],
                                 bank_of(q, "t")[:, 0:256].bitcast(f16).rearrange("p (h t) -> p h t", t=C))
                        for m in LEVELS:
                            for q in range(Q):
                                copy(q, i, f"u{m}", u16[q][:, :, :],
                                     bank_of(q, f"u{m}")[:, :].rearrange("p (h t) -> p h t", t=C), scale=-1.0)
                        for q in range(Q):
                            copy(q, i, "z0", flat(sol[q]), bank_of(q, "z0")[:, :])
                        for q in range(Q):
                            copy(q, i, "w1T", w1T[q][:, :, :],
                                 bank_of(q, "w1T")[:, 0:QP * C].rearrange("p (a t) -> p a t", t=C))
                        for q in range(Q):
                            copy(q, i, "Y", y[q][:, :, :],
                                 bank_of(q, "Y")[:, 0:QP * C].rearrange("p (a t) -> p a t", t=C))
                center(NI)
                deviation(NI)

            @block.vector
            def _(dve):
                V = nc.vector
                by_head = lambda b: b[:, :].rearrange("p (h t) -> p h t", t=C)

                def invert(i):
                    for q in range(Q):
                        wait_taken(dve, q, i, "var")
                        V.reciprocal(yn[q][:, :, :], yn[q][:, :, :]).then_inc(yn_ready, 1)

                def grow(q, m, table, mask, b, part):
                    dve.sem_inc(held, 1)
                    if m < 32:
                        V.copy_predicated(table[:, :, :], mask.bitcast(u32).unsqueeze(1).to_broadcast([P, QH, C]),
                                          by_head(b)).then_inc(took["dve"][q], 1)
                        return
                    for at in range(0, C, 2 * m):
                        down, across = slice(at + m * (1 - part), at + m * (2 - part)), slice(at + m * part, at + m * (1 + part))
                        last = V.tensor_scalar(table[down, :, across], by_head(b)[down, :, across], 1.0, None, ALU.mult)
                    last.then_inc(took["dve"][q], 1)

                dve.wait_ge(masks, set_up["n"])
                V.scalar_tensor_tensor(out=centre[:, :], in0=k.ones_head[:, :], scalar=-1.0 / HD, in1=k.ident[:, :],
                                       op0=ALU.mult, op1=ALU.add).then_inc(masks, 1)
                with dve.Fori(0, NI // 2) as j:
                    for u in range(2):
                        i = 2 * j + u
                        for name, dst, p in (("b0", att_b, 0), ("k0", att_k, 0), ("b1", att_b, 1), ("k1", att_k, 1)):
                            for q in range(Q):
                                wait_filled(dve, q, i, name)
                                if name == "b0":
                                    dve.wait_ge(lT_ready[q], CREDIT + i)
                                dve.sem_inc(held, 1)
                                V.copy_predicated(dst[q][:, p, :, :],
                                                  causal[:, :].bitcast(u32).unsqueeze(1).to_broadcast([P, 2, 2 * C]),
                                                  bank_of(q, name)[:, :].rearrange("p (h t) -> p h t", h=2))\
                                 .then_inc(took["dve"][q], 1)
                        invert(i)
                        for l, m in enumerate(LEVELS):
                            if m != LEVELS[-1]:
                                for q in range(Q):
                                    wait_filled(dve, q, i, f"w{m}")
                                    wait_taken(dve, q, i, "t" if l == 0 else f"w{m // 2}")
                                    grow(q, m, t16[q], lower[:, min(l, MASKED - 1), :], bank_of(q, f"w{m}"), 0)
                            for q in range(Q):
                                wait_filled(dve, q, i, f"wT{m}")
                                if l == 0:
                                    dve.wait_ge(tT_ready[q], CREDIT + i + 1)
                                else:
                                    wait_taken(dve, q, i, f"wT{m // 2}")
                                grow(q, m, tT16[q], upper[:, 1 + min(l, MASKED - 1), :], bank_of(q, f"wT{m}"), 1)
                        for n in range(2):
                            for q in range(Q):
                                wait_filled(dve, q, i, f"r{n}")
                                V.tensor_tensor(flat(res16[q]), flat(rhs[q]), bank_of(q, f"r{n}")[:, :], ALU.subtract)\
                                 .then_inc(took["dve"][q], 1)
                            for q in range(Q):
                                wait_filled(dve, q, i, f"d{n}")
                                if n == 0:
                                    wait_taken(dve, q, i, "z0")
                                else:
                                    wait_taken(dve, q, i, "d0")
                                V.tensor_tensor(flat(sol[q]), flat(sol[q]), bank_of(q, f"d{n}")[:, :], ALU.add)\
                                 .then_inc(took["dve"][q], 1)
                        dve.wait_ge(rows_loaded[u], CREDIT + 16 * (j + 1))
                        dve.wait_ge(scale_ready, CREDIT + 2 * i)
                        V.tensor_tensor(scale[:, :, :], scale[:, :, :], rows[u][:, :, SM:SM + 1], ALU.mult)\
                         .then_inc(scale_ready, 1)
                        dve.wait_ge(scale_ready, CREDIT + 2 * i + 1)
                        for q in range(Q):
                            wait_taken(dve, q, i - 1, "zn")
                            wait_filled(dve, q, i, "d1")
                            for p in range(QP):
                                V.scalar_tensor_tensor(
                                    out=z[q][:, p, :], in0=zt[q][:, p, :], scalar=scale[:, q * QP + p, :],
                                    in1=k.ones_head[:, :], op0=ALU.mult, op1=ALU.mult).then_inc(z_scaled[q], 1)
                        for q in range(Q):
                            dve.wait_ge(z_scaled[q], CREDIT + QP * (i + 1))
                        V.tensor_copy(scale[:, :, :], rows[u][:, :, SE:SE + 1]).then_inc(scale_ready, 1)
                        for q in range(Q):
                            wait_filled(dve, q, i, "U")
                            wait_taken(dve, q, i, "d1")
                            V.scalar_tensor_tensor(
                                out=U[q][:, :, :], in0=bank_of(q, "U")[:, 0:QP * P].rearrange("p (g d) -> p g d", g=QP),
                                scalar=-1.0, in1=sol[q][:, :, 1, :, :].rearrange("p g h d -> p g (h d)"), op0=ALU.mult, op1=ALU.subtract).then_inc(took["dve"][q], 1)
                        for q in range(Q):
                            wait_filled(dve, q, i, "zn")
                            V.tensor_tensor(zt[q][:, :, :], z[q][:, :, :],
                                            bank_of(q, "zn")[:, 0:QP * P].rearrange("p (a d) -> p a d", a=QP),
                                            ALU.add).then_inc(took["dve"][q], 1)
                invert(NI)

            @block.tensor
            def _(pe):
                T = nc.tensor
                pe.wait_ge(masks, set_up["n"] + 1)

                def take_means(i):
                    for q in range(Q):
                        if type(i) is int and i == NI:
                            for e in ("act", "dve"):
                                pe.wait_ge(took[e][q], CREDIT + per[e] * i)
                        else:
                            wait_bank(pe, q, i, "centred")
                            wait_taken(pe, q, i - 1, "Y")
                        T.matmul(bank_of(q, "centred")[:, 0:QP * C], centre[:, :],
                                 y[q][:, :, :].rearrange("p a t -> p (a t)"), start=True, stop=True)\
                         .then_inc(filled[q], 1)

                def sum_var(i):
                    for q in range(Q):
                        if not (type(i) is int and i == NI):
                            wait_bank(pe, q, i, "var")
                        wait_taken(pe, q, i, "centred")
                        T.matmul(bank_of(q, "var")[:, 0:QP * C], k.ones_head[:, :],
                                 yn[q][:, :, :].rearrange("p a t -> p (a t)"), start=True, stop=True)\
                         .then_inc(filled[q], 1)

                with pe.Fori(0, NI // 2) as j:
                    for u in range(2):
                        i = 2 * j + u
                        pe.wait_ge(rows_loaded[u], CREDIT + 16 * (j + 1))
                        for p in range(QP):
                            for q in range(Q):
                                wait_bank(pe, q, i, f"tok{p}")
                                b = bank_of(q, f"tok{p}")
                                for n, at in enumerate((SA, SB, SK, SV)):
                                    mm = T.transpose(b[:, n * P:(n + 1) * P], rows[u][:, q * QP + p, at:at + C],
                                                     k.ident[:, :])
                                mm.then_inc(filled[q], 1)
                        take_means(i)
                        for p in range(QP):
                            for q in range(Q):
                                pe.wait_ge(expanded, CREDIT + 2 * KC * i + 2 * (q * QP + p) + 2)
                                for name, at in ((f"b{p}", SB), (f"k{p}", SK)):
                                    wait_bank(pe, q, i, name)
                                    T.matmul(bank_of(q, name)[:, :], rows[u][:, q * QP + p, at:at + C],
                                             arx[q][:, p, :, :].rearrange("p h t -> p (h t)"),
                                             start=True, stop=True).then_inc(filled[q], 1)
                            if p == 0:
                                sum_var(i)
                        for q in range(Q):
                            wait_bank(pe, q, i, "mv", "k1", "tok1")
                            for h in range(QH):
                                mm = T.matmul(bank_of(q, "mv")[:, h * P:(h + 1) * P], att_k[q][:, h // 2, h % 2, 0:C],
                                              tok[q][:, h // 2, 2, :], start=True, stop=True)
                            mm.then_inc(filled[q], 1)
                        for q in range(Q):
                            wait_bank(pe, q, i, "t")
                            pe.wait_ge(tT_ready[q], CREDIT + i + 1)
                            for h in range(QH):
                                mm = T.transpose(bank_of(q, "t")[:, 64 * h:64 * (h + 1)].bitcast(f16), tT16[q][:, h, :],
                                                 ident16[:, :])
                            mm.then_inc(filled[q], 1)
                        for l, m in enumerate(LEVELS):
                            for q in range(Q):
                                wait_bank(pe, q, i, f"u{m}", "t" if l == 0 else f"w{m // 2}")
                                if l == 0:
                                    pe.wait_ge(lT_ready[q], CREDIT + i + 1)
                                for h in range(QH):
                                    mm = T.matmul(bank_of(q, f"u{m}")[:, h * C:(h + 1) * C], lT16[q][:, h, :],
                                                  t16[q][:, h, :], start=True, stop=True)
                                mm.then_inc(filled[q], 1)
                            needs = [f"u{m}"] + ([f"wT{m // 2}"] if l > 0 else [])
                            for q in range(Q):
                                if m != LEVELS[-1]:
                                    wait_bank(pe, q, i, f"w{m}", *needs)
                                    for h in range(QH):
                                        mm = T.matmul(bank_of(q, f"w{m}")[:, h * C:(h + 1) * C], tT16[q][:, h, :],
                                                      u16[q][:, h, :], start=True, stop=True)
                                    mm.then_inc(filled[q], 1)
                            for q in range(Q):
                                wait_bank(pe, q, i, f"wT{m}", *needs)
                                for h in range(QH):
                                    mm = T.matmul(bank_of(q, f"wT{m}")[:, h * C:(h + 1) * C], u16[q][:, h, :],
                                                  tT16[q][:, h, :], start=True, stop=True)
                                mm.then_inc(filled[q], 1)


                        def solve(name, lhs, right):
                            for h in range(QH):
                                out = bank_of(q, name)[:, :].rearrange("p (g a h d) -> p g a h d", g=QP, a=2, h=2)
                                mm = T.matmul(out[:, h // 2, :, h % 2, :], lhs(h), right[:, h // 2, :, h % 2, :],
                                              start=True, stop=True)
                            mm.then_inc(filled[q], 1)

                        for q in range(Q):
                            wait_bank(pe, q, i, "z0", f"wT{LEVELS[-1]}")
                            pe.wait_ge(rhs16_ready[q], CREDIT + i + 1)
                            solve("z0", lambda h: tT16[q][:, h, :], rhs16[q])
                        for n in range(2):
                            for q in range(Q):
                                wait_bank(pe, q, i, f"r{n}", "z0" if n == 0 else "d0")
                                solve(f"r{n}", lambda h: att_b[q][:, h // 2, h % 2, 0:C],
                                      sol[q])
                            for q in range(Q):
                                wait_bank(pe, q, i, f"d{n}", f"r{n}")
                                solve(f"d{n}", lambda h: tT16[q][:, h, :], res16[q])
                        for q in range(Q):
                            wait_bank(pe, q, i, "w1T", "d1")
                            for p in range(QP):
                                mm = T.transpose(bank_of(q, "w1T")[:, p * C:(p + 1) * C], sol[q][:, p, 0, :, :].rearrange("p h d -> p (h d)"),
                                                 k.ident[:, :])
                            mm.then_inc(filled[q], 1)
                        for q in range(Q):
                            wait_bank(pe, q, i, "U", "w1T")
                            pe.wait_ge(z_scaled[q], CREDIT + QP * (i + 1))
                            for p in range(QP):
                                mm = T.matmul(bank_of(q, "U")[:, p * P:(p + 1) * P], w1T[q][:, p, :], z[q][:, p, :],
                                              start=True, stop=True)
                            mm.then_inc(filled[q], 1)
                        for q in range(Q):
                            wait_bank(pe, q, i, "zn", "U")
                            for p in range(QP):
                                out = bank_of(q, "zn")[:, p * P:(p + 1) * P]
                                T.matmul(out, tok[q][:, p, 0, :], U[q][:, p, :], start=True, stop=False)
                                mm = T.matmul(out, tok[q][:, p, 1, :], tok[q][:, p, 2, :], start=False, stop=True)
                            mm.then_inc(filled[q], 1)
                        for q in range(Q):
                            wait_bank(pe, q, i, "Y")
                            b = bank_of(q, "Y")
                            for p in range(QP):
                                cols = slice(p * C, (p + 1) * C)
                                T.matmul(b[:, cols], z[q][:, p, :], rows[u][:, q * QP + p, SR:SR + C],
                                         start=True, stop=False, skip_group_check=True)
                                for of, att, last in (("U", att_b, False), ("V", att_k, True)):
                                    for h in range(2):
                                        part = slice(h * HD, (h + 1) * HD)
                                        left = U[q][:, p, part] if of == "U" else tok[q][:, p, 2, part]
                                        mm = T.matmul(b[part, cols], left, att[q][:, p, h, C:2 * C],
                                                      start=False, stop=last, skip_group_check=True)
                            mm.then_inc(filled[q], 1)
                take_means(NI)
                sum_var(NI)


def attend_out(nc, k, a, gated, h_dram, y2_dram):
    NB = S // P
    HALVES = D // 512
    HI, LO = 0, 1
    PASSES = ((HI, HI), (HI, LO), (LO, HI))
    x_rows = a["x"][0, :, :].rearrange("(n p) d -> n p d", p=P)
    w_dram = a["rwkv_w_o"][0, :, :].rearrange("(c p) f -> p c f", p=P)
    with ExitStack() as c:
        sb = lambda n, s, d=f32: c.enter_context(nc.sbuf_tensor(n, s, d))
        ps = lambda n: c.enter_context(nc.psum_tensor(n, [P, 512], f32))
        sem = lambda n: nc.alloc_semaphore(name=n)
        w_raw = sb("wo_raw", [P, KC, D])
        w = sb("wo_split", [P, 2, KC, D], f32r)
        post_g = sb("post_g", [P, D])
        g_raw = [sb(f"g_raw{s}", [P, KC, P]) for s in range(2)]
        g = [sb(f"g_split{s}", [P, 2, KC, P], f32r) for s in range(2)]
        xr = [sb(f"xr{s}", [P, D]) for s in range(2)]
        squares = sb("squares", [P, D])
        ss = [sb(f"ss{s}", [P, 2]) for s in range(2)]
        rs = [sb(f"rs{s}", [P, 1]) for s in range(2)]
        ss2 = [sb(f"ss2_{s}", [P, 1]) for s in range(2)]
        rs2 = [sb(f"rs2_{s}", [P, 1]) for s in range(2)]
        h = [sb(f"h{s}", [P, D]) for s in range(2)]
        hn = [sb(f"hn{s}", [P, D]) for s in range(2)]
        y2_raw = sb("y2_raw", [P, KC, P])
        y2 = [sb(f"y2_{s}", [P, 2, KC, P], f32r) for s in range(2)]
        eps = sb("eps_c", [P, 1])
        pO = [[ps(f"pO{s}_{j}") for j in range(HALVES)] for s in range(2)]
        pT = [[ps(f"pT{s}_{j}") for j in range(2)] for s in range(2)]

        credited = []

        def csem(n):
            credited.append(sem(n))
            return credited[-1]
        g_loaded = [csem(f"g_loaded{s}") for s in range(2)]; xr_loaded = [csem(f"xr_loaded{s}") for s in range(2)]
        g_hi = csem("g_hi"); g_lo = csem("g_lo")
        o_made = csem("o_ready"); squared = csem("squared"); mean1 = csem("mean1"); root1 = csem("root1")
        rs_ready = csem("rs_ready"); scaled = csem("scaled"); h_ready = csem("h_ready"); squared2 = csem("squared2")
        root2 = csem("root2"); rs2_ready = csem("rs2_ready"); hn_ready = csem("hn_ready")
        t_made = csem("t_ready"); y2_made = csem("y2_made"); y2_hi = csem("y2_hi"); y2_lo = csem("y2_lo")
        h_stored = [csem(f"h_stored{s}") for s in range(2)]; y2_stored = [csem(f"y2_stored{s}") for s in range(2)]
        w_loaded = [sem(f"wo_loaded{q}") for q in range(KC)]; w_hi = sem("wo_hi"); w_lo = sem("wo_lo"); eps_set = sem("eps_set")
        post_loaded = sem("post_g_loaded")

        with nc.Block() as block:
            @block.gpsimd
            def _(pool):
                for s in credited:
                    pool.sem_inc(s, CREDIT)

        def steps(eng, step):
            step(0, 0, first=True)
            with eng.Fori(0, NB // 2 - 1) as j:
                step(2 * j + 1, 1)
                step(2 * j + 2, 0)
            step(NB - 1, 1, last=True)

        with nc.Block() as block:
            @block.sync
            def _(sp):
                def load_g(n, s):
                    sp.dma_start(g_raw[s][:, :, :], gated[bass.ds(n + 1, 1), :, :, :].rearrange("o p q r -> q (o p) r"))\
                      .then_inc(g_loaded[s], 16)

                def load_x(n, s):
                    sp.dma_start(xr[s][:, :], x_rows[bass.ds(n, 1), :, :].rearrange("o p d -> p (o d)"))\
                      .then_inc(xr_loaded[s], 16)

                def step(n, s, first=False, load=True):
                    if load:
                        sp.wait_ge(g_lo, CREDIT + n + 1)
                        load_g(n + 2, s)
                    if not first:
                        sp.wait_ge(y2_lo, CREDIT + n)
                        sp.dma_start(y2_dram[:, :, :, bass.ds((n - 1) * P, P)], y2[1 - s][:, :, :, :].bitcast(f32))\
                          .then_inc(y2_stored[1 - s], 16)
                    sp.wait_ge(h_ready, CREDIT + 2 * (n + 1))
                    sp.dma_start(h_dram[bass.ds(n, 1), :, :].rearrange("o p d -> p (o d)"), h[s][:, :])\
                      .then_inc(h_stored[s], 16)
                    if load:
                        load_x(n + 2, s)

                load_g(0, 0)
                for q in range(KC):
                    sp.dma_start(w_raw[:, q, :], w_dram[:, q, :]).then_inc(w_loaded[q], 16)
                load_x(0, 0)
                sp.dma_start(post_g[:, :], a["norm_g"][0, 1:2, :].to_broadcast([P, D])).then_inc(post_loaded, 16)
                load_g(1, 1)
                load_x(1, 1)
                step(0, 0, first=True)
                with sp.Fori(0, NB // 2 - 2) as j:
                    step(2 * j + 1, 1)
                    step(2 * j + 2, 0)
                step(NB - 3, 1)
                step(NB - 2, 0, load=False)
                step(NB - 1, 1, load=False)
                sp.wait_ge(y2_lo, CREDIT + NB)
                sp.dma_start(y2_dram[:, :, :, (NB - 1) * P:NB * P], y2[1][:, :, :, :].bitcast(f32)).then_inc(y2_stored[1], 16)
                for s in range(2):
                    sp.wait_ge(h_stored[s], CREDIT + 16 * (NB // 2))
                    sp.wait_ge(y2_stored[s], CREDIT + 16 * (NB // 2))

            @block.gpsimd
            def _(pool):
                nc.gpsimd.memset(eps[:, :], NORM_EPS).then_inc(eps_set, 1)
                with pool.Fori(0, NB // 2) as j:
                    for s in range(2):
                        pool.wait_ge(y2_hi, CREDIT + 2 * j + s + 1)
                        nc.gpsimd.tensor_tensor(y2[s][:, LO, :, :], y2_raw[:, :, :], y2[s][:, HI, :, :].bitcast(f32),
                                                ALU.subtract).then_inc(y2_lo, 1)

            @block.tensor
            def _(pe):
                def transposes(n, s):
                    pe.wait_ge(hn_ready, CREDIT + n + 1)
                    pe.wait_ge(y2_made, CREDIT + 2 * (n - 1))
                    for i in range(2):
                        for q in range(4):
                            mm = nc.tensor.transpose(pT[s][i][:, q * P:(q + 1) * P],
                                                     hn[s][:, (4 * i + q) * P:(4 * i + q + 1) * P], k.ident[:, :])
                        mm.then_inc(t_made, 1)

                def step(n, s, first=False, last=False):
                    pe.wait_ge(g_lo, CREDIT + n + 1)
                    pe.wait_ge(scaled, CREDIT + 2 * (n - 1))
                    if first:
                        for q in range(KC):
                            pe.wait_ge(w_lo, q + 1)
                            for half in range(HALVES):
                                for j, (x, y) in enumerate(PASSES):
                                    mm = nc.tensor.matmul(pO[s][half][:, :], g[s][:, x, q, :],
                                                          w[:, y, q, half * 512:(half + 1) * 512],
                                                          start=(q == 0 and j == 0), stop=(q == KC - 1 and j == 2))
                                if q == KC - 1:
                                    mm.then_inc(o_made, 1)
                    else:
                        for half in range(HALVES):
                            for q in range(KC):
                                for j, (x, y) in enumerate(PASSES):
                                    mm = nc.tensor.matmul(pO[s][half][:, :], g[s][:, x, q, :],
                                                          w[:, y, q, half * 512:(half + 1) * 512],
                                                          start=(q == 0 and j == 0), stop=(q == KC - 1 and j == 2))
                            mm.then_inc(o_made, 1)
                        transposes(n - 1, 1 - s)

                steps(pe, step)
                transposes(NB - 1, 1)

            @block.scalar
            def _(act):
                def high(n, s):
                    act.wait_ge(g_loaded[s], CREDIT + 8 * (n + 2 - s))
                    act.wait_ge(o_made, CREDIT + 2 * (n - 1))
                    nc.scalar.activation(g[s][:, HI, :, :], g_raw[s][:, :, :], ACT.Copy).then_inc(g_hi, 1)

                def high_y2(n, s):
                    act.wait_ge(y2_made, CREDIT + 2 * (n + 1))
                    act.wait_ge(y2_stored[s], CREDIT + 8 * (n - s))
                    nc.scalar.activation(y2[s][:, HI, :, :], y2_raw[:, :, :], ACT.Copy).then_inc(y2_hi, 1)

                def step(n, s, first=False, last=False):
                    if not last:
                        high(n + 1, 1 - s)
                    act.wait_ge(mean1, CREDIT + n - 1)
                    for half in range(HALVES):
                        act.wait_ge(o_made, CREDIT + 2 * n + half + 1)
                        act.wait_ge(squared2, CREDIT + n)
                        nc.scalar.activation(squares[:, half * 512:(half + 1) * 512], pO[s][half][:, :], ACT.Square,
                                             accum_out=ss[s][:, half:half + 1]).then_inc(squared, 1)
                    act.wait_ge(mean1, CREDIT + n + 1)
                    act.wait_ge(scaled, CREDIT + 2 * (n - 1))
                    nc.scalar.activation(rs[s][:, :], ss[s][:, 0:1], ACT.Sqrt, bias=eps[:, :], scale=1.0 / D)\
                        .then_inc(root1, 1)
                    act.wait_ge(h_ready, CREDIT + 2 * (n + 1))
                    act.wait_ge(squared, CREDIT + 2 * (n + 1))
                    nc.scalar.activation(squares[:, :], h[s][:, :], ACT.Square, accum_out=ss2[s][:, :])\
                        .then_inc(squared2, 1)
                    act.wait_ge(squared2, CREDIT + n + 1)
                    nc.scalar.activation(rs2[s][:, :], ss2[s][:, :], ACT.Sqrt, bias=eps[:, :], scale=1.0 / D)\
                        .then_inc(root2, 1)
                    if not first:
                        high_y2(n - 1, 1 - s)

                act.wait_ge(eps_set, 1)
                high(0, 0)
                for q in range(KC):
                    act.wait_ge(w_loaded[q], 16)
                    nc.scalar.activation(w[:, HI, q, :], w_raw[:, q, :], ACT.Copy).then_inc(w_hi, 1)
                steps(act, step)
                high_y2(NB - 1, 1)

            @block.vector
            def _(dve):
                V = nc.vector

                def low(n, s):
                    dve.wait_ge(g_hi, CREDIT + n + 1)
                    V.tensor_tensor(g[s][:, LO, :, :], g_raw[s][:, :, :], g[s][:, HI, :, :].bitcast(f32), ALU.subtract)\
                     .then_inc(g_lo, 1)

                def take_y2(n, s):
                    dve.wait_ge(y2_lo, CREDIT + n)
                    for i in range(2):
                        dve.wait_ge(t_made, CREDIT + 2 * n + i + 1)
                        V.tensor_tensor(y2_raw[:, 4 * i:4 * i + 4, :], pT[s][i][:, :].rearrange("p (c t) -> p c t", t=P),
                                        k.vec[:, G2 + 4 * i:G2 + 4 * i + 4].unsqueeze(2).to_broadcast([P, 4, P]),
                                        ALU.mult).then_inc(y2_made, 1)

                def step(n, s, first=False, last=False):
                    if not last:
                        low(n + 1, 1 - s)
                    dve.wait_ge(squared, CREDIT + 2 * (n + 1))
                    V.tensor_tensor(ss[s][:, 0:1], ss[s][:, 0:1], ss[s][:, 1:2], ALU.add).then_inc(mean1, 1)
                    dve.wait_ge(root1, CREDIT + n + 1)
                    V.reciprocal(rs[s][:, :], rs[s][:, :]).then_inc(rs_ready, 1)
                    dve.wait_ge(rs_ready, CREDIT + n + 1)
                    dve.wait_ge(h_stored[s], CREDIT + 8 * (n - s))
                    for half in range(HALVES):
                        cols = slice(half * 512, (half + 1) * 512)
                        V.scalar_tensor_tensor(out=h[s][:, cols], in0=pO[s][half][:, :], scalar=rs[s][:, :],
                                               in1=post_g[:, cols], op0=ALU.mult, op1=ALU.mult).then_inc(scaled, 1)
                    dve.wait_ge(xr_loaded[s], CREDIT + 8 * (n + 2 - s))
                    for half in range(HALVES):
                        cols = slice(half * 512, (half + 1) * 512)
                        dve.wait_ge(scaled, CREDIT + 2 * n + half + 1)
                        V.tensor_tensor(h[s][:, cols], h[s][:, cols], xr[s][:, cols], ALU.add).then_inc(h_ready, 1)
                    if not first:
                        take_y2(n - 1, 1 - s)
                    dve.wait_ge(root2, CREDIT + n + 1)
                    V.reciprocal(rs2[s][:, :], rs2[s][:, :]).then_inc(rs2_ready, 1)
                    dve.wait_ge(rs2_ready, CREDIT + n + 1)
                    dve.wait_ge(t_made, CREDIT + 2 * (n - 1))
                    V.tensor_scalar(hn[s][:, :], h[s][:, :], rs2[s][:, :], None, ALU.mult).then_inc(hn_ready, 1)

                low(0, 0)
                for q in range(KC):
                    dve.wait_ge(w_hi, q + 1)
                    V.tensor_tensor(w[:, LO, q, :], w_raw[:, q, :], w[:, HI, q, :].bitcast(f32), ALU.subtract)\
                     .then_inc(w_lo, 1)
                dve.wait_ge(post_loaded, 16)
                steps(dve, step)
                take_y2(NB - 1, 1)


def ffn(nc, k, a, h_dram, y2_dram, out):
    T = 512
    NT = S // T
    TB = T // P
    HALVES = D // 512
    ITEMS = 2 * FC
    HI, LO = 0, 1
    PASSES = ((HI, HI), (HI, LO), (LO, HI))
    w_in = a["ffn_w_in"][0, :, :].rearrange("(c p) f -> p c f", p=P)
    w_out = a["ffn_w_out"][0, :, :].rearrange("(c p) f -> c p f", p=P)
    out_rows = out[0, :, :].rearrange("(n p) d -> n p d", p=P)
    with ExitStack() as c:
        sb = lambda n, s, d=f32: c.enter_context(nc.sbuf_tensor(n, s, d))
        sem = lambda n: nc.alloc_semaphore(name=n)
        post_g = sb("post_g3", [P, D])
        y2 = sb("y2_split", [P, 2, KC, T], f32r)
        w_raw = [sb(f"w_raw{s}", [P, 2, KC * P]) for s in range(2)]
        w = [sb(f"w_split{s}", [P, 2, 2, KC * P], f32r) for s in range(2)]
        acts = sb("acts", [P, FC, T])
        act = [sb(f"act_split{s}", [P, 2, T], f32r) for s in range(2)]
        halo = sb("halo", [P, FC, 2])
        gate = [sb(f"gate{s}", [P, T + 2]) for s in range(2)]
        conv = [sb(f"conv{s}", [P, T]) for s in range(2)]
        conv_rows = sb("conv_rows", [4 * FC, P])
        conv_vec = sb("conv_vec", [P, 4, FC])
        o_sb = sb("o_sb", [P, TB, D])
        hb = sb("hb", [P, TB, D])
        squares = [sb(f"squares_f{s}", [P, 512]) for s in range(2)]
        ss = sb("ss_f", [P, TB, HALVES]); ss_sum = sb("ss_sum", [P, TB]); rs = sb("rs_f", [P, TB]); eps = sb("eps_f", [P, 1])
        po = [[c.enter_context(nc.psum_tensor(f"po{b}_{h}", [P, 512], f32)) for h in range(HALVES)] for b in range(TB)]
        pg, pu = [po[s][0] for s in range(2)], [po[s][1] for s in range(2)]

        credited = []

        def csem(n):
            credited.append(sem(n))
            return credited[-1]
        w_out_loaded = [csem(f"w_out_loaded{s}") for s in range(2)]; w_in_loaded = [csem(f"w_in_loaded{s}") for s in range(2)]
        y2_loaded = sem("y2_loaded"); hb_loaded = sem("hb_loaded"); stored = sem("out_stored")
        hi_made = csem("w_hi_made"); lo_made = csem("w_lo_made"); item_done = csem("item_done")
        act_hi_made = csem("act_hi_made"); act_lo_made = csem("act_lo_made")
        gate_made = csem("gate_made"); gate_copied = csem("gate_copied"); halo_in = csem("halo_in")
        halo_out = csem("halo_out"); conv0 = csem("conv0"); conv1 = csem("conv1"); conv2 = csem("conv2")
        silu_ready = csem("silu_ready"); act_ready = csem("act_ready")
        o_made = csem("o_made"); squared = csem("squared_f"); taken = csem("taken_f"); summed = csem("summed_f")
        root = csem("root_f"); rs_ready = csem("rs_ready_f"); scaled = csem("scaled_f"); out_ready = csem("out_ready")
        conv_loaded = sem("conv_loaded"); conv_t = sem("conv_t"); set_up = sem("set_up_f"); post_loaded = sem("post_loaded")
        held = sem("held_f")

        with nc.Block() as block:
            @block.gpsimd
            def _(pool):
                for s in credited:
                    pool.sem_inc(s, CREDIT)

        with nc.Block() as block:
            @block.sync
            def _(sp):
                def load_in(m, f, s, slot_sem=None):
                    sp.wait_ge(lo_made, CREDIT + m - 1)
                    sp.dma_start(w_raw[s][:, 0, :].rearrange("p (c f) -> p c f", f=P), w_in[:, :, bass.ts(f, P)])\
                      .then_inc(w_in_loaded[s], 16)
                    sp.dma_start(w_raw[s][:, 1, :].rearrange("p (c f) -> p c f", f=P), w_in[:, :, bass.ds(f * P + F, P)])\
                      .then_inc(w_in_loaded[s], 16)

                sp.dma_start(conv_rows[0:3 * FC, :], a["ffn_conv_w"][0, :, :].rearrange("w (c p) -> (w c) p", p=P))\
                  .then_inc(conv_loaded, 16)
                sp.dma_start(conv_rows[3 * FC:4 * FC, :], a["ffn_conv_b"][0, :].rearrange("(c p) -> c p", p=P))\
                  .then_inc(conv_loaded, 16)
                with sp.Fori(0, NT) as tt:
                    m0 = ITEMS * tt
                    with sp.Fori(0, FC // 2) as g:
                        for s in range(2):
                            load_in(m0 + 2 * g + s, 2 * g + s, s)
                    with sp.Fori(0, FC // 2) as g:
                        for s in range(2):
                            f = 2 * g + s
                            sp.wait_ge(lo_made, CREDIT + m0 + FC + f - 1)
                            sp.dma_start(w_raw[s][:, 0, :], w_out[bass.ds(f, 1), :, :].rearrange("o p d -> p (o d)"))\
                              .then_inc(w_out_loaded[s], 16)
                load_in(ITEMS * NT, 0, 0)

            @block.gpsimd
            def _(pool):
                nc.gpsimd.memset(eps[:, :], NORM_EPS).then_inc(set_up, 1)
                nc.gpsimd.memset(halo[:, :, :], 0.0).then_inc(set_up, 1)
                pool.dma_start(y2[:, :, :, :].bitcast(f32), y2_dram[:, :, :, 0:T]).then_inc(y2_loaded, 16)
                pool.dma_start(post_g[:, :], a["norm_g"][0, 3:4, :].to_broadcast([P, D])).then_inc(post_loaded, 16)

                def tile(tt, last):
                    if not last:
                        pool.wait_ge(item_done, CREDIT + ITEMS * tt + FC)
                        pool.sem_inc(held, 1)
                        pool.dma_start(y2[:, :, :, :].bitcast(f32), y2_dram[:, :, :, bass.ds((tt + 1) * T, T)]).then_inc(y2_loaded, 16)
                    pool.wait_ge(hb_loaded, 16 * (tt + 1))
                    for b in range(TB):
                        pool.wait_ge(scaled, CREDIT + TB * tt + b + 1)
                        nc.gpsimd.tensor_tensor(hb[:, b, :], hb[:, b, :], o_sb[:, b, :], ALU.add).then_inc(out_ready, 1)
                        pool.wait_ge(out_ready, CREDIT + TB * tt + b + 1)
                        pool.sem_inc(held, 1)
                        pool.dma_start(out_rows[bass.ds(TB * tt + b, 1), :, :].rearrange("o p d -> p (o d)"), hb[:, b, :])\
                            .then_inc(stored, 16)

                pool.dma_start(hb[:, :, :], h_dram[0:TB, :, :].rearrange("n p d -> p n d")).then_inc(hb_loaded, 16)
                with pool.Fori(0, NT - 1) as tt:
                    tile(tt, False)
                    pool.wait_ge(stored, 16 * TB * (tt + 1))
                    pool.sem_inc(held, 1)
                    pool.dma_start(hb[:, :, :], h_dram[bass.ds(TB * (tt + 1), TB), :, :].rearrange("n p d -> p n d"))\
                        .then_inc(hb_loaded, 16)
                tile(NT - 1, True)
                pool.wait_ge(stored, 16 * TB * NT)
                for s in range(2):
                    pool.wait_ge(w_in_loaded[s], CREDIT + 32 * (FC // 2 * NT + 1 - s))

            @block.tensor
            def _(pe):
                pe.wait_ge(conv_loaded, 32)
                nc.tensor.transpose(po[0][0][:, 0:4 * FC], conv_rows[:, :], k.ident[0:4 * FC, 0:4 * FC]).then_inc(conv_t, 1)
                pe.wait_ge(set_up, 3)
                with pe.Fori(0, NT) as tt:
                    with pe.Fori(0, FC // 2) as g:
                        for s in range(2):
                            n = FC * tt + 2 * g + s
                            pe.wait_ge(lo_made, CREDIT + ITEMS * tt + 2 * g + s + 1)
                            pe.wait_ge(y2_loaded, 16 * (tt + 1))
                            pe.wait_ge(gate_copied, CREDIT + n - 1)
                            pe.wait_ge(squared, CREDIT + HALVES * (TB * (tt - 1) + s + 1))
                            pe.wait_ge(taken, CREDIT + HALVES * (TB * (tt - 1) + s + 1))
                            for part, bank in ((0, pg[s]), (1, pu[s])):
                                if part == 1:
                                    pe.wait_ge(act_ready, CREDIT + n - 1)
                                for q in range(KC):
                                    for j, (x, y) in enumerate(PASSES):
                                        mm = nc.tensor.matmul(bank[:, :], w[s][:, x, part, q * P:(q + 1) * P],
                                                              y2[:, y, q, :], start=(q == 0 and j == 0),
                                                              stop=(q == KC - 1 and j == 2))
                                mm.then_inc((gate_made, item_done)[part], 1)

                    def outputs(f, s, first=False, last=False):
                        pe.wait_ge(lo_made, CREDIT + ITEMS * tt + FC + f + 1)
                        pe.wait_ge(act_lo_made, CREDIT + FC * tt + f + 1)
                        for b in ((0, 1, 2, 3) if last else (2, 3, 0, 1)):
                            if first:
                                if b < 2:
                                    pe.wait_ge(act_ready, CREDIT + FC * (tt + 1) - 1 + b)
                                pe.wait_ge(squared, CREDIT + HALVES * TB * tt)
                                pe.wait_ge(taken, CREDIT + HALVES * TB * tt)
                            for j, (x, y) in enumerate(PASSES):
                                for half in range(HALVES):
                                    mm = nc.tensor.matmul(po[b][half][:, :], act[s][:, x, b * P:(b + 1) * P],
                                                          w[s][:, y, 0, half * 512:(half + 1) * 512],
                                                          start=(first and j == 0), stop=(last and j == 2))
                            if last and b < TB - 1:
                                mm.then_inc(o_made, 1)
                        mm.then_inc(item_done, 1)

                    outputs(0, 0, first=True)
                    outputs(1, 1)
                    with pe.Fori(1, FC // 2 - 1) as g:
                        for s in range(2):
                            outputs(2 * g + s, s)
                    outputs(FC - 2, 0)
                    outputs(FC - 1, 1, last=True)

            def wait_block(eng, tt, b):
                if b < TB - 1:
                    eng.wait_ge(o_made, CREDIT + (TB - 1) * tt + b + 1)
                else:
                    eng.wait_ge(item_done, CREDIT + ITEMS * (tt + 1))

            @block.scalar
            def _(sc):
                def hi_in(m, n, s):
                    sc.wait_ge(w_in_loaded[s], CREDIT + 32 * (n + 1))
                    sc.wait_ge(item_done, CREDIT + m - 1)
                    nc.scalar.activation(w[s][:, HI, :, :], w_raw[s][:, :, :], ACT.Copy).then_inc(hi_made, 1)

                def hi_out(tt, f, g, s):
                    sc.wait_ge(w_out_loaded[s], CREDIT + 16 * (FC // 2 * tt + g + 1))
                    sc.wait_ge(item_done, CREDIT + ITEMS * tt + FC + f - 1)
                    nc.scalar.activation(w[s][:, HI, 0, :], w_raw[s][:, 0, :], ACT.Copy).then_inc(hi_made, 1)
                    sc.wait_ge(act_ready, CREDIT + FC * tt + f + 1)
                    nc.scalar.activation(act[s][:, HI, :], acts[:, bass.ds(f, 1), :].rearrange("p o t -> p (o t)"),
                                         ACT.Copy).then_inc(act_hi_made, 1)

                def gate_silu(tt, f, s):
                    n = FC * tt + f
                    sc.wait_ge(gate_made, CREDIT + n + 1)
                    sc.wait_ge(conv2, CREDIT + n - 1)
                    sc.wait_ge(halo_out, CREDIT + n - 1)
                    nc.scalar.activation(gate[s][:, 2:T + 2], pg[s][:, :], ACT.Copy).then_inc(gate_copied, 1)
                    sc.wait_ge(conv2, CREDIT + n + 1)
                    nc.scalar.activation(conv[s][:, :], conv[s][:, :], ACT.Silu).then_inc(silu_ready, 1)

                sc.wait_ge(set_up, 2)
                hi_in(0, 0, 0)
                with sc.Fori(0, NT) as tt:
                    with sc.Fori(0, FC // 2 - 1) as g:
                        hi_in(ITEMS * tt + 2 * g + 1, FC // 2 * tt + g, 1)
                        gate_silu(tt, 2 * g, 0)
                        hi_in(ITEMS * tt + 2 * g + 2, FC // 2 * tt + g + 1, 0)
                        gate_silu(tt, 2 * g + 1, 1)
                    hi_in(ITEMS * tt + FC - 1, FC // 2 * tt + FC // 2 - 1, 1)
                    gate_silu(tt, FC - 2, 0)
                    hi_out(tt, 0, 0, 0)
                    gate_silu(tt, FC - 1, 1)
                    with sc.Fori(0, FC // 2 - 1) as g:
                        hi_out(tt, 2 * g + 1, g, 1)
                        hi_out(tt, 2 * g + 2, g + 1, 0)
                    hi_out(tt, FC - 1, FC // 2 - 1, 1)
                    hi_in(ITEMS * (tt + 1), FC // 2 * (tt + 1), 0)
                    sc.wait_ge(summed, CREDIT + tt)
                    for b in range(TB):
                        wait_block(sc, tt, b)
                        for half in range(HALVES):
                            sc.wait_ge(squared, CREDIT + HALVES * (TB * tt + b) + half - 1)
                            nc.scalar.activation(squares[half][:, :], po[b][half][:, :], ACT.Square,
                                                 accum_out=ss[:, b, half:half + 1]).then_inc(squared, 1)
                    sc.wait_ge(summed, CREDIT + tt + 1)
                    sc.wait_ge(scaled, CREDIT + TB * tt)
                    nc.scalar.activation(rs[:, :], ss_sum[:, :], ACT.Sqrt, bias=eps[:, :], scale=1.0 / D).then_inc(root, 1)
                    sc.wait_ge(rs_ready, CREDIT + tt + 1)
                    for b in range(TB):
                        nc.scalar.activation(o_sb[:, b, :], o_sb[:, b, :], ACT.Copy, scale=rs[:, b:b + 1])\
                          .then_inc(scaled, 1)

            @block.vector
            def _(dve):
                V = nc.vector

                def lo_in(m, s):
                    dve.wait_ge(hi_made, CREDIT + m + 1)
                    V.tensor_tensor(w[s][:, LO, :, :], w_raw[s][:, :, :], w[s][:, HI, :, :].bitcast(f32), ALU.subtract)\
                     .then_inc(lo_made, 1)

                def lo_out(tt, f, s):
                    dve.wait_ge(hi_made, CREDIT + ITEMS * tt + FC + f + 1)
                    V.tensor_tensor(w[s][:, LO, 0, :], w_raw[s][:, 0, :], w[s][:, HI, 0, :].bitcast(f32), ALU.subtract)\
                     .then_inc(lo_made, 1)
                    dve.wait_ge(act_hi_made, CREDIT + FC * tt + f + 1)
                    V.tensor_tensor(act[s][:, LO, :], acts[:, bass.ds(f, 1), :].rearrange("p o t -> p (o t)"),
                                    act[s][:, HI, :].bitcast(f32), ALU.subtract).then_inc(act_lo_made, 1)

                def conv_gate(tt, f, s):
                    n = FC * tt + f
                    weight = lambda x: conv_vec[:, x, bass.ds(f, 1)]
                    dve.wait_ge(conv2, CREDIT + n - 1)
                    V.tensor_scalar(gate[s][:, 0:2], halo[:, bass.ds(f, 1), :].rearrange("p o t -> p (o t)"),
                                    1.0, None, ALU.mult).then_inc(halo_in, 1)
                    dve.wait_ge(gate_copied, CREDIT + n + 1)
                    dve.wait_ge(act_ready, CREDIT + n - 1)
                    V.tensor_scalar(conv[s][:, :], gate[s][:, 2:T + 2], weight(2), weight(3), ALU.mult, ALU.add)\
                     .then_inc(conv0, 1)
                    dve.wait_ge(halo_in, CREDIT + n + 1)
                    V.tensor_scalar(halo[:, bass.ds(f, 1), :].rearrange("p o t -> p (o t)"),
                                    gate[s][:, T:T + 2], 1.0, None, ALU.mult)\
                     .then_inc(halo_out, 1)
                    dve.wait_ge(conv0, CREDIT + n + 1)
                    V.scalar_tensor_tensor(out=conv[s][:, :], in0=gate[s][:, 1:T + 1], scalar=weight(1),
                                           in1=conv[s][:, :], op0=ALU.mult, op1=ALU.add).then_inc(conv1, 1)
                    dve.wait_ge(conv1, CREDIT + n + 1)
                    V.scalar_tensor_tensor(out=conv[s][:, :], in0=gate[s][:, 0:T], scalar=weight(0),
                                           in1=conv[s][:, :], op0=ALU.mult, op1=ALU.add).then_inc(conv2, 1)
                    dve.wait_ge(silu_ready, CREDIT + n + 1)
                    dve.wait_ge(item_done, CREDIT + ITEMS * tt + f + 1)
                    dve.wait_ge(act_lo_made, CREDIT + FC * tt)
                    V.tensor_tensor(acts[:, bass.ds(f, 1), :].rearrange("p o t -> p (o t)"), conv[s][:, :],
                                    pu[s][:, :], ALU.mult).then_inc(act_ready, 1)

                dve.wait_ge(conv_t, 1)
                dve.wait_ge(set_up, 2)
                V.tensor_copy(conv_vec[:, :, :].rearrange("p w c -> p (w c)"), po[0][0][:, 0:4 * FC]).then_inc(set_up, 1)
                dve.wait_ge(set_up, 3)
                dve.wait_ge(post_loaded, 16)
                lo_in(0, 0)
                with dve.Fori(0, NT) as tt:
                    with dve.Fori(0, FC // 2 - 1) as g:
                        for s in range(2):
                            lo_in(ITEMS * tt + 2 * g + s + 1, 1 - s)
                            conv_gate(tt, 2 * g + s, s)
                    lo_in(ITEMS * tt + FC - 1, 1)
                    conv_gate(tt, FC - 2, 0)
                    lo_out(tt, 0, 0)
                    conv_gate(tt, FC - 1, 1)
                    with dve.Fori(0, FC // 2 - 1) as g:
                        for s in range(2):
                            lo_out(tt, 2 * g + s + 1, 1 - s)
                    lo_out(tt, FC - 1, 1)
                    lo_in(ITEMS * (tt + 1), 0)
                    dve.wait_ge(out_ready, CREDIT + TB * tt)
                    for b in range(TB):
                        wait_block(dve, tt, b)
                        for half in range(HALVES):
                            cols = slice(half * 512, (half + 1) * 512)
                            dve.wait_ge(squared, CREDIT + HALVES * (TB * tt + b) + half + 1)
                            V.tensor_tensor(o_sb[:, b, cols], po[b][half][:, :], post_g[:, cols], ALU.mult)\
                             .then_inc(taken, 1)
                    dve.wait_ge(squared, CREDIT + HALVES * TB * (tt + 1))
                    dve.wait_ge(root, CREDIT + tt)
                    V.tensor_tensor(ss_sum[:, :], ss[:, :, 0], ss[:, :, 1], ALU.add).then_inc(summed, 1)
                    dve.wait_ge(root, CREDIT + tt + 1)
                    V.reciprocal(rs[:, :], rs[:, :]).then_inc(rs_ready, 1)


def trunk(nc: bass.Bass, a, out):
    scratch = nc.dram_tensor("scratch_rows", [NCH, KC, P, ROW], f32, kind="Internal").ap()
    gated = nc.dram_tensor("gated", [NCH + 1, KC, P, C], f32, kind="Internal").ap()
    h_dram = nc.dram_tensor("h_dram", [S // P, P, D], f32, kind="Internal").ap()
    y2_dram = nc.dram_tensor("y2_dram", [P, 2, KC, S], f32, kind="Internal").ap()
    with ExitStack() as ctx:
        k = constants(nc, ctx, a)
        with nc.cleanup_on_exit():
            project(nc, k, a, scratch)
        with nc.cleanup_on_exit():
            recur(nc, k, scratch, gated)
        with nc.cleanup_on_exit():
            attend_out(nc, k, a, gated, h_dram, y2_dram)
        with nc.cleanup_on_exit():
            ffn(nc, k, a, h_dram, y2_dram, out)


_INS = ["x", "norm_g", "ffn_w_in", "ffn_conv_w", "ffn_conv_b", "ffn_w_out", "rwkv_mu", "rwkv_w_rkv", "rwkv_w0",
        "rwkv_w1", "rwkv_w2", "rwkv_a0", "rwkv_a1", "rwkv_a2", "rwkv_g1", "rwkv_g2", "rwkv_k_k", "rwkv_k_a",
        "rwkv_r_k", "rwkv_ln_w", "rwkv_ln_b", "rwkv_w_o"]


def kernel(**inputs):
    import numpy as _np
    import concourse.bacc as _bacc
    from concourse import mybir as _mybir
    from concourse.bass_utils import run_bass_kernel_spmd as _run

    nc = _bacc.Bacc("TRN2", target_bir_lowering=False, num_devices=1)
    arrays, args = {}, {}
    for name in _INS:
        a = _np.ascontiguousarray(inputs[name])
        arrays[f"in_{name}_dram"] = a
        args[name] = nc.dram_tensor(f"in_{name}_dram", a.shape, _mybir.dt.from_np(a.dtype), kind="ExternalInput").ap()
    out = nc.dram_tensor("out_0_dram", (1, S, D), _mybir.dt.float32, kind="ExternalOutput").ap()
    trunk(nc, args, out)
    r = _run(nc, [arrays], core_ids=[0])
    return r.results[0]["out_0_dram"]
```

```python
import concourse.bass as bass
from concourse import mybir
from contextlib import ExitStack

import numpy as np

f32 = mybir.dt.float32
f16 = mybir.dt.float16
bf16 = mybir.dt.bfloat16
u32 = mybir.dt.uint32
f32r = mybir.dt.float32r
ALU = mybir.AluOpType
ACT = mybir.ActivationFunctionType

P = 128
D = 1024
S = 2048
KC = D // P
HD = 64
C = 128
NCH = S // C
LW, LA, LG = 64, 64, 128
F = 2816
FC = F // P
NORM_EPS = 1e-6
GN_EPS = 64e-5
CREDIT = 64
DECAY = float(np.exp(-0.5))

G0, MU, W0, A0, K_K, K_A, R_K, LN_W, LN_B, G2 = 0, 8, 56, 64, 72, 80, 88, 96, 104, 112
NV = 120
SA, SR, SB, SK, SV, SG, SBV, SM, SE = 0, 128, 256, 384, 512, 640, 768, 896, 897
ROW = 898


class Consts:
    pass


def constants(nc, ctx, a):
    k = Consts()
    sb = lambda n, s, d=f32: ctx.enter_context(nc.sbuf_tensor(n, s, d))
    k.ident = sb("ident", [P, P])
    k.ones_head = sb("ones_head", [P, P])
    k.vec = sb("vec", [P, NV])
    k.w0_half = sb("w0_half", [P, KC])
    k.a0_half = sb("a0_half", [P, KC])
    k.one_less_ka = sb("one_less_ka", [P, KC])
    with ExitStack() as c:
        rows = c.enter_context(nc.sbuf_tensor("vec_rows", [P, P], f32))
        pv = c.enter_context(nc.psum_tensor("pv", [P, P], f32))
        sem = lambda n: c.enter_context(nc.semaphore(n))
        rows_loaded, built, transposed, copied = sem("rows_loaded"), sem("built"), sem("transposed"), sem("copied")
        with nc.Block() as block:
            @block.sync
            def _(sp):
                lots = [(G0, a["norm_g"][0, 0, :]), (W0, a["rwkv_w0"][0, :]), (A0, a["rwkv_a0"][0, :]),
                        (K_K, a["rwkv_k_k"][0, :]), (K_A, a["rwkv_k_a"][0, :]), (LN_W, a["rwkv_ln_w"][0, :]),
                        (LN_B, a["rwkv_ln_b"][0, :]), (G2, a["norm_g"][0, 2, :])]
                for at, v in lots:
                    sp.dma_start(rows[at:at + KC, :], v.rearrange("(c p) -> c p", p=P)).then_inc(rows_loaded, 16)
                sp.dma_start(rows[R_K:R_K + KC, :],
                             a["rwkv_r_k"][0, :, :].rearrange("(c h) n -> c (h n)", h=2)).then_inc(rows_loaded, 16)
                sp.dma_start(rows[MU:MU + 6 * KC, :],
                             a["rwkv_mu"][0, :, :].rearrange("m (c p) -> (m c) p", p=P)).then_inc(rows_loaded, 16)

            @block.gpsimd
            def _(pool):
                nc.gpsimd.memset(k.ident[:, :], 0.0).then_inc(built, 1)
                nc.gpsimd.memset(k.ones_head[:, :], 1.0).then_inc(built, 1)
                pool.wait_ge(built, 2)
                nc.gpsimd.affine_select(out=k.ident[:, :], in_=k.ident[:, :], pattern=[[-1, P]],
                                        compare_op=ALU.not_equal, fill=1.0, base=0,
                                        channel_multiplier=1).then_inc(built, 1)
                nc.gpsimd.affine_select(out=k.ones_head[:, 0:HD], in_=k.ones_head[:, 0:HD], pattern=[[0, HD]],
                                        compare_op=ALU.is_ge, fill=0.0, base=HD - 1,
                                        channel_multiplier=-1).then_inc(built, 1)
                nc.gpsimd.affine_select(out=k.ones_head[:, HD:P], in_=k.ones_head[:, HD:P], pattern=[[0, HD]],
                                        compare_op=ALU.is_ge, fill=0.0, base=-HD,
                                        channel_multiplier=1).then_inc(built, 1)

            @block.tensor
            def _(pe):
                pe.wait_ge(built, 5)
                pe.wait_ge(rows_loaded, 160)
                nc.tensor.transpose(pv[:, 0:NV], rows[0:NV, :], k.ident[0:NV, 0:NV]).then_inc(transposed, 1)

            @block.vector
            def _(dve):
                dve.wait_ge(transposed, 1)
                nc.vector.tensor_copy(k.vec[:, :], pv[:, 0:NV]).then_inc(copied, 1)
                dve.wait_ge(copied, 1)
                nc.vector.tensor_scalar(k.w0_half[:, :], k.vec[:, W0:W0 + KC], 0.5, None, ALU.mult).then_inc(copied, 1)
                nc.vector.tensor_scalar(k.a0_half[:, :], k.vec[:, A0:A0 + KC], 0.5, None, ALU.mult).then_inc(copied, 1)
                nc.vector.tensor_scalar(k.one_less_ka[:, :], k.vec[:, K_A:K_A + KC], -1.0, 1.0,
                                        ALU.mult, ALU.add).then_inc(copied, 1)
                dve.wait_ge(copied, 4)
    return k


def project(nc, k, a, scratch):
    T = 256
    NT = S // T
    TB = T // P
    assert TB == T // C
    x_rows = a["x"][0, :, :].rearrange("(n p) d -> n p d", p=P)
    with ExitStack() as c:
        sb = lambda n, s, d=f32: c.enter_context(nc.sbuf_tensor(n, s, d))
        ps = lambda n: c.enter_context(nc.psum_tensor(n, [P, 512], f32))
        sem = lambda n: nc.alloc_semaphore(name=n)
        w_rkv = [sb(f"w_{n}", [P, KC, D]) for n in "rkv"]
        w1 = sb("w1", [P, KC, LW]); a1 = sb("a1", [P, KC, LA]); g1 = sb("g1", [P, KC, LG])
        w2 = sb("w2", [LW, D]); a2 = sb("a2", [LA, D]); g2 = sb("g2", [LG, D])
        xb = sb("xb", [P, TB, D])
        xsq = sb("xsq", [P, 2]); rstd = sb("rstd", [P, 2])
        yT = sb("yT", [P, KC, T + 1])
        xx = sb("xx", [P, KC, T])
        mix = [sb(f"mix{i}", [P, KC, T]) for i in range(2)]
        hid_w = sb("hid_w", [LW, T]); hid_a = sb("hid_a", [LA, T]); hid_g = sb("hid_g", [LG, T])
        kT = sb("kT", [P, KC, T])
        rnorm = sb("rnorm", [P, KC, T])
        out_rows = [sb(f"out_rows{i}", [P, TB, ROW]) for i in range(2)]
        sq = sb("sq", [P, T])
        not_first = sb("not_first", [P, T])
        tw = sb("tw", [P, T]); lw = sb("lw", [P, T]); cum = sb("cum", [P, T]); cm = sb("cm", [P, T])
        cx = sb("cx", [P, T]); e_in = sb("e_in", [P, T]); e_out = sb("e_out", [P, T]); e_pre = sb("e_pre", [P, T])
        gS = sb("gS", [P, T]); ta = sb("ta", [P, T]); kk = sb("kk", [P, T]); kn = sb("kn", [P, T]); rS = sb("rS", [P, T])
        zero = sb("zero", [P, KC, 1])

        pX = [ps("pX0"), ps("pX1")]; pP = [ps("pP0"), ps("pP1")]
        pH, pZ, pG, pS = ps("pH"), ps("pZ"), ps("pG"), ps("pS")

        credited = []

        def csem(n):
            credited.append(sem(n))
            return credited[-1]
        x_loaded = csem("x_loaded"); rkv_loaded = [sem(f"{n}_loaded") for n in ("wr", "wk", "wv")]
        lora_loaded = sem("lora_loaded")
        x_squared = csem("x_squared"); x_root = csem("x_root"); mean_ready = csem("mean_ready")
        rstd_ready = csem("rstd_ready"); xn_ready = csem("xn_ready")
        xt_ready = csem("xt_ready"); yt_ready = csem("yt_ready"); carried = csem("carried"); xx_ready = csem("xx_ready")
        mix_ready = csem("mix_ready"); hid_ready = csem("hid_ready"); hid_taken = csem("hid_taken")
        proj_ready = csem("proj_ready"); proj_taken = csem("proj_taken")
        sq_ready = csem("sq_ready"); ss_ready = csem("ss_ready"); ss_taken = csem("ss_taken")
        norm_root = csem("norm_root"); norm_ready = csem("norm_ready"); hid_g_ready = csem("hid_g_ready")
        z_ready = csem("z_ready"); zw_taken = csem("zw_taken"); za_taken = csem("za_taken")
        gate_ready = csem("gate_ready"); gate_taken = csem("gate_taken")
        lw_ready = csem("lw_ready"); cum_ready = csem("cum_ready"); cm_ready = csem("cm_ready"); cx_ready = csem("cx_ready")
        exp_ready = csem("exp_ready"); ends_ready = csem("ends_ready"); mid_ready = csem("mid_ready")
        rate_ready = csem("rate_ready"); kk_ready = csem("kk_ready"); b_ready = csem("b_ready")
        kn_ready = csem("kn_ready"); k_half = csem("k_half"); rk_ready = csem("rk_ready")
        bonus_ready = csem("bonus_ready"); bonus_taken = csem("bonus_taken"); rows_ready = csem("rows_ready")
        rows_stored = [csem(f"rows_stored{i}") for i in range(2)]
        set_up = sem("set_up"); zero_stored = sem("zero_stored")

        with nc.Block() as block:
            @block.gpsimd
            def _(pool):
                for s in credited:
                    pool.sem_inc(s, CREDIT)

        with nc.Block() as block:
            @block.sync
            def _(sp):
                sp.dma_start(xb[:, :, :], x_rows[0:TB, :, :].rearrange("n p d -> p n d")).then_inc(x_loaded, 16)
                for n in (1, 0, 2):
                    sp.dma_start(w_rkv[n][:, :, :], a["rwkv_w_rkv"][0, n, :, :].rearrange("(c p) f -> p c f", p=P))\
                      .then_inc(rkv_loaded[n], 16)
                    if n == 1:
                        for t, s in ((w1, "rwkv_w1"), (a1, "rwkv_a1"), (g1, "rwkv_g1")):
                            sp.dma_start(t[:, :, :], a[s][0, :, :].rearrange("(c p) f -> p c f", p=P))\
                              .then_inc(lora_loaded, 16)
                        for t, s in ((w2, "rwkv_w2"), (a2, "rwkv_a2"), (g2, "rwkv_g2")):
                            sp.dma_start(t[:, :], a[s][0, :, :]).then_inc(lora_loaded, 16)

                def load_x(tt):
                    sp.wait_ge(xt_ready, CREDIT + 2 * TB * tt)
                    sp.dma_start(xb[:, :, :], x_rows[bass.ts(tt, TB), :, :].rearrange("n p d -> p n d"))\
                      .then_inc(x_loaded, 16)

                def store_rows(tt):
                    for p in range(KC):
                        sp.wait_ge(rows_ready, CREDIT + KC * tt + p + 1)
                        sp.dma_start(scratch[bass.ts(tt, TB), p, :, :].rearrange("c q r -> q c r"),
                                     out_rows[p % 2][:, :, :]).then_inc(rows_stored[p % 2], 16)

                load_x(1)
                with sp.Fori(0, NT - 2) as tt:
                    store_rows(tt)
                    load_x(tt + 2)
                store_rows(NT - 2)
                store_rows(NT - 1)

            @block.gpsimd
            def _(pool):
                nc.gpsimd.memset(not_first[:, :], 1.0).then_inc(set_up, 1)
                pool.wait_ge(set_up, 1)
                nc.gpsimd.memset(not_first[:, 0:T:C], 0.0).then_inc(set_up, 1)
                nc.gpsimd.memset(yT[:, :, T:T + 1], 0.0).then_inc(set_up, 1)
                nc.gpsimd.memset(zero[:, :, :], 0.0).then_inc(set_up, 1)
                for i in range(2):
                    pool.wait_ge(rows_stored[i], CREDIT + 16 * NT * KC // 2)
                pool.dma_start(scratch[0, :, :, SM:SM + 1].rearrange("h q r -> q h r"),
                               zero[:, :, :], allow_slow_non_contiguous=True).then_inc(zero_stored, 16)
                pool.wait_ge(zero_stored, 16)

            @block.scalar
            def _(act):
                def square_x(tt):
                    act.wait_ge(x_loaded, CREDIT + 16 * (tt + 1))
                    act.wait_ge(mix_ready, CREDIT + 6 * tt)
                    for b in range(TB):
                        nc.scalar.activation(xx[:, b * (D // T):(b + 1) * (D // T), :], xb[:, b, :], ACT.Square,
                                             accum_out=xsq[:, b:b + 1]).then_inc(x_squared, 1)

                def root_x(tt):
                    act.wait_ge(mean_ready, CREDIT + tt + 1)
                    act.wait_ge(xn_ready, CREDIT + TB * tt)
                    nc.scalar.activation(rstd[:, :], xsq[:, :], ACT.Sqrt).then_inc(x_root, 1)

                def scale_x(tt):
                    act.wait_ge(rstd_ready, CREDIT + tt + 1)
                    for b in range(TB):
                        nc.scalar.activation(xb[:, b, :], xb[:, b, :], ACT.Copy, scale=rstd[:, b:b + 1])\
                          .then_inc(xn_ready, 1)

                def tile(tt, last):
                    def take_k(p):
                        act.wait_ge(proj_ready, CREDIT + 3 * KC * tt + p + 1)
                        if p == 0:
                            act.wait_ge(k_half, CREDIT + KC * tt)
                        nc.scalar.activation(kT[:, p, :], pP[p % 2][:, 0:T], ACT.Copy).then_inc(proj_taken, 1)
                        act.wait_ge(proj_taken, CREDIT + 3 * KC * tt + p + 1)
                        if p == 0:
                            act.wait_ge(ss_ready, CREDIT + KC * tt)
                        else:
                            act.wait_ge(ss_ready, CREDIT + KC * tt + p)
                        nc.scalar.activation(sq[:, :], kT[:, p, :], ACT.Square,
                                             scale=k.vec[:, K_K + p:K_K + p + 1]).then_inc(sq_ready, 1)

                    for p in range(KC):
                        take_k(p)
                    act.wait_ge(hid_ready, CREDIT + 3 * tt + 1)
                    nc.scalar.activation(hid_w[:, :], pX[0][0:LW, 0:T], ACT.Tanh).then_inc(hid_taken, 1)
                    act.wait_ge(hid_ready, CREDIT + 3 * tt + 2)
                    nc.scalar.activation(hid_a[:, :], pX[1][0:LA, 0:T], ACT.Copy).then_inc(hid_taken, 1)
                    act.wait_ge(hid_ready, CREDIT + 3 * tt + 3)
                    nc.scalar.activation(hid_g[:, :], pH[:, 0:T], ACT.Tanh, scale=0.5).then_inc(hid_taken, 1)
                    act.wait_ge(ss_taken, CREDIT + KC * (tt + 1))
                    nc.scalar.activation(rnorm[:, :, :], rnorm[:, :, :], ACT.Sqrt).then_inc(norm_root, 1)
                    for p in range(KC):
                        rows = out_rows[p % 2]
                        n = KC * tt + p
                        act.wait_ge(z_ready, CREDIT + n + 1)
                        act.wait_ge(lw_ready, CREDIT + n)
                        nc.scalar.activation(tw[:, :], pZ[:, 0:T], ACT.Tanh, bias=k.w0_half[:, p:p + 1],
                                             scale=0.5).then_inc(zw_taken, 1)
                        act.wait_ge(rk_ready, CREDIT + n)
                        nc.scalar.activation(ta[:, :], pZ[:, T:2 * T], ACT.Tanh, bias=k.a0_half[:, p:p + 1],
                                             scale=0.5).then_inc(za_taken, 1)
                        act.wait_ge(proj_ready, CREDIT + 3 * KC * tt + KC + 2 * p + 1)
                        act.wait_ge(bonus_ready, CREDIT + n)
                        nc.scalar.activation(rS[:, :], pP[0][:, 0:T], ACT.Copy).then_inc(proj_taken, 1)
                        act.wait_ge(rows_stored[p % 2], CREDIT + 16 * (KC // 2 * tt + p // 2))
                        act.wait_ge(gate_ready, CREDIT + n + 1)
                        act.wait_ge(rows_ready, CREDIT + n)
                        nc.scalar.activation(gS[:, :], pG[:, 0:T], ACT.Copy).then_inc(gate_taken, 1)
                        act.wait_ge(proj_ready, CREDIT + 3 * KC * tt + KC + 2 * p + 2)
                        nc.scalar.activation(rows[:, :, SV:SV + C], pP[1][:, 0:T].rearrange("q (c t) -> q c t", t=C),
                                             ACT.Copy).then_inc(proj_taken, 1)
                        act.wait_ge(cm_ready, CREDIT + n + 1)
                        nc.scalar.activation(e_in[:, :], cm[:, :], ACT.Exp).then_inc(exp_ready, 1)
                        nc.scalar.activation(e_out[:, :], cm[:, :], ACT.Exp, scale=-1.0).then_inc(exp_ready, 1)
                        act.wait_ge(cx_ready, CREDIT + n + 1)
                        nc.scalar.activation(e_pre[:, :], cx[:, :], ACT.Exp).then_inc(exp_ready, 1)
                        nc.scalar.activation(rows[:, :, SM], cum[:, C // 2 - 1:T:C], ACT.Exp).then_inc(exp_ready, 1)
                        nc.scalar.activation(rows[:, :, SE], cm[:, C - 1:T:C], ACT.Exp).then_inc(exp_ready, 1)
                        if p == 2 and not last:
                            square_x(tt + 1)
                        if p == 3 and not last:
                            root_x(tt + 1)
                        if p == 4 and not last:
                            scale_x(tt + 1)

                square_x(0)
                root_x(0)
                scale_x(0)
                with act.Fori(0, NT - 1) as tt:
                    tile(tt, False)
                tile(NT - 1, True)

            @block.vector
            def _(dve):
                V = nc.vector
                dve.wait_ge(set_up, 4)
                def mean_x(tt):
                    dve.wait_ge(x_squared, CREDIT + TB * (tt + 1))
                    V.tensor_scalar(xsq[:, :], xsq[:, :], 1.0 / D, NORM_EPS, ALU.mult, ALU.add).then_inc(mean_ready, 1)

                def invert_root(tt):
                    dve.wait_ge(x_root, CREDIT + tt + 1)
                    V.reciprocal(rstd[:, :], rstd[:, :]).then_inc(rstd_ready, 1)

                def take_y(tt, b):
                    if b == 0:
                        dve.wait_ge(mix_ready, CREDIT + 6 * tt)
                        V.tensor_copy(yT[:, :, 0:1], yT[:, :, T:T + 1]).then_inc(carried, 1)
                        dve.wait_ge(carried, CREDIT + tt + 1)
                    for q in range(2):
                        dve.wait_ge(xt_ready, CREDIT + 2 * TB * tt + 2 * b + q + 1)
                        V.tensor_tensor(yT[:, 4 * q:4 * q + 4, 1 + b * P:1 + (b + 1) * P],
                                        pX[q][:, :].rearrange("p (c t) -> p c t", t=P),
                                        k.vec[:, G0 + 4 * q:G0 + 4 * q + 4].unsqueeze(2).to_broadcast([P, 4, P]),
                                        ALU.mult).then_inc(yt_ready, 1)
                    if b == TB - 1:
                        dve.wait_ge(yt_ready, CREDIT + 2 * TB * (tt + 1))
                        V.tensor_tensor(xx[:, :, :], yT[:, :, 0:T], yT[:, :, 1:T + 1], ALU.subtract).then_inc(xx_ready, 1)

                def blend(tt, n, m):
                    if n < 2:
                        dve.wait_ge(proj_ready, CREDIT + 3 * KC * tt - 1 + n)
                    elif n == 2:
                        dve.wait_ge(proj_ready, CREDIT + 3 * KC * tt + KC)
                    else:
                        dve.wait_ge(hid_ready, CREDIT + 3 * tt + n - 2)
                    dve.wait_ge(xx_ready, CREDIT + tt + 1)
                    for q in range(KC):
                        last = V.scalar_tensor_tensor(
                            out=mix[n % 2][:, q, :], in0=xx[:, q, :],
                            scalar=k.vec[:, MU + m * KC + q:MU + m * KC + q + 1],
                            in1=yT[:, q, 1:T + 1], op0=ALU.mult, op1=ALU.add)
                    last.then_inc(mix_ready, 1)

                def tile(tt, last):
                    blend(tt, 1, 1)
                    dve.wait_ge(kk_ready, CREDIT + KC * tt)
                    for p in range(KC):
                        dve.wait_ge(ss_ready, CREDIT + KC * tt + p + 1)
                        V.tensor_scalar(rnorm[:, p, :], pS[:, 0:T], 1e-24, None, ALU.max).then_inc(ss_taken, 1)
                    blend(tt, 2, 4)
                    blend(tt, 3, 5)
                    blend(tt, 4, 0)
                    dve.wait_ge(hid_taken, CREDIT + 3 * tt + 3)
                    V.tensor_scalar(hid_g[:, :], hid_g[:, :], 0.5, 0.5, ALU.mult, ALU.add).then_inc(hid_g_ready, 1)
                    blend(tt, 5, 3)
                    dve.wait_ge(norm_root, CREDIT + tt + 1)
                    for p in range(KC):
                        rows = out_rows[p % 2]
                        n = KC * tt + p
                        by_chunk = lambda t: t[:, :].rearrange("q (c t) -> q c t", t=C)
                        if p == KC - 1 and not last:
                            blend(tt + 1, 0, 2)
                        if p == 3 and not last:
                            mean_x(tt + 1)
                        dve.wait_ge(zw_taken, CREDIT + n + 1)
                        V.tensor_scalar(lw[:, :], tw[:, :], -0.5 * DECAY, -0.5 * DECAY, ALU.mult, ALU.add)\
                            .then_inc(lw_ready, 1)
                        dve.wait_ge(lw_ready, CREDIT + n + 1)
                        dve.wait_ge(exp_ready, CREDIT + 5 * n)
                        V.tensor_tensor_scan(cum[:, :], not_first[:, :], lw[:, :], 0.0, ALU.mult, ALU.add)\
                            .then_inc(cum_ready, 1)
                        dve.wait_ge(cum_ready, CREDIT + n + 1)
                        V.tensor_tensor(by_chunk(cm), by_chunk(cum),
                                        cum[:, C // 2 - 1:T:C].unsqueeze(2).to_broadcast([P, TB, C]),
                                        ALU.subtract).then_inc(cm_ready, 1)
                        dve.wait_ge(cm_ready, CREDIT + n + 1)
                        V.tensor_tensor(cx[:, :], cm[:, :], lw[:, :], ALU.subtract).then_inc(cx_ready, 1)
                        V.reciprocal(rnorm[:, p, :], rnorm[:, p, :]).then_inc(norm_ready, 1)
                        dve.wait_ge(norm_ready, CREDIT + n + 1)
                        V.scalar_tensor_tensor(out=kk[:, :], in0=kT[:, p, :], scalar=k.vec[:, K_K + p:K_K + p + 1],
                                               in1=rnorm[:, p, :], op0=ALU.mult, op1=ALU.mult).then_inc(kk_ready, 1)
                        dve.wait_ge(za_taken, CREDIT + n + 1)
                        V.tensor_scalar(ta[:, :], ta[:, :], 0.5, 0.5, ALU.mult, ALU.add).then_inc(rate_ready, 1)
                        dve.wait_ge(rate_ready, CREDIT + n + 1)
                        V.tensor_scalar(kn[:, :], ta[:, :], k.vec[:, K_A + p:K_A + p + 1], k.one_less_ka[:, p:p + 1],
                                        ALU.mult, ALU.add).then_inc(kn_ready, 1)
                        dve.wait_ge(kn_ready, CREDIT + 2 * n + 1)
                        V.tensor_tensor(kn[:, :], kn[:, :], kT[:, p, :], ALU.mult).then_inc(kn_ready, 1)
                        dve.wait_ge(kn_ready, CREDIT + 2 * n + 2)
                        dve.wait_ge(rows_stored[p % 2], CREDIT + 16 * (KC // 2 * tt + p // 2))
                        dve.wait_ge(kk_ready, CREDIT + n + 1)
                        V.tensor_tensor(ta[:, :], ta[:, :], kk[:, :], ALU.mult).then_inc(b_ready, 1)
                        dve.wait_ge(exp_ready, CREDIT + 5 * n + 5)
                        V.tensor_tensor(rows[:, :, SK:SK + C], by_chunk(kn), by_chunk(e_out), ALU.mult)\
                            .then_inc(k_half, 1)
                        V.tensor_tensor(rows[:, :, SA:SA + C], by_chunk(kk), by_chunk(e_pre), ALU.mult)
                        dve.wait_ge(b_ready, CREDIT + n + 1)
                        V.tensor_tensor(rows[:, :, SB:SB + C], by_chunk(ta), by_chunk(e_out), ALU.mult)
                        dve.wait_ge(proj_taken, CREDIT + 3 * KC * tt + KC + 2 * p + 2)
                        V.tensor_tensor(rows[:, :, SR:SR + C], by_chunk(rS), by_chunk(e_in), ALU.mult)
                        V.scalar_tensor_tensor(out=rS[:, :], in0=rS[:, :], scalar=k.vec[:, R_K + p:R_K + p + 1],
                                               in1=kn[:, :], op0=ALU.mult, op1=ALU.mult).then_inc(rk_ready, 1)
                        dve.wait_ge(gate_taken, CREDIT + n + 1)
                        V.tensor_scalar(rows[:, :, SG:SG + C], by_chunk(gS), k.vec[:, LN_W + p:LN_W + p + 1], None,
                                        ALU.mult)
                        dve.wait_ge(bonus_ready, CREDIT + n + 1)
                        V.tensor_tensor(by_chunk(cx), pS[:, 0:T].rearrange("q (c t) -> q c t", t=C),
                                        rows[:, :, SV:SV + C], ALU.mult).then_inc(bonus_taken, 1)
                        dve.wait_ge(bonus_taken, CREDIT + n + 1)
                        V.scalar_tensor_tensor(out=rows[:, :, SBV:SBV + C], in0=by_chunk(cx),
                                               scalar=k.vec[:, LN_B + p:LN_B + p + 1], in1=by_chunk(gS),
                                               op0=ALU.add, op1=ALU.mult).then_inc(rows_ready, 1)
                        if p == 3 and not last:
                            invert_root(tt + 1)
                        if p in (5, 6) and not last:
                            take_y(tt + 1, p - 5)

                mean_x(0)
                invert_root(0)
                take_y(0, 0)
                take_y(0, 1)
                blend(0, 0, 2)
                with dve.Fori(0, NT - 1) as tt:
                    tile(tt, False)
                tile(NT - 1, True)

            @block.tensor
            def _(pe):
                T_ = nc.tensor

                def proj(n, w, p, m, tt):
                    pe.wait_ge(proj_taken, CREDIT + 3 * KC * tt + n - 1)
                    for q in range(KC):
                        mm = T_.matmul(pP[n % 2][:, 0:T], w[:, q, p * P:(p + 1) * P], mix[m % 2][:, q, :],
                                       start=(q == 0), stop=(q == KC - 1))
                    mm.then_inc(proj_ready, 1)

                def transposes(tt, b):
                    pe.wait_ge(hid_taken, CREDIT + 3 * tt)
                    pe.wait_ge(xn_ready, CREDIT + TB * tt + b + 1)
                    for q in range(2):
                        if b >= 1:
                            pe.wait_ge(yt_ready, CREDIT + 2 * TB * tt + 2 * b + q - 1)
                        for j in range(4):
                            mm = T_.transpose(pX[q][:, j * P:(j + 1) * P],
                                              xb[:, b, (4 * q + j) * P:(4 * q + j + 1) * P], k.ident[:, :])
                        mm.then_inc(xt_ready, 1)

                def first_key(tt):
                    pe.wait_ge(mix_ready, CREDIT + 6 * tt + 1)
                    proj(0, w_rkv[1], 0, 0, tt)

                def tile(tt, last):
                    def sums(p):
                        pe.wait_ge(sq_ready, CREDIT + KC * tt + p + 1)
                        pe.wait_ge(ss_taken, CREDIT + KC * tt + p)
                        if p == 0:
                            pe.wait_ge(rows_ready, CREDIT + KC * tt)
                        T_.matmul(pS[:, 0:T], k.ones_head[:, :], sq[:, :], start=True, stop=True).then_inc(ss_ready, 1)

                    for p in range(1, KC):
                        proj(p, w_rkv[1], p, 0, tt)
                        sums(p - 1)
                    pe.wait_ge(lora_loaded, 96)
                    sums(KC - 1)
                    pe.wait_ge(yt_ready, CREDIT + 2 * TB * (tt + 1))
                    for i, (dst, w) in enumerate(((pX[0][0:LW, 0:T], w1), (pX[1][0:LA, 0:T], a1), (pH[:, 0:T], g1))):
                        pe.wait_ge(mix_ready, CREDIT + 6 * tt + 2 + i)
                        for q in range(KC):
                            mm = T_.matmul(dst, w[:, q, :], mix[(1 + i) % 2][:, q, :],
                                           start=(q == 0), stop=(q == KC - 1))
                        mm.then_inc(hid_ready, 1)
                    pe.wait_ge(hid_taken, CREDIT + 3 * tt + 3)
                    pe.wait_ge(hid_g_ready, CREDIT + tt + 1)

                    def bonus(p):
                        pe.wait_ge(rk_ready, CREDIT + KC * tt + p + 1)
                        pe.wait_ge(rows_ready, CREDIT + KC * tt + p)
                        T_.matmul(pS[:, 0:T], k.ones_head[:, :], rS[:, :], start=True, stop=True)\
                            .then_inc(bonus_ready, 1)

                    for p in range(KC):
                        n = KC * tt + p
                        f = slice(p * P, (p + 1) * P)
                        pe.wait_ge(za_taken, CREDIT + n)
                        T_.matmul(pZ[:, 0:T], w2[:, f], hid_w[:, :], start=True, stop=True)
                        T_.matmul(pZ[:, T:2 * T], a2[:, f], hid_a[:, :], start=True, stop=True).then_inc(z_ready, 1)
                        if p == 0:
                            pe.wait_ge(mix_ready, CREDIT + 6 * tt + 5)
                            pe.wait_ge(rkv_loaded[0], 16)
                        proj(KC + 2 * p, w_rkv[0], p, 0, tt)
                        if p == KC - 1 and not last:
                            transposes(tt + 1, 1)
                        pe.wait_ge(gate_taken, CREDIT + n)
                        T_.matmul(pG[:, 0:T], g2[:, f], hid_g[:, :], start=True, stop=True).then_inc(gate_ready, 1)
                        if p == 0:
                            pe.wait_ge(mix_ready, CREDIT + 6 * tt + 6)
                            pe.wait_ge(rkv_loaded[2], 16)
                        if p >= 1:
                            bonus(p - 1)
                        proj(KC + 2 * p + 1, w_rkv[2], p, 1, tt)
                        if p == 5 and not last:
                            transposes(tt + 1, 0)
                    if not last:
                        first_key(tt + 1)
                    bonus(KC - 1)

                transposes(0, 0)
                transposes(0, 1)
                pe.wait_ge(rkv_loaded[1], 16)
                first_key(0)
                with pe.Fori(0, NT - 1) as tt:
                    tile(tt, False)
                tile(NT - 1, True)




def recur(nc, k, scratch, gated):
    Q = 4
    NBK = 2
    GROUPS = ((0, 1), (2, 3))
    QP = KC // Q
    QH = 2 * QP
    LEVELS = [2, 4, 8, 16, 32, 64]
    MASKED = 4
    NI = NCH
    with ExitStack() as c:
        sb = lambda n, s, d=f32: c.enter_context(nc.sbuf_tensor(n, s, d))
        sem = lambda n: nc.alloc_semaphore(name=n)
        rows = [sb(f"rows{i}", [P, KC, ROW]) for i in range(2)]
        arx = [sb(f"arx{q}", [P, QP, 2, 2 * C]) for q in range(Q)]
        att_b = [sb(f"att_b{q}", [P, QP, 2, 2 * C]) for q in range(Q)]
        att_k = [sb(f"att_k{q}", [P, QP, 2, 2 * C]) for q in range(Q)]
        tok = [sb(f"tok{q}", [P, QP, 3, P]) for q in range(Q)]
        rhs = [sb(f"rhs{q}", [P, QP, 2, 2, HD]) for q in range(Q)]
        rhs16 = [sb(f"rhs16_{q}", [P, QP, 2, 2, HD], bf16) for q in range(Q)]
        res16 = [sb(f"res16_{q}", [P, QP, 2, 2, HD], bf16) for q in range(Q)]
        sol = [sb(f"sol{q}", [P, QP, 2, 2, HD]) for q in range(Q)]
        lT16 = [sb(f"lT16_{q}", [P, QH, C], f16) for q in range(Q)]
        t16 = [sb(f"t16_{q}", [P, QH, C], f16) for q in range(Q)]
        tT16 = [sb(f"tT16_{q}", [P, QH, C], f16) for q in range(Q)]
        u16 = [sb(f"u16_{q}", [P, QH, C], f16) for q in range(Q)]
        w1T = [sb(f"w1T{q}", [P, QP, C]) for q in range(Q)]
        U = [sb(f"U{q}", [P, QP, P]) for q in range(Q)]
        z = [sb(f"z{q}", [P, QP, P]) for q in range(Q)]
        zt = [sb(f"zt{q}", [P, QP, P]) for q in range(Q)]
        scale = [sb(f"scale{g}", [P, KC // 2, 1]) for g in range(2)]
        eps = sb("eps", [P, 1])
        y = [sb(f"y{q}", [P, QP, C]) for q in range(Q)]
        yc = [sb(f"yc{q}", [P, QP, C]) for q in range(Q)]
        yn = [sb(f"yn{q}", [P, QP, C]) for q in range(Q)]
        yg = [sb(f"yg{q}", [P, QP, C]) for q in range(Q)]
        causal = sb("causal", [P, 2 * C])
        lower = sb("lower", [P, MASKED, C])
        upper = sb("upper", [P, 1 + MASKED, C])
        start = sb("start", [P, C])
        centre = sb("centre", [P, P])
        ident16 = sb("ident16", [P, P], f16)

        bank = [[c.enter_context(nc.psum_tensor(f"bank{q}_{j}", [P, 512], f32)) for j in range(NBK)] for q in range(Q)]

        fills = [("tok0", "act"), ("tok1", "act"), ("centred", "act"), ("b0", "dve"), ("k0", "dve"),
                 ("var", "act"), ("b1", "dve"), ("k1", "dve"),
                 ("mv", "act"), ("t", "act")]
        for m in LEVELS:
            fills += [(f"u{m}", "act")] + ([(f"w{m}", "dve")] if m != LEVELS[-1] else []) + [(f"wT{m}", "dve")]
        fills += [("z0", "act"), ("r0", "dve"), ("d0", "dve"), ("r1", "dve"), ("d1", "dve"),
                  ("w1T", "act"), ("U", "dve"), ("zn", "dve"), ("Y", "act")]
        names = [f for f, _ in fills]
        NF = len(fills)
        assert NF % NBK == 0
        per = {e: sum(t == e for _, t in fills) for e in ("act", "dve")}
        place = lambda name: names.index(name)
        bank_of = lambda q, name: bank[q][place(name) % NBK]

        credited = []

        def csem(n):
            credited.append(sem(n))
            return credited[-1]

        ends = {"centred": 1, "var": 2}

        def nth(name, i=0):
            n = place(name)
            after = type(i) is int and i == NI
            return fills[n][1], ends[name] if after else sum(t == fills[n][1] for _, t in fills[:n + 1])

        filled = [csem(f"filled{q}") for q in range(Q)]
        took = {e: [csem(f"{e}_took{q}") for q in range(Q)] for e in ("act", "dve")}

        def wait_taken(eng, q, i, name):
            e, n = nth(name, i)
            eng.wait_ge(took[e][q], CREDIT + per[e] * i + n)

        def wait_filled(eng, q, i, name):
            n = ends[name] if type(i) is int and i == NI else place(name) + 1
            eng.wait_ge(filled[q], CREDIT + NF * i + n)

        def wait_bank(eng, q, i, name, *needs):
            n = place(name)
            for e in ("act", "dve"):
                counts = [nth(f)[1] for f in needs if nth(f)[0] == e]
                last, its = fills[n - NBK]
                if its == e:
                    counts.append(nth(last)[1] - (per[e] if n < NBK else 0))
                if counts:
                    eng.wait_ge(took[e][q], CREDIT + per[e] * i + max(counts))

        rows_loaded = [csem(f"rowsB_loaded{u}") for u in range(2)]
        expanded = csem("expanded"); lT_ready = [csem(f"lT_ready{q}") for q in range(Q)]
        tT_ready = [csem(f"tT_ready{q}") for q in range(Q)]; rhs16_ready = [csem(f"rhs16_ready{q}") for q in range(Q)]
        scale_ready = [csem(f"scale_ready{g}") for g in range(2)]; z_scaled = [csem(f"z_scaled{q}") for q in range(Q)]
        masks = sem("masks"); cleared = sem("cleared")
        held = sem("held")
        yn_ready = csem("yn_ready"); ya_ready = csem("ya_ready"); gated_ready = csem("gated_ready")
        yg_ready = csem("yg_ready")
        yg_stored = csem("yg_stored")

        flat = lambda t: t[:, :, :, :, :].rearrange("p g a h d -> p (g a h d)")
        set_up = {}

        def wait_set_up(eng):
            eng.wait_ge(masks, set_up["masks"])
            eng.wait_ge(cleared, set_up["cleared"])

        rounds = ["tok0", "tok1", "centred", "bk0", "var", "bk1", "mv", "t"]
        rounds += [f"{kind}{m}" for m in LEVELS for kind in ("u", "w", "wT") if (kind, m) != ("w", LEVELS[-1])]
        rounds += ["z0", "r0", "d0", "r1", "d1", "w1T", "U", "zn", "Y"]
        LAG = 9

        def all_steps(eng, do):
            def step(i, u, first=False):
                for n, name in enumerate(rounds):
                    do(name, i, u, GROUPS[0], 0)
                    if n >= LAG:
                        do(rounds[n - LAG], i, u, GROUPS[1], 1)
                    elif not first:
                        do(rounds[n - LAG], i - 1, 1 - u, GROUPS[1], 1)

            step(0, 0, first=True)
            with eng.Fori(0, NI // 2 - 1) as j:
                step(2 * j + 1, 1)
                step(2 * j + 2, 0)
            step(NI - 1, 1)
            for name in rounds[-LAG:]:
                do(name, NI - 1, 1, GROUPS[1], 1)

        def wait_rows(eng, i, u):
            eng.wait_ge(rows_loaded[u], CREDIT + 8 * (i - u) + 16)

        with nc.Block() as block:
            @block.gpsimd
            def _(pool):
                for s in credited:
                    pool.sem_inc(s, CREDIT)

        with nc.Block() as block:
            @block.gpsimd
            def _(pool):
                G = nc.gpsimd
                n = 0
                for t in (causal, lower, upper):
                    G.memset(t[:], 1.0).then_inc(masks, 1); n += 1
                G.tensor_copy(ident16[:, :], k.ident[:, :]).then_inc(masks, 1); n += 1
                pool.wait_ge(masks, n)
                for j, op in ((0, ALU.is_gt), (1, ALU.is_ge)):
                    v = causal[:, j * C:(j + 1) * C]
                    G.affine_select(out=v, in_=v, pattern=[[1, C]], compare_op=op, fill=0.0, base=0,
                                    channel_multiplier=-1).then_inc(masks, 1); n += 1
                for table, part, sizes in ((lower, 0, LEVELS[:MASKED]), (upper, 1, [1] + LEVELS[:MASKED])):
                    for j, m in enumerate(sizes):
                        v = table[:, j, :].rearrange("p (b e x) -> p b e x", e=2, x=m)
                        G.memset(v[:, :, 1 - part, :], 0.0).then_inc(masks, 1); n += 1
                        v = v[:, :, part, :]
                        row0 = m * (1 - part)
                        G.affine_select(out=v, in_=v, pattern=[[-2 * m, C // (2 * m)], [0, m]], compare_op=ALU.is_ge,
                                        fill=0.0, base=-row0, channel_multiplier=1).then_inc(masks, 1); n += 1
                        pool.wait_ge(masks, n)
                        G.affine_select(out=v, in_=v, pattern=[[2 * m, C // (2 * m)], [0, m]], compare_op=ALU.is_ge,
                                        fill=0.0, base=row0 + m - 1, channel_multiplier=-1).then_inc(masks, 1); n += 1
                pool.wait_ge(masks, n)
                G.tensor_tensor(start[:, :], k.ident[:, :], upper[:, 0, :], ALU.subtract).then_inc(masks, 1); n += 1
                pool.wait_ge(masks, n)
                for t in arx:
                    G.memset(t[:], 0.0).then_inc(masks, 1); n += 1
                set_up["masks"] = n

                set_up["cleared"] = len(att_b + att_k + zt + z + y + scale) + 2 + 2 * KC + 1
                wait_set_up(pool)

                def finish(i, slot, qs):
                    for q in qs:
                        pool.wait_ge(yn_ready, CREDIT + Q * i + q + 1)
                        pairs = slice(q * QP, (q + 1) * QP)
                        if q == qs[0]:
                            pool.wait_ge(yg_stored, CREDIT + 16 * Q * i)
                        G.tensor_tensor(yg[q][:, :, :], yc[q][:, :, :], yn[q][:, :, :], ALU.mult).then_inc(ya_ready, 1)
                        pool.wait_ge(ya_ready, CREDIT + Q * i + q + 1)
                        G.tensor_tensor(yg[q][:, :, :], yg[q][:, :, :], rows[slot][:, pairs, SG:SG + C], ALU.mult)\
                         .then_inc(gated_ready, 1)
                        pool.wait_ge(gated_ready, CREDIT + Q * i + q + 1)
                        G.tensor_tensor(yg[q][:, :, :], yg[q][:, :, :], rows[slot][:, pairs, SBV:SBV + C], ALU.add)\
                         .then_inc(yg_ready, 1)
                    pool.wait_ge(yg_ready, CREDIT + Q * i + qs[-1] + 1)

                with pool.Fori(0, NI // 2) as j:
                    for u in range(2):
                        i = 2 * j + u
                        wait_rows(pool, i, u)
                        for qs in GROUPS:
                            wait_filled(pool, qs[-1], i - 1, "k1")
                            pool.sem_inc(held, 1)
                            for q in qs:
                                for p in range(QP):
                                    for h in range(2):
                                        part = slice(h * HD, (h + 1) * HD)
                                        G.tensor_copy(arx[q][part, p, h, :], rows[u][part, q * QP + p, SA:SB])\
                                            .then_inc(expanded, 1)
                        pool.wait_ge(expanded, CREDIT + 2 * KC * (i + 1))
                        for qs in GROUPS:
                            for q in qs:
                                wait_taken(pool, q, i, "b1")
                                G.tensor_tensor(tT16[q][:, :, :].rearrange("p (a h) t -> p (a h) t", h=2),
                                                att_b[q][:, :, :, 0:C].rearrange("p a h t -> p (a h) t"),
                                                start[:, :].unsqueeze(1).to_broadcast([P, QH, C]), ALU.mult)\
                                 .then_inc(tT_ready[q], 1)
                            for q in qs:
                                wait_taken(pool, q, i, "mv")
                                pool.sem_inc(held, 1)
                                G.tensor_copy(flat(rhs16[q]), flat(rhs[q])).then_inc(rhs16_ready[q], 1)
                            finish(i, 1 - u, qs)
                finish(NI, 1, range(Q))

            @block.sync
            def _(sp):
                def store(i):
                    for q in range(Q):
                        sp.wait_ge(yg_ready, CREDIT + Q * i + q + 1)
                        sp.dma_start(gated[bass.ds(i, 1), q * QP:(q + 1) * QP, :, :].rearrange("o p q r -> q (o p) r"),
                                     yg[q][:, :, :]).then_inc(yg_stored, 16)

                def load(i, u):
                    sp.wait_ge(yg_ready, CREDIT + Q * i)
                    sp.dma_start(rows[u][:, :, :], scratch[bass.ds(i, 1), :, :, :].rearrange("o p q r -> q (o p) r"))\
                      .then_inc(rows_loaded[u], 16)

                load(0, 0)
                with sp.Fori(0, NI // 2 - 1) as j:
                    for u in range(2):
                        store(2 * j + u)
                        load(2 * j + u + 1, 1 - u)
                store(NI - 2)
                load(NI - 1, 1)
                store(NI - 1)
                store(NI)
                sp.wait_ge(yg_stored, CREDIT + 16 * Q * (NI + 1))

            @block.scalar
            def _(act):
                def copy(q, i, name, out, in_, scale=1.0, last=True):
                    wait_filled(act, q, i, name)
                    ins = nc.scalar.activation(out, in_, ACT.Copy, scale=scale)
                    if last:
                        ins.then_inc(took["act"][q], 1)

                def do(name, i, u, qs, g):
                    for q in qs:
                        if name in ("tok0", "tok1"):
                            p, b = int(name[-1]), bank_of(q, name)
                            copy(q, i, name, rhs[q][:, p, 0, :, :],
                                 b[:, 0:P].rearrange("p (h d) -> p h d", h=2), last=False)
                            copy(q, i, name, tok[q][:, p, :, :], b[:, P:4 * P].rearrange("p (a d) -> p a d", a=3))
                        elif name == "centred":
                            act.wait_ge(ya_ready, CREDIT + Q * (i - 1) + q + 1)
                            wait_filled(act, q, i, "centred")
                            got = bank_of(q, "centred")[:, 0:QP * C].rearrange("p (a t) -> p a t", t=C)
                            nc.scalar.activation(yc[q][:, :, :], got, ACT.Copy)
                            nc.scalar.activation(yn[q][:, :, :], got, ACT.Square).then_inc(took["act"][q], 1)
                        elif name == "var":
                            wait_filled(act, q, i, "var")
                            nc.scalar.activation(yn[q][:, :, :], bank_of(q, "var")[:, 0:QP * C]
                                                 .rearrange("p (a t) -> p a t", t=C), ACT.Sqrt,
                                                 bias=eps[:, :], scale=1.0 / HD).then_inc(took["act"][q], 1)
                        elif name == "mv":
                            b = bank_of(q, "mv")[:, :].rearrange("p (a h e d) -> p a h e d", a=QP, h=2, e=2)
                            for h in range(2):
                                copy(q, i, "mv", rhs[q][:, :, 1, h, :], b[:, :, h, h, :], last=(h == 1))
                            wait_taken(act, q, i, "b1")
                            nc.scalar.activation(lT16[q][:, :, :].rearrange("p (a h) t -> p a h t", h=2),
                                                 att_b[q][:, :, :, 0:C], ACT.Copy).then_inc(lT_ready[q], 1)
                        elif name == "t":
                            copy(q, i, "t", t16[q][:, :, :],
                                 bank_of(q, "t")[:, 0:256].bitcast(f16).rearrange("p (h t) -> p h t", t=C))
                        elif name[0] == "u":
                            copy(q, i, name, u16[q][:, :, :],
                                 bank_of(q, name)[:, :].rearrange("p (h t) -> p h t", t=C), scale=-1.0)
                        elif name == "z0":
                            copy(q, i, "z0", flat(sol[q]), bank_of(q, "z0")[:, :])
                        elif name == "w1T":
                            copy(q, i, "w1T", w1T[q][:, :, :],
                                 bank_of(q, "w1T")[:, 0:QP * C].rearrange("p (a t) -> p a t", t=C))
                        elif name == "Y":
                            copy(q, i, "Y", y[q][:, :, :],
                                 bank_of(q, "Y")[:, 0:QP * C].rearrange("p (a t) -> p a t", t=C))

                wait_set_up(act)
                all_steps(act, do)
                do("centred", NI, 0, range(Q), 0)
                do("var", NI, 0, range(Q), 0)

            @block.vector
            def _(dve):
                V = nc.vector
                by_head = lambda b: b[:, :].rearrange("p (h t) -> p h t", t=C)
                both_masks = causal[:, :].bitcast(u32).unsqueeze(1).to_broadcast([P, 2, 2 * C])

                def grow(q, m, table, mask, b, part):
                    dve.sem_inc(held, 1)
                    if m < 32:
                        V.copy_predicated(table[:, :, :], mask.bitcast(u32).unsqueeze(1).to_broadcast([P, QH, C]),
                                          by_head(b)).then_inc(took["dve"][q], 1)
                        return
                    for at in range(0, C, 2 * m):
                        down = slice(at + m * (1 - part), at + m * (2 - part))
                        across = slice(at + m * part, at + m * (1 + part))
                        last = V.tensor_scalar(table[down, :, across], by_head(b)[down, :, across], 1.0, None, ALU.mult)
                    last.then_inc(took["dve"][q], 1)

                def do(name, i, u, qs, g):
                    if name == "w1T":
                        pairs = slice(qs[0] * QP, (qs[-1] + 1) * QP)
                        wait_rows(dve, i, u)
                        dve.wait_ge(scale_ready[g], CREDIT + 2 * i)
                        V.tensor_tensor(scale[g][:, :, :], scale[g][:, :, :], rows[u][:, pairs, SM:SM + 1], ALU.mult)\
                         .then_inc(scale_ready[g], 1)
                        dve.wait_ge(scale_ready[g], CREDIT + 2 * i + 1)
                        for n, q in enumerate(qs):
                            wait_taken(dve, q, i - 1, "zn")
                            wait_filled(dve, q, i, "d1")
                            for p in range(QP):
                                V.scalar_tensor_tensor(
                                    out=z[q][:, p, :], in0=zt[q][:, p, :], scalar=scale[g][:, n * QP + p, :],
                                    in1=k.ones_head[:, :], op0=ALU.mult, op1=ALU.mult).then_inc(z_scaled[q], 1)
                        for q in qs:
                            dve.wait_ge(z_scaled[q], CREDIT + QP * (i + 1))
                        V.tensor_copy(scale[g][:, :, :], rows[u][:, pairs, SE:SE + 1]).then_inc(scale_ready[g], 1)
                        return
                    for q in qs:
                        if name in ("bk0", "bk1"):
                            p = int(name[-1])
                            for fill, dst in ((f"b{p}", att_b), (f"k{p}", att_k)):
                                wait_filled(dve, q, i, fill)
                                if fill == "b0":
                                    dve.wait_ge(lT_ready[q], CREDIT + i)
                                dve.sem_inc(held, 1)
                                V.copy_predicated(dst[q][:, p, :, :], both_masks,
                                                  bank_of(q, fill)[:, :].rearrange("p (h t) -> p h t", h=2))\
                                 .then_inc(took["dve"][q], 1)
                        elif name == "u2":
                            wait_taken(dve, q, i, "var")
                            V.reciprocal(yn[q][:, :, :], yn[q][:, :, :]).then_inc(yn_ready, 1)
                        elif name[0] == "w":
                            m = int(name.lstrip("wT"))
                            l = LEVELS.index(m)
                            mask = min(l, MASKED - 1)
                            wait_filled(dve, q, i, name)
                            if name[1] == "T":
                                if l == 0:
                                    dve.wait_ge(tT_ready[q], CREDIT + i + 1)
                                else:
                                    wait_taken(dve, q, i, f"wT{m // 2}")
                                grow(q, m, tT16[q], upper[:, 1 + mask, :], bank_of(q, name), 1)
                            else:
                                wait_taken(dve, q, i, "t" if l == 0 else f"w{m // 2}")
                                grow(q, m, t16[q], lower[:, mask, :], bank_of(q, name), 0)
                        elif name in ("r0", "r1"):
                            wait_filled(dve, q, i, name)
                            V.tensor_tensor(flat(res16[q]), flat(rhs[q]), bank_of(q, name)[:, :], ALU.subtract)\
                             .then_inc(took["dve"][q], 1)
                        elif name in ("d0", "d1"):
                            wait_filled(dve, q, i, name)
                            wait_taken(dve, q, i, "z0" if name == "d0" else "d0")
                            V.tensor_tensor(flat(sol[q]), flat(sol[q]), bank_of(q, name)[:, :], ALU.add)\
                             .then_inc(took["dve"][q], 1)
                        elif name == "U":
                            wait_filled(dve, q, i, "U")
                            wait_taken(dve, q, i, "d1")
                            V.scalar_tensor_tensor(
                                out=U[q][:, :, :], in0=bank_of(q, "U")[:, 0:QP * P].rearrange("p (g d) -> p g d", g=QP),
                                scalar=-1.0, in1=sol[q][:, :, 1, :, :].rearrange("p g h d -> p g (h d)"),
                                op0=ALU.mult, op1=ALU.subtract).then_inc(took["dve"][q], 1)
                        elif name == "zn":
                            wait_filled(dve, q, i, "zn")
                            V.tensor_tensor(zt[q][:, :, :], z[q][:, :, :],
                                            bank_of(q, "zn")[:, 0:QP * P].rearrange("p (a d) -> p a d", a=QP),
                                            ALU.add).then_inc(took["dve"][q], 1)

                for t in att_b + att_k + zt + z + y + scale:
                    V.memset(t[:], 0.0).then_inc(cleared, 1)
                V.memset(eps[:, :], GN_EPS).then_inc(cleared, 1)
                V.memset(rows[1][:, :, SG:ROW], 0.0).then_inc(cleared, 1)
                dve.wait_ge(cleared, set_up["cleared"] - 2 * KC - 1)
                for q in range(Q):
                    for p in range(QP):
                        for h in range(2):
                            V.tensor_copy(att_b[q][:, p, h, 0:C], k.ident[:, :]).then_inc(cleared, 1)
                V.scalar_tensor_tensor(out=centre[:, :], in0=k.ones_head[:, :], scalar=-1.0 / HD, in1=k.ident[:, :],
                                       op0=ALU.mult, op1=ALU.add).then_inc(cleared, 1)
                wait_set_up(dve)
                all_steps(dve, do)
                do("u2", NI, 0, range(Q), 0)

            @block.tensor
            def _(pe):
                T = nc.tensor

                def solve(q, name, lhs, right):
                    out = bank_of(q, name)[:, :].rearrange("p (g a h d) -> p g a h d", g=QP, a=2, h=2)
                    for h in range(QH):
                        mm = T.matmul(out[:, h // 2, :, h % 2, :], lhs(h), right[:, h // 2, :, h % 2, :],
                                      start=True, stop=True)
                    mm.then_inc(filled[q], 1)

                def do(name, i, u, qs, g):
                    if name == "tok0":
                        wait_rows(pe, i, u)
                    for q in qs:
                        if name in ("tok0", "tok1"):
                            wait_bank(pe, q, i, name)
                            for n, at in enumerate((SA, SB, SK, SV)):
                                mm = T.transpose(bank_of(q, name)[:, n * P:(n + 1) * P],
                                                 rows[u][:, q * QP + int(name[-1]), at:at + C], k.ident[:, :])
                            mm.then_inc(filled[q], 1)
                        elif name == "centred":
                            if type(i) is int and i == NI:
                                for e in ("act", "dve"):
                                    pe.wait_ge(took[e][q], CREDIT + per[e] * i)
                            else:
                                wait_bank(pe, q, i, "centred")
                                wait_taken(pe, q, i - 1, "Y")
                            T.matmul(bank_of(q, "centred")[:, 0:QP * C], centre[:, :],
                                     y[q][:, :, :].rearrange("p a t -> p (a t)"), start=True, stop=True)\
                             .then_inc(filled[q], 1)
                        elif name == "var":
                            if not (type(i) is int and i == NI):
                                wait_bank(pe, q, i, "var")
                            wait_taken(pe, q, i, "centred")
                            T.matmul(bank_of(q, "var")[:, 0:QP * C], k.ones_head[:, :],
                                     yn[q][:, :, :].rearrange("p a t -> p (a t)"), start=True, stop=True)\
                             .then_inc(filled[q], 1)
                        elif name in ("bk0", "bk1"):
                            p = int(name[-1])
                            pe.wait_ge(expanded, CREDIT + 2 * KC * i + 2 * (q * QP + p) + 2)
                            for fill, at in ((f"b{p}", SB), (f"k{p}", SK)):
                                wait_bank(pe, q, i, fill)
                                T.matmul(bank_of(q, fill)[:, :], rows[u][:, q * QP + p, at:at + C],
                                         arx[q][:, p, :, :].rearrange("p h t -> p (h t)"),
                                         start=True, stop=True).then_inc(filled[q], 1)
                        elif name == "mv":
                            wait_bank(pe, q, i, "mv", "k1", "tok1")
                            for h in range(QH):
                                mm = T.matmul(bank_of(q, "mv")[:, h * P:(h + 1) * P], att_k[q][:, h // 2, h % 2, 0:C],
                                              tok[q][:, h // 2, 2, :], start=True, stop=True)
                            mm.then_inc(filled[q], 1)
                        elif name == "t":
                            wait_bank(pe, q, i, "t")
                            pe.wait_ge(tT_ready[q], CREDIT + i + 1)
                            for h in range(QH):
                                mm = T.transpose(bank_of(q, "t")[:, 64 * h:64 * (h + 1)].bitcast(f16), tT16[q][:, h, :],
                                                 ident16[:, :])
                            mm.then_inc(filled[q], 1)
                        elif name[0] == "u":
                            m = int(name[1:])
                            wait_bank(pe, q, i, name, "t" if m == LEVELS[0] else f"w{m // 2}")
                            if m == LEVELS[0]:
                                pe.wait_ge(lT_ready[q], CREDIT + i + 1)
                            for h in range(QH):
                                mm = T.matmul(bank_of(q, name)[:, h * C:(h + 1) * C], lT16[q][:, h, :],
                                              t16[q][:, h, :], start=True, stop=True)
                            mm.then_inc(filled[q], 1)
                        elif name == "w1T":
                            wait_bank(pe, q, i, "w1T", "d1")
                            for p in range(QP):
                                mm = T.transpose(bank_of(q, "w1T")[:, p * C:(p + 1) * C],
                                                 sol[q][:, p, 0, :, :].rearrange("p h d -> p (h d)"), k.ident[:, :])
                            mm.then_inc(filled[q], 1)
                        elif name[0] == "w":
                            m = int(name.lstrip("wT"))
                            wait_bank(pe, q, i, name, f"u{m}", *([f"wT{m // 2}"] if m != LEVELS[0] else []))
                            for h in range(QH):
                                left, right = (u16, tT16) if name[1] == "T" else (tT16, u16)
                                mm = T.matmul(bank_of(q, name)[:, h * C:(h + 1) * C], left[q][:, h, :],
                                              right[q][:, h, :], start=True, stop=True)
                            mm.then_inc(filled[q], 1)
                        elif name == "z0":
                            wait_bank(pe, q, i, "z0", f"wT{LEVELS[-1]}")
                            pe.wait_ge(rhs16_ready[q], CREDIT + i + 1)
                            solve(q, name, lambda h: tT16[q][:, h, :], rhs16[q])
                        elif name in ("r0", "r1"):
                            wait_bank(pe, q, i, name, "z0" if name == "r0" else "d0")
                            solve(q, name, lambda h: att_b[q][:, h // 2, h % 2, 0:C], sol[q])
                        elif name in ("d0", "d1"):
                            wait_bank(pe, q, i, name, "r" + name[1])
                            solve(q, name, lambda h: tT16[q][:, h, :], res16[q])
                        elif name == "U":
                            wait_bank(pe, q, i, "U", "w1T")
                            pe.wait_ge(z_scaled[q], CREDIT + QP * (i + 1))
                            for p in range(QP):
                                mm = T.matmul(bank_of(q, "U")[:, p * P:(p + 1) * P], w1T[q][:, p, :], z[q][:, p, :],
                                              start=True, stop=True)
                            mm.then_inc(filled[q], 1)
                        elif name == "zn":
                            wait_bank(pe, q, i, "zn", "U")
                            for p in range(QP):
                                out = bank_of(q, "zn")[:, p * P:(p + 1) * P]
                                T.matmul(out, tok[q][:, p, 0, :], U[q][:, p, :], start=True, stop=False)
                                mm = T.matmul(out, tok[q][:, p, 1, :], tok[q][:, p, 2, :], start=False, stop=True)
                            mm.then_inc(filled[q], 1)
                        elif name == "Y":
                            wait_bank(pe, q, i, "Y")
                            b = bank_of(q, "Y")
                            for p in range(QP):
                                cols = slice(p * C, (p + 1) * C)
                                T.matmul(b[:, cols], z[q][:, p, :], rows[u][:, q * QP + p, SR:SR + C],
                                         start=True, stop=False, skip_group_check=True)
                                for of, att, last in (("U", att_b, False), ("V", att_k, True)):
                                    for h in range(2):
                                        part = slice(h * HD, (h + 1) * HD)
                                        left = U[q][:, p, part] if of == "U" else tok[q][:, p, 2, part]
                                        mm = T.matmul(b[part, cols], left, att[q][:, p, h, C:2 * C],
                                                      start=False, stop=last, skip_group_check=True)
                            mm.then_inc(filled[q], 1)

                wait_set_up(pe)
                all_steps(pe, do)
                do("centred", NI, 0, range(Q), 0)
                do("var", NI, 0, range(Q), 0)


def attend_out(nc, k, a, gated, h_dram, y2_dram):
    NB = S // P
    HALVES = D // 512
    HI, LO = 0, 1
    PASSES = ((HI, HI), (HI, LO), (LO, HI))
    x_rows = a["x"][0, :, :].rearrange("(n p) d -> n p d", p=P)
    w_dram = a["rwkv_w_o"][0, :, :].rearrange("(c p) f -> p c f", p=P)
    with ExitStack() as c:
        sb = lambda n, s, d=f32: c.enter_context(nc.sbuf_tensor(n, s, d))
        ps = lambda n: c.enter_context(nc.psum_tensor(n, [P, 512], f32))
        sem = lambda n: nc.alloc_semaphore(name=n)
        w_raw = sb("wo_raw", [P, KC, D])
        w = sb("wo_split", [P, 2, KC, D], f32r)
        post_g = sb("post_g", [P, D])
        g_raw = [sb(f"g_raw{s}", [P, KC, P]) for s in range(2)]
        g = [sb(f"g_split{s}", [P, 2, KC, P], f32r) for s in range(2)]
        xr = [sb(f"xr{s}", [P, D]) for s in range(2)]
        squares = sb("squares", [P, D])
        ss = [sb(f"ss{s}", [P, 2]) for s in range(2)]
        rs = [sb(f"rs{s}", [P, 1]) for s in range(2)]
        ss2 = [sb(f"ss2_{s}", [P, 1]) for s in range(2)]
        rs2 = [sb(f"rs2_{s}", [P, 1]) for s in range(2)]
        h = [sb(f"h{s}", [P, D]) for s in range(2)]
        hn = [sb(f"hn{s}", [P, D]) for s in range(2)]
        y2_raw = sb("y2_raw", [P, KC, P])
        y2 = [sb(f"y2_{s}", [P, 2, KC, P], f32r) for s in range(2)]
        eps = sb("eps_c", [P, 1])
        pO = [[ps(f"pO{s}_{j}") for j in range(HALVES)] for s in range(2)]
        pT = [[ps(f"pT{s}_{j}") for j in range(2)] for s in range(2)]

        credited = []

        def csem(n):
            credited.append(sem(n))
            return credited[-1]
        g_loaded = [csem(f"g_loaded{s}") for s in range(2)]; xr_loaded = [csem(f"xr_loaded{s}") for s in range(2)]
        g_hi = csem("g_hi"); g_lo = csem("g_lo")
        o_made = csem("o_ready"); squared = csem("squared"); mean1 = csem("mean1"); root1 = csem("root1")
        rs_ready = csem("rs_ready"); scaled = csem("scaled"); h_ready = csem("h_ready"); squared2 = csem("squared2")
        root2 = csem("root2"); rs2_ready = csem("rs2_ready"); hn_ready = csem("hn_ready")
        t_made = csem("t_ready"); y2_made = csem("y2_made"); y2_hi = csem("y2_hi"); y2_lo = csem("y2_lo")
        h_stored = [csem(f"h_stored{s}") for s in range(2)]; y2_stored = [csem(f"y2_stored{s}") for s in range(2)]
        w_loaded = [sem(f"wo_loaded{q}") for q in range(KC)]; w_hi = sem("wo_hi"); w_lo = sem("wo_lo")
        eps_set = sem("eps_set")
        post_loaded = sem("post_g_loaded")

        with nc.Block() as block:
            @block.gpsimd
            def _(pool):
                for s in credited:
                    pool.sem_inc(s, CREDIT)

        def steps(eng, step):
            step(0, 0, first=True)
            with eng.Fori(0, NB // 2 - 1) as j:
                step(2 * j + 1, 1)
                step(2 * j + 2, 0)
            step(NB - 1, 1, last=True)

        with nc.Block() as block:
            @block.sync
            def _(sp):
                def load_g(n, s):
                    sp.dma_start(g_raw[s][:, :, :], gated[bass.ds(n + 1, 1), :, :, :].rearrange("o p q r -> q (o p) r"))\
                      .then_inc(g_loaded[s], 16)

                def load_x(n, s):
                    sp.dma_start(xr[s][:, :], x_rows[bass.ds(n, 1), :, :].rearrange("o p d -> p (o d)"))\
                      .then_inc(xr_loaded[s], 16)

                def step(n, s, first=False, load=True):
                    if load:
                        sp.wait_ge(g_lo, CREDIT + n + 1)
                        load_g(n + 2, s)
                    if not first:
                        sp.wait_ge(y2_lo, CREDIT + n)
                        sp.dma_start(y2_dram[:, :, :, bass.ds((n - 1) * P, P)], y2[1 - s][:, :, :, :].bitcast(f32))\
                          .then_inc(y2_stored[1 - s], 16)
                    sp.wait_ge(h_ready, CREDIT + 2 * (n + 1))
                    sp.dma_start(h_dram[bass.ds(n, 1), :, :].rearrange("o p d -> p (o d)"), h[s][:, :])\
                      .then_inc(h_stored[s], 16)
                    if load:
                        load_x(n + 2, s)

                load_g(0, 0)
                for q in range(KC):
                    sp.dma_start(w_raw[:, q, :], w_dram[:, q, :]).then_inc(w_loaded[q], 16)
                load_x(0, 0)
                sp.dma_start(post_g[:, :], a["norm_g"][0, 1:2, :].to_broadcast([P, D])).then_inc(post_loaded, 16)
                load_g(1, 1)
                load_x(1, 1)
                step(0, 0, first=True)
                with sp.Fori(0, NB // 2 - 2) as j:
                    step(2 * j + 1, 1)
                    step(2 * j + 2, 0)
                step(NB - 3, 1)
                step(NB - 2, 0, load=False)
                step(NB - 1, 1, load=False)
                sp.wait_ge(y2_lo, CREDIT + NB)
                sp.dma_start(y2_dram[:, :, :, (NB - 1) * P:NB * P], y2[1][:, :, :, :].bitcast(f32))\
                  .then_inc(y2_stored[1], 16)
                for s in range(2):
                    sp.wait_ge(h_stored[s], CREDIT + 16 * (NB // 2))
                    sp.wait_ge(y2_stored[s], CREDIT + 16 * (NB // 2))

            @block.gpsimd
            def _(pool):
                nc.gpsimd.memset(eps[:, :], NORM_EPS).then_inc(eps_set, 1)
                with pool.Fori(0, NB // 2) as j:
                    for s in range(2):
                        pool.wait_ge(y2_hi, CREDIT + 2 * j + s + 1)
                        nc.gpsimd.tensor_tensor(y2[s][:, LO, :, :], y2_raw[:, :, :], y2[s][:, HI, :, :].bitcast(f32),
                                                ALU.subtract).then_inc(y2_lo, 1)

            @block.tensor
            def _(pe):
                def transposes(n, s):
                    pe.wait_ge(hn_ready, CREDIT + n + 1)
                    pe.wait_ge(y2_made, CREDIT + 2 * (n - 1))
                    for i in range(2):
                        for q in range(4):
                            mm = nc.tensor.transpose(pT[s][i][:, q * P:(q + 1) * P],
                                                     hn[s][:, (4 * i + q) * P:(4 * i + q + 1) * P], k.ident[:, :])
                        mm.then_inc(t_made, 1)

                def step(n, s, first=False, last=False):
                    pe.wait_ge(g_lo, CREDIT + n + 1)
                    pe.wait_ge(scaled, CREDIT + 2 * (n - 1))
                    if first:
                        for q in range(KC):
                            pe.wait_ge(w_lo, q + 1)
                            for half in range(HALVES):
                                for j, (x, y) in enumerate(PASSES):
                                    mm = nc.tensor.matmul(pO[s][half][:, :], g[s][:, x, q, :],
                                                          w[:, y, q, half * 512:(half + 1) * 512],
                                                          start=(q == 0 and j == 0), stop=(q == KC - 1 and j == 2))
                                if q == KC - 1:
                                    mm.then_inc(o_made, 1)
                    else:
                        for half in range(HALVES):
                            for q in range(KC):
                                for j, (x, y) in enumerate(PASSES):
                                    mm = nc.tensor.matmul(pO[s][half][:, :], g[s][:, x, q, :],
                                                          w[:, y, q, half * 512:(half + 1) * 512],
                                                          start=(q == 0 and j == 0), stop=(q == KC - 1 and j == 2))
                            mm.then_inc(o_made, 1)
                        transposes(n - 1, 1 - s)

                steps(pe, step)
                transposes(NB - 1, 1)

            @block.scalar
            def _(act):
                def high(n, s):
                    act.wait_ge(g_loaded[s], CREDIT + 8 * (n + 2 - s))
                    act.wait_ge(o_made, CREDIT + 2 * (n - 1))
                    nc.scalar.activation(g[s][:, HI, :, :], g_raw[s][:, :, :], ACT.Copy).then_inc(g_hi, 1)

                def high_y2(n, s):
                    act.wait_ge(y2_made, CREDIT + 2 * (n + 1))
                    act.wait_ge(y2_stored[s], CREDIT + 8 * (n - s))
                    nc.scalar.activation(y2[s][:, HI, :, :], y2_raw[:, :, :], ACT.Copy).then_inc(y2_hi, 1)

                def step(n, s, first=False, last=False):
                    if not last:
                        high(n + 1, 1 - s)
                    act.wait_ge(mean1, CREDIT + n - 1)
                    for half in range(HALVES):
                        act.wait_ge(o_made, CREDIT + 2 * n + half + 1)
                        act.wait_ge(squared2, CREDIT + n)
                        nc.scalar.activation(squares[:, half * 512:(half + 1) * 512], pO[s][half][:, :], ACT.Square,
                                             accum_out=ss[s][:, half:half + 1]).then_inc(squared, 1)
                    act.wait_ge(mean1, CREDIT + n + 1)
                    act.wait_ge(scaled, CREDIT + 2 * (n - 1))
                    nc.scalar.activation(rs[s][:, :], ss[s][:, 0:1], ACT.Sqrt, bias=eps[:, :], scale=1.0 / D)\
                        .then_inc(root1, 1)
                    act.wait_ge(h_ready, CREDIT + 2 * (n + 1))
                    act.wait_ge(squared, CREDIT + 2 * (n + 1))
                    nc.scalar.activation(squares[:, :], h[s][:, :], ACT.Square, accum_out=ss2[s][:, :])\
                        .then_inc(squared2, 1)
                    act.wait_ge(squared2, CREDIT + n + 1)
                    nc.scalar.activation(rs2[s][:, :], ss2[s][:, :], ACT.Sqrt, bias=eps[:, :], scale=1.0 / D)\
                        .then_inc(root2, 1)
                    if not first:
                        high_y2(n - 1, 1 - s)

                act.wait_ge(eps_set, 1)
                high(0, 0)
                for q in range(KC):
                    act.wait_ge(w_loaded[q], 16)
                    nc.scalar.activation(w[:, HI, q, :], w_raw[:, q, :], ACT.Copy).then_inc(w_hi, 1)
                steps(act, step)
                high_y2(NB - 1, 1)

            @block.vector
            def _(dve):
                V = nc.vector

                def low(n, s):
                    dve.wait_ge(g_hi, CREDIT + n + 1)
                    V.tensor_tensor(g[s][:, LO, :, :], g_raw[s][:, :, :], g[s][:, HI, :, :].bitcast(f32), ALU.subtract)\
                     .then_inc(g_lo, 1)

                def take_y2(n, s):
                    dve.wait_ge(y2_lo, CREDIT + n)
                    for i in range(2):
                        dve.wait_ge(t_made, CREDIT + 2 * n + i + 1)
                        V.tensor_tensor(y2_raw[:, 4 * i:4 * i + 4, :], pT[s][i][:, :].rearrange("p (c t) -> p c t", t=P),
                                        k.vec[:, G2 + 4 * i:G2 + 4 * i + 4].unsqueeze(2).to_broadcast([P, 4, P]),
                                        ALU.mult).then_inc(y2_made, 1)

                def step(n, s, first=False, last=False):
                    if not last:
                        low(n + 1, 1 - s)
                    dve.wait_ge(squared, CREDIT + 2 * (n + 1))
                    V.tensor_tensor(ss[s][:, 0:1], ss[s][:, 0:1], ss[s][:, 1:2], ALU.add).then_inc(mean1, 1)
                    dve.wait_ge(root1, CREDIT + n + 1)
                    V.reciprocal(rs[s][:, :], rs[s][:, :]).then_inc(rs_ready, 1)
                    dve.wait_ge(rs_ready, CREDIT + n + 1)
                    dve.wait_ge(h_stored[s], CREDIT + 8 * (n - s))
                    for half in range(HALVES):
                        cols = slice(half * 512, (half + 1) * 512)
                        V.scalar_tensor_tensor(out=h[s][:, cols], in0=pO[s][half][:, :], scalar=rs[s][:, :],
                                               in1=post_g[:, cols], op0=ALU.mult, op1=ALU.mult).then_inc(scaled, 1)
                    dve.wait_ge(xr_loaded[s], CREDIT + 8 * (n + 2 - s))
                    for half in range(HALVES):
                        cols = slice(half * 512, (half + 1) * 512)
                        dve.wait_ge(scaled, CREDIT + 2 * n + half + 1)
                        V.tensor_tensor(h[s][:, cols], h[s][:, cols], xr[s][:, cols], ALU.add).then_inc(h_ready, 1)
                    if not first:
                        take_y2(n - 1, 1 - s)
                    dve.wait_ge(root2, CREDIT + n + 1)
                    V.reciprocal(rs2[s][:, :], rs2[s][:, :]).then_inc(rs2_ready, 1)
                    dve.wait_ge(rs2_ready, CREDIT + n + 1)
                    dve.wait_ge(t_made, CREDIT + 2 * (n - 1))
                    V.tensor_scalar(hn[s][:, :], h[s][:, :], rs2[s][:, :], None, ALU.mult).then_inc(hn_ready, 1)

                low(0, 0)
                for q in range(KC):
                    dve.wait_ge(w_hi, q + 1)
                    V.tensor_tensor(w[:, LO, q, :], w_raw[:, q, :], w[:, HI, q, :].bitcast(f32), ALU.subtract)\
                     .then_inc(w_lo, 1)
                dve.wait_ge(post_loaded, 16)
                steps(dve, step)
                take_y2(NB - 1, 1)


def ffn(nc, k, a, h_dram, y2_dram, out):
    T = 512
    NT = S // T
    TB = T // P
    HALVES = D // 512
    ITEMS = 2 * FC
    HI, LO = 0, 1
    PASSES = ((HI, HI), (HI, LO), (LO, HI))
    w_in = a["ffn_w_in"][0, :, :].rearrange("(c p) f -> p c f", p=P)
    w_out = a["ffn_w_out"][0, :, :].rearrange("(c p) f -> c p f", p=P)
    out_rows = out[0, :, :].rearrange("(n p) d -> n p d", p=P)
    with ExitStack() as c:
        sb = lambda n, s, d=f32: c.enter_context(nc.sbuf_tensor(n, s, d))
        sem = lambda n: nc.alloc_semaphore(name=n)
        post_g = sb("post_g3", [P, D])
        y2 = sb("y2_split", [P, 2, KC, T], f32r)
        w_raw = [sb(f"w_raw{s}", [P, 2, KC * P]) for s in range(2)]
        w = [sb(f"w_split{s}", [P, 2, 2, KC * P], f32r) for s in range(2)]
        acts = sb("acts", [P, FC, T])
        act = [sb(f"act_split{s}", [P, 2, T], f32r) for s in range(2)]
        halo = sb("halo", [P, FC, 2])
        gate = [sb(f"gate{s}", [P, T + 2]) for s in range(2)]
        conv = [sb(f"conv{s}", [P, T]) for s in range(2)]
        conv_rows = sb("conv_rows", [4 * FC, P])
        conv_vec = sb("conv_vec", [P, 4, FC])
        o_sb = sb("o_sb", [P, TB, D])
        hb = sb("hb", [P, TB, D])
        squares = [sb(f"squares_f{s}", [P, 512]) for s in range(2)]
        ss = sb("ss_f", [P, TB, HALVES]); ss_sum = sb("ss_sum", [P, TB]); rs = sb("rs_f", [P, TB]); eps = sb("eps_f", [P, 1])
        po = [[c.enter_context(nc.psum_tensor(f"po{b}_{h}", [P, 512], f32)) for h in range(HALVES)] for b in range(TB)]
        pg, pu = [po[s][0] for s in range(2)], [po[s][1] for s in range(2)]

        credited = []

        def csem(n):
            credited.append(sem(n))
            return credited[-1]
        w_out_loaded = [csem(f"w_out_loaded{s}") for s in range(2)]
        w_in_loaded = [csem(f"w_in_loaded{s}") for s in range(2)]
        y2_loaded = sem("y2_loaded"); hb_loaded = sem("hb_loaded"); stored = sem("out_stored")
        hi_made = csem("w_hi_made"); lo_made = csem("w_lo_made"); item_done = csem("item_done")
        act_hi_made = csem("act_hi_made"); act_lo_made = csem("act_lo_made")
        gate_made = csem("gate_made"); gate_copied = csem("gate_copied"); halo_in = csem("halo_in")
        halo_out = csem("halo_out"); conv0 = csem("conv0"); conv1 = csem("conv1"); conv2 = csem("conv2")
        silu_ready = csem("silu_ready"); act_ready = csem("act_ready")
        o_made = csem("o_made"); squared = csem("squared_f"); taken = csem("taken_f"); summed = csem("summed_f")
        root = csem("root_f"); rs_ready = csem("rs_ready_f"); scaled = csem("scaled_f"); out_ready = csem("out_ready")
        conv_loaded = sem("conv_loaded"); conv_t = sem("conv_t"); set_up = sem("set_up_f"); post_loaded = sem("post_loaded")
        held = sem("held_f")

        with nc.Block() as block:
            @block.gpsimd
            def _(pool):
                for s in credited:
                    pool.sem_inc(s, CREDIT)

        with nc.Block() as block:
            @block.sync
            def _(sp):
                def load_in(m, f, s):
                    sp.wait_ge(lo_made, CREDIT + m - 1)
                    sp.dma_start(w_raw[s][:, 0, :].rearrange("p (c f) -> p c f", f=P), w_in[:, :, bass.ts(f, P)])\
                      .then_inc(w_in_loaded[s], 16)
                    sp.dma_start(w_raw[s][:, 1, :].rearrange("p (c f) -> p c f", f=P), w_in[:, :, bass.ds(f * P + F, P)])\
                      .then_inc(w_in_loaded[s], 16)

                sp.dma_start(conv_rows[0:3 * FC, :], a["ffn_conv_w"][0, :, :].rearrange("w (c p) -> (w c) p", p=P))\
                  .then_inc(conv_loaded, 16)
                sp.dma_start(conv_rows[3 * FC:4 * FC, :], a["ffn_conv_b"][0, :].rearrange("(c p) -> c p", p=P))\
                  .then_inc(conv_loaded, 16)
                with sp.Fori(0, NT) as tt:
                    m0 = ITEMS * tt
                    with sp.Fori(0, FC // 2) as g:
                        for s in range(2):
                            load_in(m0 + 2 * g + s, 2 * g + s, s)
                    with sp.Fori(0, FC // 2) as g:
                        for s in range(2):
                            f = 2 * g + s
                            sp.wait_ge(lo_made, CREDIT + m0 + FC + f - 1)
                            sp.dma_start(w_raw[s][:, 0, :], w_out[bass.ds(f, 1), :, :].rearrange("o p d -> p (o d)"))\
                              .then_inc(w_out_loaded[s], 16)
                load_in(ITEMS * NT, 0, 0)

            @block.gpsimd
            def _(pool):
                nc.gpsimd.memset(eps[:, :], NORM_EPS).then_inc(set_up, 1)
                nc.gpsimd.memset(halo[:, :, :], 0.0).then_inc(set_up, 1)
                for q in range(KC):
                    pool.dma_start(y2[:, :, q, :].bitcast(f32), y2_dram[:, :, q, 0:T]).then_inc(y2_loaded, 16)
                pool.dma_start(post_g[:, :], a["norm_g"][0, 3:4, :].to_broadcast([P, D])).then_inc(post_loaded, 16)

                def tile(tt, last):
                    if not last:
                        for q in range(KC):
                            pool.wait_ge(item_done, CREDIT + ITEMS * tt + FC + 2 * q)
                            pool.sem_inc(held, 1)
                            pool.dma_start(y2[:, :, q, :].bitcast(f32), y2_dram[:, :, q, bass.ds((tt + 1) * T, T)])\
                                .then_inc(y2_loaded, 16)
                    pool.wait_ge(hb_loaded, 16 * (tt + 1))
                    pool.wait_ge(rs_ready, CREDIT + tt + 1)
                    pool.sem_inc(held, 1)
                    for b in range(TB):
                        nc.gpsimd.tensor_scalar(o_sb[:, b, :], o_sb[:, b, :], rs[:, b:b + 1], None, ALU.mult)\
                            .then_inc(scaled, 1)
                        pool.wait_ge(scaled, CREDIT + TB * tt + b + 1)
                        nc.gpsimd.tensor_tensor(hb[:, b, :], hb[:, b, :], o_sb[:, b, :], ALU.add).then_inc(out_ready, 1)
                        pool.wait_ge(out_ready, CREDIT + TB * tt + b + 1)
                        pool.sem_inc(held, 1)
                        pool.dma_start(out_rows[bass.ds(TB * tt + b, 1), :, :].rearrange("o p d -> p (o d)"), hb[:, b, :])\
                            .then_inc(stored, 16)

                pool.dma_start(hb[:, :, :], h_dram[0:TB, :, :].rearrange("n p d -> p n d")).then_inc(hb_loaded, 16)
                with pool.Fori(0, NT - 1) as tt:
                    tile(tt, False)
                    pool.wait_ge(stored, 16 * TB * (tt + 1))
                    pool.sem_inc(held, 1)
                    pool.dma_start(hb[:, :, :], h_dram[bass.ds(TB * (tt + 1), TB), :, :].rearrange("n p d -> p n d"))\
                        .then_inc(hb_loaded, 16)
                tile(NT - 1, True)
                pool.wait_ge(stored, 16 * TB * NT)
                for s in range(2):
                    pool.wait_ge(w_in_loaded[s], CREDIT + 32 * (FC // 2 * NT + 1 - s))

            @block.tensor
            def _(pe):
                pe.wait_ge(conv_loaded, 32)
                nc.tensor.transpose(po[0][0][:, 0:4 * FC], conv_rows[:, :], k.ident[0:4 * FC, 0:4 * FC]).then_inc(conv_t, 1)
                pe.wait_ge(set_up, 3)
                with pe.Fori(0, NT) as tt:
                    with pe.Fori(0, FC // 2) as g:
                        for s in range(2):
                            n = FC * tt + 2 * g + s
                            pe.wait_ge(lo_made, CREDIT + ITEMS * tt + 2 * g + s + 1)
                            pe.wait_ge(y2_loaded, 16 * KC * (tt + 1))
                            pe.wait_ge(gate_copied, CREDIT + n - 1)
                            pe.wait_ge(squared, CREDIT + HALVES * (TB * (tt - 1) + s + 1))
                            pe.wait_ge(taken, CREDIT + HALVES * (TB * (tt - 1) + s + 1))
                            for part, bank in ((0, pg[s]), (1, pu[s])):
                                if part == 1:
                                    pe.wait_ge(act_ready, CREDIT + n - 1)
                                for q in range(KC):
                                    for j, (x, y) in enumerate(PASSES):
                                        mm = nc.tensor.matmul(bank[:, :], w[s][:, x, part, q * P:(q + 1) * P],
                                                              y2[:, y, q, :], start=(q == 0 and j == 0),
                                                              stop=(q == KC - 1 and j == 2))
                                mm.then_inc((gate_made, item_done)[part], 1)

                    def outputs(f, s, first=False, last=False):
                        pe.wait_ge(lo_made, CREDIT + ITEMS * tt + FC + f + 1)
                        pe.wait_ge(act_lo_made, CREDIT + FC * tt + f + 1)
                        for b in ((0, 1, 2, 3) if last else (2, 3, 0, 1)):
                            if first:
                                if b < 2:
                                    pe.wait_ge(act_ready, CREDIT + FC * (tt + 1) - 1 + b)
                                pe.wait_ge(squared, CREDIT + HALVES * TB * tt)
                                pe.wait_ge(taken, CREDIT + HALVES * TB * tt)
                            for j, (x, y) in enumerate(PASSES):
                                for half in range(HALVES):
                                    mm = nc.tensor.matmul(po[b][half][:, :], act[s][:, x, b * P:(b + 1) * P],
                                                          w[s][:, y, 0, half * 512:(half + 1) * 512],
                                                          start=(first and j == 0), stop=(last and j == 2))
                            if last and b < TB - 1:
                                mm.then_inc(o_made, 1)
                        mm.then_inc(item_done, 1)

                    outputs(0, 0, first=True)
                    outputs(1, 1)
                    with pe.Fori(1, FC // 2 - 1) as g:
                        for s in range(2):
                            outputs(2 * g + s, s)
                    outputs(FC - 2, 0)
                    outputs(FC - 1, 1, last=True)

            def wait_block(eng, tt, b):
                if b < TB - 1:
                    eng.wait_ge(o_made, CREDIT + (TB - 1) * tt + b + 1)
                else:
                    eng.wait_ge(item_done, CREDIT + ITEMS * (tt + 1))

            @block.scalar
            def _(sc):
                def hi_in(m, n, s):
                    sc.wait_ge(w_in_loaded[s], CREDIT + 32 * (n + 1))
                    sc.wait_ge(item_done, CREDIT + m - 1)
                    nc.scalar.activation(w[s][:, HI, :, :], w_raw[s][:, :, :], ACT.Copy).then_inc(hi_made, 1)

                def hi_out(tt, f, g, s):
                    sc.wait_ge(w_out_loaded[s], CREDIT + 16 * (FC // 2 * tt + g + 1))
                    sc.wait_ge(item_done, CREDIT + ITEMS * tt + FC + f - 1)
                    nc.scalar.activation(w[s][:, HI, 0, :], w_raw[s][:, 0, :], ACT.Copy).then_inc(hi_made, 1)
                    sc.wait_ge(act_ready, CREDIT + FC * tt + f + 1)
                    nc.scalar.activation(act[s][:, HI, :], acts[:, bass.ds(f, 1), :].rearrange("p o t -> p (o t)"),
                                         ACT.Copy).then_inc(act_hi_made, 1)

                def gate_silu(tt, f, s):
                    n = FC * tt + f
                    sc.wait_ge(gate_made, CREDIT + n + 1)
                    sc.wait_ge(conv2, CREDIT + n - 1)
                    sc.wait_ge(halo_out, CREDIT + n - 1)
                    nc.scalar.activation(gate[s][:, 2:T + 2], pg[s][:, :], ACT.Copy).then_inc(gate_copied, 1)
                    sc.wait_ge(conv2, CREDIT + n + 1)
                    nc.scalar.activation(conv[s][:, :], conv[s][:, :], ACT.Silu).then_inc(silu_ready, 1)

                sc.wait_ge(set_up, 2)
                hi_in(0, 0, 0)
                with sc.Fori(0, NT) as tt:
                    with sc.Fori(0, FC // 2 - 1) as g:
                        hi_in(ITEMS * tt + 2 * g + 1, FC // 2 * tt + g, 1)
                        gate_silu(tt, 2 * g, 0)
                        hi_in(ITEMS * tt + 2 * g + 2, FC // 2 * tt + g + 1, 0)
                        gate_silu(tt, 2 * g + 1, 1)
                    hi_in(ITEMS * tt + FC - 1, FC // 2 * tt + FC // 2 - 1, 1)
                    gate_silu(tt, FC - 2, 0)
                    hi_out(tt, 0, 0, 0)
                    gate_silu(tt, FC - 1, 1)
                    with sc.Fori(0, FC // 2 - 1) as g:
                        hi_out(tt, 2 * g + 1, g, 1)
                        hi_out(tt, 2 * g + 2, g + 1, 0)
                    hi_out(tt, FC - 1, FC // 2 - 1, 1)
                    hi_in(ITEMS * (tt + 1), FC // 2 * (tt + 1), 0)
                    sc.wait_ge(summed, CREDIT + tt)
                    for b in range(TB):
                        wait_block(sc, tt, b)
                        for half in range(HALVES):
                            sc.wait_ge(squared, CREDIT + HALVES * (TB * tt + b) + half - 1)
                            nc.scalar.activation(squares[half][:, :], po[b][half][:, :], ACT.Square,
                                                 accum_out=ss[:, b, half:half + 1]).then_inc(squared, 1)
                    sc.wait_ge(summed, CREDIT + tt + 1)
                    sc.wait_ge(out_ready, CREDIT + TB * tt)
                    nc.scalar.activation(rs[:, :], ss_sum[:, :], ACT.Sqrt, bias=eps[:, :], scale=1.0 / D).then_inc(root, 1)

            @block.vector
            def _(dve):
                V = nc.vector

                def lo_in(m, s):
                    dve.wait_ge(hi_made, CREDIT + m + 1)
                    V.tensor_tensor(w[s][:, LO, :, :], w_raw[s][:, :, :], w[s][:, HI, :, :].bitcast(f32), ALU.subtract)\
                     .then_inc(lo_made, 1)

                def lo_out(tt, f, s):
                    dve.wait_ge(hi_made, CREDIT + ITEMS * tt + FC + f + 1)
                    V.tensor_tensor(w[s][:, LO, 0, :], w_raw[s][:, 0, :], w[s][:, HI, 0, :].bitcast(f32), ALU.subtract)\
                     .then_inc(lo_made, 1)
                    dve.wait_ge(act_hi_made, CREDIT + FC * tt + f + 1)
                    V.tensor_tensor(act[s][:, LO, :], acts[:, bass.ds(f, 1), :].rearrange("p o t -> p (o t)"),
                                    act[s][:, HI, :].bitcast(f32), ALU.subtract).then_inc(act_lo_made, 1)

                def conv_gate(tt, f, s):
                    n = FC * tt + f
                    weight = lambda x: conv_vec[:, x, bass.ds(f, 1)]
                    dve.wait_ge(conv2, CREDIT + n - 1)
                    V.tensor_scalar(gate[s][:, 0:2], halo[:, bass.ds(f, 1), :].rearrange("p o t -> p (o t)"),
                                    1.0, None, ALU.mult).then_inc(halo_in, 1)
                    dve.wait_ge(gate_copied, CREDIT + n + 1)
                    dve.wait_ge(act_ready, CREDIT + n - 1)
                    V.tensor_scalar(conv[s][:, :], gate[s][:, 2:T + 2], weight(2), weight(3), ALU.mult, ALU.add)\
                     .then_inc(conv0, 1)
                    dve.wait_ge(halo_in, CREDIT + n + 1)
                    V.tensor_scalar(halo[:, bass.ds(f, 1), :].rearrange("p o t -> p (o t)"),
                                    gate[s][:, T:T + 2], 1.0, None, ALU.mult)\
                     .then_inc(halo_out, 1)
                    dve.wait_ge(conv0, CREDIT + n + 1)
                    V.scalar_tensor_tensor(out=conv[s][:, :], in0=gate[s][:, 1:T + 1], scalar=weight(1),
                                           in1=conv[s][:, :], op0=ALU.mult, op1=ALU.add).then_inc(conv1, 1)
                    dve.wait_ge(conv1, CREDIT + n + 1)
                    V.scalar_tensor_tensor(out=conv[s][:, :], in0=gate[s][:, 0:T], scalar=weight(0),
                                           in1=conv[s][:, :], op0=ALU.mult, op1=ALU.add).then_inc(conv2, 1)
                    dve.wait_ge(silu_ready, CREDIT + n + 1)
                    dve.wait_ge(item_done, CREDIT + ITEMS * tt + f + 1)
                    dve.wait_ge(act_lo_made, CREDIT + FC * tt)
                    V.tensor_tensor(acts[:, bass.ds(f, 1), :].rearrange("p o t -> p (o t)"), conv[s][:, :],
                                    pu[s][:, :], ALU.mult).then_inc(act_ready, 1)

                dve.wait_ge(conv_t, 1)
                dve.wait_ge(set_up, 2)
                V.tensor_copy(conv_vec[:, :, :].rearrange("p w c -> p (w c)"), po[0][0][:, 0:4 * FC]).then_inc(set_up, 1)
                dve.wait_ge(set_up, 3)
                dve.wait_ge(post_loaded, 16)
                lo_in(0, 0)
                with dve.Fori(0, NT) as tt:
                    with dve.Fori(0, FC // 2 - 1) as g:
                        for s in range(2):
                            lo_in(ITEMS * tt + 2 * g + s + 1, 1 - s)
                            conv_gate(tt, 2 * g + s, s)
                    lo_in(ITEMS * tt + FC - 1, 1)
                    conv_gate(tt, FC - 2, 0)
                    lo_out(tt, 0, 0)
                    conv_gate(tt, FC - 1, 1)
                    with dve.Fori(0, FC // 2 - 1) as g:
                        for s in range(2):
                            lo_out(tt, 2 * g + s + 1, 1 - s)
                    lo_out(tt, FC - 1, 1)
                    lo_in(ITEMS * (tt + 1), 0)
                    dve.wait_ge(out_ready, CREDIT + TB * tt)
                    for b in range(TB):
                        wait_block(dve, tt, b)
                        for half in range(HALVES):
                            cols = slice(half * 512, (half + 1) * 512)
                            dve.wait_ge(squared, CREDIT + HALVES * (TB * tt + b) + half + 1)
                            V.tensor_tensor(o_sb[:, b, cols], po[b][half][:, :], post_g[:, cols], ALU.mult)\
                             .then_inc(taken, 1)
                    dve.wait_ge(squared, CREDIT + HALVES * TB * (tt + 1))
                    dve.wait_ge(root, CREDIT + tt)
                    V.tensor_tensor(ss_sum[:, :], ss[:, :, 0], ss[:, :, 1], ALU.add).then_inc(summed, 1)
                    dve.wait_ge(root, CREDIT + tt + 1)
                    V.reciprocal(rs[:, :], rs[:, :]).then_inc(rs_ready, 1)


def trunk(nc: bass.Bass, a, out):
    scratch = nc.dram_tensor("scratch_rows", [NCH, KC, P, ROW], f32, kind="Internal").ap()
    gated = nc.dram_tensor("gated", [NCH + 1, KC, P, C], f32, kind="Internal").ap()
    h_dram = nc.dram_tensor("h_dram", [S // P, P, D], f32, kind="Internal").ap()
    y2_dram = nc.dram_tensor("y2_dram", [P, 2, KC, S], f32, kind="Internal").ap()
    with ExitStack() as ctx:
        k = constants(nc, ctx, a)
        with nc.cleanup_on_exit():
            project(nc, k, a, scratch)
        with nc.cleanup_on_exit():
            recur(nc, k, scratch, gated)
        with nc.cleanup_on_exit():
            attend_out(nc, k, a, gated, h_dram, y2_dram)
        with nc.cleanup_on_exit():
            ffn(nc, k, a, h_dram, y2_dram, out)


_INS = ["x", "norm_g", "ffn_w_in", "ffn_conv_w", "ffn_conv_b", "ffn_w_out", "rwkv_mu", "rwkv_w_rkv", "rwkv_w0",
        "rwkv_w1", "rwkv_w2", "rwkv_a0", "rwkv_a1", "rwkv_a2", "rwkv_g1", "rwkv_g2", "rwkv_k_k", "rwkv_k_a",
        "rwkv_r_k", "rwkv_ln_w", "rwkv_ln_b", "rwkv_w_o"]


def kernel(**inputs):
    import numpy as _np
    import concourse.bacc as _bacc
    from concourse import mybir as _mybir
    from concourse.bass_utils import run_bass_kernel_spmd as _run

    nc = _bacc.Bacc("TRN2", target_bir_lowering=False, num_devices=1)
    arrays, args = {}, {}
    for name in _INS:
        a = _np.ascontiguousarray(inputs[name])
        arrays[f"in_{name}_dram"] = a
        args[name] = nc.dram_tensor(f"in_{name}_dram", a.shape, _mybir.dt.from_np(a.dtype), kind="ExternalInput").ap()
    out = nc.dram_tensor("out_0_dram", (1, S, D), _mybir.dt.float32, kind="ExternalOutput").ap()
    trunk(nc, args, out)
    r = _run(nc, [arrays], core_ids=[0])
    return r.results[0]["out_0_dram"]
```
